# Optimizing a Trainium2 kernel written in Bass

```python
import math
import jax, jax.numpy as jnp
from jax import lax
import numpy as np

D_MODEL = 1024
BATCH = 1
SEQ = 256
DEPTH = 1

CONV_DIM = 512
CONV_WIDTH = 3
NSA_HEADS = 8
NSA_KV_GROUPS = 2
NSA_HPG = NSA_HEADS // NSA_KV_GROUPS
NSA_HEAD_DIM = 64
NSA_DIM = NSA_HEADS * NSA_HEAD_DIM
CMP_LEN = 32
CMP_STRIDE = 16
CMP_HIDDEN = 256
SLC_LEN = 64
SLC_TOPN = 8
SLC_FORCE_BONUS = 1e6
WINDOW = 512
NSA_QBLOCK = 64
GDN_HEADS = 4
GDN_HEAD_DIM = 128
GDN_DIM = GDN_HEADS * GDN_HEAD_DIM
GDN_CONV = 4
GDN_CHUNK = 64
N_BRANCH = 3
BRANCH_DIM = 512
IN_SPLITS = (3 * CONV_DIM, NSA_DIM, 6 * NSA_KV_GROUPS * NSA_HEAD_DIM, 3 * NSA_HEADS, 3 * GDN_DIM, GDN_DIM, GDN_HEADS, GDN_HEADS)
D_IN = 3 * CONV_DIM + NSA_DIM + 6 * NSA_KV_GROUPS * NSA_HEAD_DIM + 3 * NSA_HEADS + 4 * GDN_DIM + 2 * GDN_HEADS
MOE_GROUPS = 4
EXPERTS_PER_GROUP = 8
N_EXPERTS = MOE_GROUPS * EXPERTS_PER_GROUP
TOPK_IN_GROUP = 2
EXPERT_FF = 512
MOE_BLOCK = 256
RMS_EPS = 1e-6
NEG_INF = -1e30


def split_last(u, sizes):
    out, start = [], 0
    for n in sizes:
        out.append(u[..., start:start + n])
        start += n
    return out

def rms_norm(x, gain):
    xf = x.astype(jnp.float32)
    y = xf * lax.rsqrt(jnp.mean(xf * xf, axis=-1, keepdims=True) + RMS_EPS)
    return (y * gain.astype(jnp.float32)).astype(x.dtype)

def l2_norm(x):
    return x * lax.rsqrt(jnp.sum(x * x, axis=-1, keepdims=True) + RMS_EPS)

def causal_depthwise_conv(x, w):
    k, c = w.shape
    return lax.conv_general_dilated(x, w[:, None, :].astype(x.dtype), window_strides=(1,), padding=[(k - 1, 0)], dimension_numbers=('NWC', 'WIO', 'NWC'), feature_group_count=c)

def alibi_slopes(n):
    return 2.0 ** (-8.0 * jnp.arange(1, n + 1, dtype=jnp.float32) / n)

def short_conv_mixer(u_a, conv_w):
    b_gate, c_gate, x_in = split_last(u_a, (CONV_DIM, CONV_DIM, CONV_DIM))
    return b_gate * causal_depthwise_conv(c_gate * x_in, conv_w)

def nsa_compress(kv, pe, w1, w2):
    b, s, g, d = kv.shape
    n_cmp = (s - CMP_LEN) // CMP_STRIDE + 1
    idx = jnp.arange(n_cmp)[:, None] * CMP_STRIDE + jnp.arange(CMP_LEN)[None, :]
    blocks = kv[:, idx] + pe[:, None, :]
    flat = jnp.moveaxis(blocks, 3, 2).reshape(b, n_cmp, g, CMP_LEN * d)
    return jax.nn.gelu(flat @ w1) @ w2

def nsa_mixer(u_q, u_kv, u_g, qk_gain, cmp_pe, cmp_w1, cmp_w2):
    b, s, _ = u_q.shape
    g, hpg, d, qbl = NSA_KV_GROUPS, NSA_HPG, NSA_HEAD_DIM, NSA_QBLOCK
    f32 = jnp.float32
    scale = d ** -0.5
    q = rms_norm(u_q.reshape(b, s, g, hpg, d), qk_gain[0])
    kv = u_kv.reshape(b, s, 6, g, d)
    k_c = rms_norm(nsa_compress(kv[:, :, 0], cmp_pe[0], cmp_w1[0], cmp_w2[0]), qk_gain[1])
    v_c = nsa_compress(kv[:, :, 1], cmp_pe[1], cmp_w1[1], cmp_w2[1])
    n_cmp = k_c.shape[1]
    n_slc = s // SLC_LEN
    top_n = min(SLC_TOPN, n_slc)
    k_s = rms_norm(kv[:, :, 2], qk_gain[2]).reshape(b, n_slc, SLC_LEN, g, d).transpose(0, 3, 1, 2, 4)
    v_s = kv[:, :, 3].reshape(b, n_slc, SLC_LEN, g, d).transpose(0, 3, 1, 2, 4)
    pad = ((0, 0), (WINDOW, 0), (0, 0), (0, 0))
    k_w = jnp.pad(rms_norm(kv[:, :, 4], qk_gain[3]), pad)
    v_w = jnp.pad(kv[:, :, 5], pad)
    gates = jax.nn.sigmoid(u_g.astype(f32)).reshape(b, s, 3, g, hpg)
    slopes = alibi_slopes(NSA_HEADS).reshape(g, hpg)
    cmp_lo = jnp.arange(n_cmp) * CMP_STRIDE
    cmp_end = cmp_lo + CMP_LEN - 1
    slc_lo = jnp.arange(n_slc) * SLC_LEN
    overlap = ((cmp_lo[:, None] < slc_lo[None, :] + SLC_LEN) & (cmp_lo[:, None] + CMP_LEN > slc_lo[None, :])).astype(f32)
    n_qb = s // qbl
    q_blocks = jnp.moveaxis(q.reshape(b, n_qb, qbl, g, hpg, d), 1, 0)
    g_blocks = jnp.moveaxis(gates.reshape(b, n_qb, qbl, 3, g, hpg), 1, 0)
    bi = jnp.arange(b)[:, None, None, None]
    gi = jnp.arange(g)[None, :, None, None]
    j_idx = jnp.arange(n_slc)

    def query_block(args):
        qb, gb, blk = args
        q0 = blk * qbl
        t = q0 + jnp.arange(qbl)
        dist_c = (t[:, None] - cmp_end[None, :]).astype(f32)
        ok_c = dist_c >= 0
        s_c = jnp.einsum('bqghd,bcgd->bghqc', qb, k_c).astype(f32) * scale
        s_c = jnp.where(ok_c, s_c - slopes[:, :, None, None] * dist_c, NEG_INF)
        p_c = jax.nn.softmax(s_c, axis=-1) * jnp.any(ok_c, axis=-1)[:, None].astype(f32)
        o_c = jnp.einsum('bghqc,bcgd->bqghd', p_c.astype(v_c.dtype), v_c)
        imp = jnp.einsum('bghqc,cj->bgqj', p_c, overlap)
        jt = (t // SLC_LEN)[:, None]
        forced = (j_idx[None, :] == 0) | (j_idx[None, :] == jt) | (j_idx[None, :] == jt - 1)
        score = jnp.where(j_idx[None, :] <= jt, imp + jnp.where(forced, SLC_FORCE_BONUS, 0.0), NEG_INF)
        _, sel = lax.top_k(score, top_n)
        k_sel = k_s[bi, gi, sel].reshape(b, g, qbl, top_n * SLC_LEN, d)
        v_sel = v_s[bi, gi, sel].reshape(b, g, qbl, top_n * SLC_LEN, d)
        pos_s = (sel[..., None] * SLC_LEN + jnp.arange(SLC_LEN)).reshape(b, g, qbl, top_n * SLC_LEN)
        dist_s = (t[None, None, :, None] - pos_s).astype(f32)[:, :, None]
        s_s = jnp.einsum('bqghd,bgqkd->bghqk', qb, k_sel).astype(f32) * scale
        s_s = jnp.where(dist_s >= 0, s_s - slopes[None, :, :, None, None] * dist_s, NEG_INF)
        p_s = jax.nn.softmax(s_s, axis=-1)
        o_s = jnp.einsum('bghqk,bgqkd->bqghd', p_s.astype(v_sel.dtype), v_sel)
        k_wb = lax.dynamic_slice_in_dim(k_w, q0, WINDOW + qbl, axis=1)
        v_wb = lax.dynamic_slice_in_dim(v_w, q0, WINDOW + qbl, axis=1)
        pos_w = q0 - WINDOW + jnp.arange(WINDOW + qbl)
        dist_w = t[:, None] - pos_w[None, :]
        ok_w = (dist_w >= 0) & (dist_w < WINDOW) & (pos_w[None, :] >= 0)
        s_w = jnp.einsum('bqghd,bkgd->bghqk', qb, k_wb).astype(f32) * scale
        s_w = jnp.where(ok_w, s_w - slopes[:, :, None, None] * dist_w.astype(f32), NEG_INF)
        p_w = jax.nn.softmax(s_w, axis=-1)
        o_w = jnp.einsum('bghqk,bkgd->bqghd', p_w.astype(v_wb.dtype), v_wb)
        o = gb[:, :, 0, :, :, None] * o_c + gb[:, :, 1, :, :, None] * o_s + gb[:, :, 2, :, :, None] * o_w
        return o.reshape(b, qbl, NSA_DIM).astype(qb.dtype)

    out = lax.map(query_block, (q_blocks, g_blocks, jnp.arange(n_qb)))
    return jnp.moveaxis(out, 0, 1).reshape(b, s, NSA_DIM)

def chunk_gated_delta_rule(q, k, v, g, beta):
    b, s, h, dk = q.shape
    dv = v.shape[-1]
    c = GDN_CHUNK
    n = s // c

    def to_chunks(a):
        return jnp.moveaxis(a.reshape((b, n, c, h) + a.shape[3:]), 3, 1)

    q, k, v, beta = to_chunks(q), to_chunks(k), to_chunks(v), to_chunks(beta)
    gc = jnp.cumsum(to_chunks(g), axis=-1)
    tri = jnp.tril(jnp.ones((c, c), dtype=bool))
    decay = jnp.where(tri, jnp.exp(jnp.where(tri, gc[..., :, None] - gc[..., None, :], 0.0)), 0.0)
    k_beta = k * beta[..., None]
    m = jnp.einsum('bhncd,bhnsd->bhncs', k_beta, k) * decay
    t_inv = lax.linalg.triangular_solve(m, jnp.broadcast_to(jnp.eye(c, dtype=m.dtype), m.shape), left_side=True, lower=True, unit_diagonal=True)
    u = t_inv @ (v * beta[..., None])
    w = t_inv @ (k_beta * jnp.exp(gc)[..., None])
    attn = jnp.einsum('bhncd,bhnsd->bhncs', q, k) * decay
    q_dec = q * jnp.exp(gc)[..., None]
    g_last = gc[..., -1:]
    k_dec = k * jnp.exp(g_last - gc)[..., None]
    chunk_decay = jnp.exp(g_last[..., 0])

    def step(state, xs):
        q_i, k_i, u_i, w_i, a_i, d_i = xs
        v_new = u_i - jnp.einsum('bhcd,bhde->bhce', w_i, state)
        o_i = jnp.einsum('bhcd,bhde->bhce', q_i, state) + jnp.einsum('bhcs,bhse->bhce', a_i, v_new)
        state = state * d_i[..., None, None] + jnp.einsum('bhcd,bhce->bhde', k_i, v_new)
        return state, o_i

    xs = tuple(jnp.moveaxis(a, 2, 0) for a in (q_dec, k_dec, u, w, attn, chunk_decay))
    _, o = lax.scan(step, jnp.zeros((b, h, dk, dv), q.dtype), xs)
    return o.transpose(1, 0, 3, 2, 4).reshape(b, s, h, dv)

def gated_deltanet_mixer(u_qkv, u_z, u_b, u_a, conv_w, a_log, dt_bias, out_gain):
    b, s, _ = u_qkv.shape
    f32 = jnp.float32
    qkv = jax.nn.silu(causal_depthwise_conv(u_qkv, conv_w)).astype(f32).reshape(b, s, 3, GDN_HEADS, GDN_HEAD_DIM)
    q = l2_norm(qkv[:, :, 0]) * GDN_HEAD_DIM ** -0.5
    k = l2_norm(qkv[:, :, 1])
    v = qkv[:, :, 2]
    beta = jax.nn.sigmoid(u_b.astype(f32))
    g = -jnp.exp(a_log.astype(f32)) * jax.nn.softplus(u_a.astype(f32) + dt_bias.astype(f32))
    o = chunk_gated_delta_rule(q, k, v, g, beta)
    o = rms_norm(o, out_gain) * jax.nn.silu(u_z.astype(f32).reshape(b, s, GDN_HEADS, GDN_HEAD_DIM))
    return o.reshape(b, s, GDN_DIM).astype(u_qkv.dtype)

def hybrid_mixer(h, w_in, conv_a_w, nsa_qk_gain, cmp_pe, cmp_w1, cmp_w2, gdn_conv_w, gdn_a_log, gdn_dt_bias, gdn_out_gain, w_branch, w_gate, b_gate, w_out):
    b, s, dm = h.shape
    u = h @ w_in
    u_a, u_nq, u_nkv, u_ng, u_gqkv, u_gz, u_gb, u_ga = split_last(u, IN_SPLITS)
    y_a = short_conv_mixer(u_a, conv_a_w)
    y_n = nsa_mixer(u_nq, u_nkv, u_ng, nsa_qk_gain, cmp_pe, cmp_w1, cmp_w2)
    y_g = gated_deltanet_mixer(u_gqkv, u_gz, u_gb, u_ga, gdn_conv_w, gdn_a_log, gdn_dt_bias, gdn_out_gain)
    branches = jnp.einsum('bsrc,rcd->bsrd', jnp.stack([y_a, y_n, y_g], axis=2), w_branch)
    gates = jax.nn.sigmoid((h @ w_gate + b_gate).astype(jnp.float32)).reshape(b, s, N_BRANCH, dm)
    merged = jnp.sum(gates * branches, axis=2).astype(h.dtype)
    return merged @ w_out

def hier_moe(h, w_rg, b_rg, w_re, b_re, w_eg, w_eu, w_ed):
    b, s, dm = h.shape
    n_tok = b * s
    n_asg = n_tok * TOPK_IN_GROUP
    xt = h.reshape(n_tok, dm)
    lg = (xt @ w_rg + b_rg).astype(jnp.float32)
    grp = jnp.argmax(lg, axis=-1)
    p_grp = jnp.take_along_axis(jax.nn.softmax(lg, axis=-1), grp[:, None], axis=-1)
    le = (xt @ w_re + b_re).astype(jnp.float32).reshape(n_tok, MOE_GROUPS, EXPERTS_PER_GROUP)
    le = jnp.take_along_axis(le, grp[:, None, None], axis=1)[:, 0]
    top_p, top_i = lax.top_k(jax.nn.softmax(le, axis=-1), TOPK_IN_GROUP)
    gate = top_p / jnp.sum(top_p, axis=-1, keepdims=True) * p_grp
    expert = (grp[:, None] * EXPERTS_PER_GROUP + top_i).reshape(n_asg)
    token = jnp.arange(n_asg) // TOPK_IN_GROUP
    order = jnp.argsort(expert)
    e_s, tok_s, gate_s = expert[order], token[order], gate.reshape(n_asg)[order]
    counts = jnp.bincount(expert, length=N_EXPERTS)
    n_blk = (counts + MOE_BLOCK - 1) // MOE_BLOCK
    start = jnp.cumsum(counts) - counts
    pad_start = (jnp.cumsum(n_blk) - n_blk) * MOE_BLOCK
    dest = pad_start[e_s] + jnp.arange(n_asg) - start[e_s]
    total_blk = n_asg // MOE_BLOCK + N_EXPERTS
    buf = jnp.zeros((total_blk * MOE_BLOCK, dm), h.dtype).at[dest].set(xt[tok_s])
    blk_expert = jnp.repeat(jnp.arange(N_EXPERTS), n_blk, total_repeat_length=total_blk)

    def expert_block(args):
        xb, e = args
        return (jax.nn.silu(xb @ w_eg[e]) * (xb @ w_eu[e])) @ w_ed[e]

    yb = lax.map(expert_block, (buf.reshape(total_blk, MOE_BLOCK, dm), blk_expert))
    y = yb.reshape(total_blk * MOE_BLOCK, dm)[dest] * gate_s[:, None].astype(h.dtype)
    return jax.ops.segment_sum(y, tok_s, num_segments=n_tok).reshape(b, s, dm)

def first_inputs(seed: int = 0) -> dict:
    key = jax.random.key(seed)
    ks = jax.random.split(key, 24)
    f32 = jnp.float32

    def nrm(k, shape, scale):
        return jax.random.normal(k, shape, f32) * scale

    out_scale = (2 * DEPTH) ** -0.5
    dt = jnp.exp(jax.random.uniform(ks[10], (DEPTH, GDN_HEADS), f32, math.log(1e-3), math.log(1e-1)))
    return {
        'x': nrm(ks[0], (BATCH, SEQ, D_MODEL), 1.0),
        'norm_mix': 1.0 + nrm(ks[1], (DEPTH, D_MODEL), 0.02),
        'w_in': nrm(ks[2], (DEPTH, D_MODEL, D_IN), D_MODEL ** -0.5),
        'conv_a_w': nrm(ks[3], (DEPTH, CONV_WIDTH, CONV_DIM), CONV_WIDTH ** -0.5),
        'nsa_qk_gain': 1.0 + nrm(ks[4], (DEPTH, 4, NSA_HEAD_DIM), 0.02),
        'cmp_pe': nrm(ks[5], (DEPTH, 2, CMP_LEN, NSA_HEAD_DIM), 0.02),
        'cmp_w1': nrm(ks[6], (DEPTH, 2, CMP_LEN * NSA_HEAD_DIM, CMP_HIDDEN), (CMP_LEN * NSA_HEAD_DIM) ** -0.5),
        'cmp_w2': nrm(ks[7], (DEPTH, 2, CMP_HIDDEN, NSA_HEAD_DIM), CMP_HIDDEN ** -0.5),
        'gdn_conv_w': nrm(ks[8], (DEPTH, GDN_CONV, 3 * GDN_DIM), GDN_CONV ** -0.5),
        'gdn_a_log': jnp.log(jax.random.uniform(ks[9], (DEPTH, GDN_HEADS), f32, 1.0, 16.0)),
        'gdn_dt_bias': dt + jnp.log(-jnp.expm1(-dt)),
        'gdn_out_gain': 1.0 + nrm(ks[11], (DEPTH, GDN_HEAD_DIM), 0.02),
        'w_branch': nrm(ks[12], (DEPTH, N_BRANCH, BRANCH_DIM, D_MODEL), BRANCH_DIM ** -0.5),
        'w_gate': nrm(ks[13], (DEPTH, D_MODEL, N_BRANCH * D_MODEL), D_MODEL ** -0.5),
        'b_gate': nrm(ks[14], (DEPTH, N_BRANCH * D_MODEL), 0.01),
        'w_out': nrm(ks[15], (DEPTH, D_MODEL, D_MODEL), D_MODEL ** -0.5 * out_scale),
        'norm_ffn': 1.0 + nrm(ks[16], (DEPTH, D_MODEL), 0.02),
        'w_router_group': nrm(ks[17], (DEPTH, D_MODEL, MOE_GROUPS), D_MODEL ** -0.5),
        'b_router_group': nrm(ks[18], (DEPTH, MOE_GROUPS), 0.01),
        'w_router_expert': nrm(ks[19], (DEPTH, D_MODEL, N_EXPERTS), D_MODEL ** -0.5),
        'b_router_expert': nrm(ks[20], (DEPTH, N_EXPERTS), 0.01),
        'w_expert_gate': nrm(ks[21], (DEPTH, N_EXPERTS, D_MODEL, EXPERT_FF), D_MODEL ** -0.5),
        'w_expert_up': nrm(ks[22], (DEPTH, N_EXPERTS, D_MODEL, EXPERT_FF), D_MODEL ** -0.5),
        'w_expert_down': nrm(ks[23], (DEPTH, N_EXPERTS, EXPERT_FF, D_MODEL), EXPERT_FF ** -0.5 * out_scale),
    }

def first_block(x, norm_mix, w_in, conv_a_w, nsa_qk_gain, cmp_pe, cmp_w1, cmp_w2, gdn_conv_w, gdn_a_log, gdn_dt_bias, gdn_out_gain, w_branch, w_gate, b_gate, w_out, norm_ffn, w_router_group, b_router_group, w_router_expert, b_router_expert, w_expert_gate, w_expert_up, w_expert_down):
    for l in range(DEPTH):
        h = rms_norm(x, norm_mix[l])
        x = x + hybrid_mixer(h, w_in[l], conv_a_w[l], nsa_qk_gain[l], cmp_pe[l], cmp_w1[l], cmp_w2[l], gdn_conv_w[l], gdn_a_log[l], gdn_dt_bias[l], gdn_out_gain[l], w_branch[l], w_gate[l], b_gate[l], w_out[l])
        h = rms_norm(x, norm_ffn[l])
        x = x + hier_moe(h, w_router_group[l], b_router_group[l], w_router_expert[l], b_router_expert[l], w_expert_gate[l], w_expert_up[l], w_expert_down[l])
    return x


DEPTH_2 = 2

CHUNK = 64
Q_BLOCK = 128
N_MIXERS = 2
EPS = 1e-6

MLA_HEADS = 16
MLA_NOPE = 64
MLA_ROPE = 32
MLA_V = 64
MLA_Q_LORA = 384
MLA_KV_LORA = 256
MLA_IN = MLA_Q_LORA + MLA_KV_LORA + MLA_ROPE
ROPE_THETA = 10000.0

SSM_EXPAND = 2
D_INNER = SSM_EXPAND * D_MODEL
SSM_HEADDIM = 64
SSM_HEADS = D_INNER // SSM_HEADDIM
SSM_GROUPS = 4
SSM_HPG = SSM_HEADS // SSM_GROUPS
SSM_STATE = 128
SSM_CONV = 4
SSM_CHUNK = CHUNK
CONV_DIM_2 = D_INNER + 2 * SSM_GROUPS * SSM_STATE
SSM_IN = D_INNER + CONV_DIM_2 + SSM_HEADS

D_FF = 2816
N_EXPERTS_2 = 8
TOP_K = 2
D_EXPERT = 2816


def rmsnorm(x, g):
    xf = x.astype(jnp.float32)
    y = xf * lax.rsqrt(jnp.mean(xf * xf, axis=-1, keepdims=True) + EPS)
    return (y * g.astype(jnp.float32)).astype(x.dtype)

def modulate(h, shift, scale):
    return h * (1.0 + scale[:, None, :]) + shift[:, None, :]

def rope_tables(positions):
    inv_freq = ROPE_THETA ** (-jnp.arange(0, MLA_ROPE, 2, dtype=jnp.float32) / MLA_ROPE)
    ang = positions.astype(jnp.float32)[..., None] * inv_freq
    return jnp.cos(ang), jnp.sin(ang)

def apply_rope(t, cos, sin):
    t1, t2 = jnp.split(t, 2, axis=-1)
    cos = cos.astype(t.dtype)
    sin = sin.astype(t.dtype)
    return jnp.concatenate([t1 * cos - t2 * sin, t1 * sin + t2 * cos], axis=-1)

def chunk_causal_mla_attention(q_nope, q_rope, k_nope, k_rope, v):
    bsz, seq, nh, _ = q_nope.shape
    nb = seq // Q_BLOCK
    scale = (MLA_NOPE + MLA_ROPE) ** -0.5
    qn = q_nope.reshape(bsz, nb, Q_BLOCK, nh, MLA_NOPE).transpose(1, 0, 2, 3, 4)
    qr = q_rope.reshape(bsz, nb, Q_BLOCK, nh, MLA_ROPE).transpose(1, 0, 2, 3, 4)
    key_chunk = jnp.arange(seq) // CHUNK

    def one_block(args):
        blk, qn_b, qr_b = args
        s = (jnp.einsum('bqhd,bkhd->bhqk', qn_b, k_nope, preferred_element_type=jnp.float32)
             + jnp.einsum('bqhr,bkr->bhqk', qr_b, k_rope, preferred_element_type=jnp.float32)) * scale
        q_chunk = (blk * Q_BLOCK + jnp.arange(Q_BLOCK)) // CHUNK
        mask = key_chunk[None, :] <= q_chunk[:, None]
        s = jnp.where(mask[None, None], s, -jnp.inf)
        p = jax.nn.softmax(s, axis=-1).astype(v.dtype)
        return jnp.einsum('bhqk,bkhd->bqhd', p, v)

    o = lax.map(one_block, (jnp.arange(nb), qn, qr))
    return o.transpose(1, 0, 2, 3, 4).reshape(bsz, seq, nh, MLA_V)

def mla_mixer(h, cos, sin, w_in, q_norm, kv_norm, w_uq, w_ukv, w_out):
    bsz, seq, _ = h.shape
    proj = h @ w_in
    c_q = rmsnorm(proj[..., :MLA_Q_LORA], q_norm)
    c_kv = rmsnorm(proj[..., MLA_Q_LORA:MLA_Q_LORA + MLA_KV_LORA], kv_norm)
    k_rope = apply_rope(proj[..., MLA_Q_LORA + MLA_KV_LORA:], cos, sin)
    q = (c_q @ w_uq).reshape(bsz, seq, MLA_HEADS, MLA_NOPE + MLA_ROPE)
    q_nope = q[..., :MLA_NOPE]
    q_rope = apply_rope(q[..., MLA_NOPE:], cos[:, :, None, :], sin[:, :, None, :])
    kv = (c_kv @ w_ukv).reshape(bsz, seq, MLA_HEADS, MLA_NOPE + MLA_V)
    k_nope = kv[..., :MLA_NOPE]
    v = kv[..., MLA_NOPE:]
    o = chunk_causal_mla_attention(q_nope, q_rope, k_nope, k_rope, v)
    return o.reshape(bsz, seq, MLA_HEADS * MLA_V) @ w_out

def causal_depthwise_conv_2(u, w, b):
    y = lax.conv_general_dilated(
        u, w[:, None, :].astype(u.dtype), window_strides=(1,), padding=[(SSM_CONV - 1, 0)],
        dimension_numbers=('NWC', 'WIO', 'NWC'), feature_group_count=u.shape[-1])
    return y + b.astype(u.dtype)

def ssd_chunked(x, dt, a, bm, cm):
    bsz, seq = x.shape[:2]
    nc = seq // SSM_CHUNK
    L = SSM_CHUNK
    x = x.reshape(bsz, nc, L, SSM_GROUPS, SSM_HPG, SSM_HEADDIM)
    dt = dt.reshape(bsz, nc, L, SSM_GROUPS, SSM_HPG)
    bm = bm.reshape(bsz, nc, L, SSM_GROUPS, SSM_STATE)
    cm = cm.reshape(bsz, nc, L, SSM_GROUPS, SSM_STATE)
    a_cs = jnp.cumsum(dt * a.reshape(SSM_GROUPS, SSM_HPG), axis=2)
    xdt = x * dt[..., None]
    a_t = a_cs.transpose(0, 1, 3, 4, 2)
    seg = a_t[..., :, None] - a_t[..., None, :]
    causal = jnp.tril(jnp.ones((L, L), dtype=bool))
    decay = jnp.where(causal, jnp.exp(jnp.where(causal, seg, 0.0)), 0.0)
    cb = jnp.einsum('bclgn,bcsgn->bcgls', cm, bm)
    y_diag = jnp.einsum('bcgls,bcghls,bcsghp->bclghp', cb, decay, xdt)
    decay_to_end = jnp.exp(a_cs[:, :, -1:] - a_cs)
    states = jnp.einsum('bclgn,bclgh,bclghp->bcghpn', bm, decay_to_end, xdt)
    chunk_decay = jnp.exp(a_cs[:, :, -1])

    def step(state, inp):
        st_c, dec_c = inp
        return state * dec_c[..., None, None] + st_c, state

    init = jnp.zeros((bsz, SSM_GROUPS, SSM_HPG, SSM_HEADDIM, SSM_STATE), jnp.float32)
    _, prev = lax.scan(step, init, (jnp.moveaxis(states, 1, 0), jnp.moveaxis(chunk_decay, 1, 0)))
    prev = jnp.moveaxis(prev, 0, 1)
    y_off = jnp.einsum('bclgn,bcghpn,bclgh->bclghp', cm, prev, jnp.exp(a_cs))
    return (y_diag + y_off).reshape(bsz, seq, SSM_HEADS, SSM_HEADDIM)

def mamba2_mixer(h, w_in, conv_w, conv_b, dt_bias, a_log, d_skip, norm_g, w_out):
    bsz, seq, _ = h.shape
    proj = h @ w_in
    z = proj[..., :D_INNER]
    xbc = jax.nn.silu(causal_depthwise_conv_2(proj[..., D_INNER:D_INNER + CONV_DIM_2], conv_w, conv_b))
    dt_raw = proj[..., D_INNER + CONV_DIM_2:]
    xs = xbc[..., :D_INNER].reshape(bsz, seq, SSM_HEADS, SSM_HEADDIM).astype(jnp.float32)
    bm = xbc[..., D_INNER:D_INNER + SSM_GROUPS * SSM_STATE].reshape(bsz, seq, SSM_GROUPS, SSM_STATE).astype(jnp.float32)
    cm = xbc[..., D_INNER + SSM_GROUPS * SSM_STATE:].reshape(bsz, seq, SSM_GROUPS, SSM_STATE).astype(jnp.float32)
    dt = jax.nn.softplus(dt_raw.astype(jnp.float32) + dt_bias.astype(jnp.float32))
    a = -jnp.exp(a_log.astype(jnp.float32))
    y = ssd_chunked(xs, dt, a, bm, cm) + d_skip.astype(jnp.float32)[:, None] * xs
    y = y.reshape(bsz, seq, D_INNER).astype(h.dtype)
    yg = (y * jax.nn.silu(z)).reshape(bsz, seq, SSM_GROUPS, D_INNER // SSM_GROUPS)
    yf = yg.astype(jnp.float32)
    yf = yf * lax.rsqrt(jnp.mean(yf * yf, axis=-1, keepdims=True) + EPS)
    y = (yf.reshape(bsz, seq, D_INNER) * norm_g.astype(jnp.float32)).astype(h.dtype)
    return y @ w_out

def swiglu(t, w_gate, w_up, w_down):
    return (jax.nn.silu(t @ w_gate) * (t @ w_up)) @ w_down

def moe_swiglu(h, w_router, w_gate, w_up, w_down):
    bsz, seq, d = h.shape
    t = h.reshape(bsz * seq, d)
    logits = (t @ w_router).astype(jnp.float32)
    top_vals, top_idx = lax.top_k(logits, TOP_K)
    top_w = jax.nn.softmax(top_vals, axis=-1)
    gates = jnp.sum(jax.nn.one_hot(top_idx, N_EXPERTS_2, dtype=jnp.float32) * top_w[..., None], axis=1)
    out = jnp.zeros_like(t)
    for e in range(N_EXPERTS_2):
        out = out + gates[:, e:e + 1].astype(t.dtype) * swiglu(t, w_gate[e], w_up[e], w_down[e])
    return out.reshape(bsz, seq, d)

def second_inputs(seed: int = 0) -> dict:
    key = jax.random.key(seed)
    ks = jax.random.split(key, 40)
    n_att = (DEPTH_2 + 1) // 2
    n_ssm = DEPTH_2 // 2
    f32 = jnp.float32

    def nrm(i, shape, fan_in, mult=1.0):
        return jax.random.normal(ks[i], shape, f32) * (mult * fan_in ** -0.5)

    def gain(i, shape):
        return 1.0 + 0.1 * jax.random.normal(ks[i], shape, f32)

    x = jax.random.normal(ks[0], (BATCH, SEQ, D_MODEL), f32)
    c = jax.random.normal(ks[1], (BATCH, D_MODEL), f32)
    offsets = jax.random.randint(ks[2], (BATCH, 1), 0, 4096, dtype=jnp.int32)
    positions = (jnp.arange(SEQ, dtype=jnp.int32)[None, :] + offsets).astype(jnp.int32)
    dt0 = jnp.exp(jax.random.uniform(ks[3], (n_ssm, SSM_HEADS), f32, np.log(1e-3), np.log(1e-1)))
    return {
        "x": x,
        "c": c,
        "positions": positions,
        "ada_w": nrm(4, (DEPTH_2, D_MODEL, 6 * D_MODEL), D_MODEL, 0.5),
        "ada_b": 0.02 * jax.random.normal(ks[5], (DEPTH_2, 6 * D_MODEL), f32),
        "norm_g": gain(6, (DEPTH_2, 2, D_MODEL)),
        "mla_w_in": nrm(7, (n_att, D_MODEL, MLA_IN), D_MODEL),
        "mla_q_norm": gain(8, (n_att, MLA_Q_LORA)),
        "mla_kv_norm": gain(9, (n_att, MLA_KV_LORA)),
        "mla_w_uq": nrm(10, (n_att, MLA_Q_LORA, MLA_HEADS * (MLA_NOPE + MLA_ROPE)), MLA_Q_LORA),
        "mla_w_ukv": nrm(11, (n_att, MLA_KV_LORA, MLA_HEADS * (MLA_NOPE + MLA_V)), MLA_KV_LORA),
        "mla_w_out": nrm(12, (n_att, MLA_HEADS * MLA_V, D_MODEL), MLA_HEADS * MLA_V),
        "ssm_w_in": nrm(13, (n_ssm, D_MODEL, SSM_IN), D_MODEL),
        "ssm_conv_w": nrm(14, (n_ssm, SSM_CONV, CONV_DIM_2), SSM_CONV),
        "ssm_conv_b": 0.02 * jax.random.normal(ks[15], (n_ssm, CONV_DIM_2), f32),
        "ssm_dt_bias": dt0 + jnp.log(-jnp.expm1(-dt0)),
        "ssm_a_log": jnp.log(jax.random.uniform(ks[16], (n_ssm, SSM_HEADS), f32, 1.0, 16.0)),
        "ssm_d": gain(17, (n_ssm, SSM_HEADS)),
        "ssm_norm": gain(18, (n_ssm, D_INNER)),
        "ssm_w_out": nrm(19, (n_ssm, D_INNER, D_MODEL), D_INNER),
        "ffn_w_gate": nrm(20, (n_att, D_MODEL, D_FF), D_MODEL),
        "ffn_w_up": nrm(21, (n_att, D_MODEL, D_FF), D_MODEL),
        "ffn_w_down": nrm(22, (n_att, D_FF, D_MODEL), D_FF),
        "moe_w_router": nrm(23, (n_ssm, D_MODEL, N_EXPERTS_2), D_MODEL),
        "moe_w_gate": nrm(24, (n_ssm, N_EXPERTS_2, D_MODEL, D_EXPERT), D_MODEL),
        "moe_w_up": nrm(25, (n_ssm, N_EXPERTS_2, D_MODEL, D_EXPERT), D_MODEL),
        "moe_w_down": nrm(26, (n_ssm, N_EXPERTS_2, D_EXPERT, D_MODEL), D_EXPERT),
        "final_norm": gain(27, (D_MODEL,)),
    }

def second_block(x, c, positions, ada_w, ada_b, norm_g,
              mla_w_in, mla_q_norm, mla_kv_norm, mla_w_uq, mla_w_ukv, mla_w_out,
              ssm_w_in, ssm_conv_w, ssm_conv_b, ssm_dt_bias, ssm_a_log, ssm_d, ssm_norm, ssm_w_out,
              ffn_w_gate, ffn_w_up, ffn_w_down,
              moe_w_router, moe_w_gate, moe_w_up, moe_w_down, final_norm):
    cos, sin = rope_tables(positions)
    cond = jax.nn.silu(c)
    for i in range(DEPTH_2):
        j = i // N_MIXERS
        mod = cond @ ada_w[i] + ada_b[i]
        sh1, sc1, g1, sh2, sc2, g2 = jnp.split(mod, 6, axis=-1)
        h = modulate(rmsnorm(x, norm_g[i, 0]), sh1, sc1)
        if i % N_MIXERS == 0:
            y = mla_mixer(h, cos, sin, mla_w_in[j], mla_q_norm[j], mla_kv_norm[j],
                          mla_w_uq[j], mla_w_ukv[j], mla_w_out[j])
        else:
            y = mamba2_mixer(h, ssm_w_in[j], ssm_conv_w[j], ssm_conv_b[j], ssm_dt_bias[j],
                             ssm_a_log[j], ssm_d[j], ssm_norm[j], ssm_w_out[j])
        x = x + g1[:, None, :] * y
        h = modulate(rmsnorm(x, norm_g[i, 1]), sh2, sc2)
        if i % 2 == 0:
            y = swiglu(h, ffn_w_gate[j], ffn_w_up[j], ffn_w_down[j])
        else:
            y = moe_swiglu(h, moe_w_router[j], moe_w_gate[j], moe_w_up[j], moe_w_down[j])
        x = x + g2[:, None, :] * y
    return rmsnorm(x, final_norm)


def setup_inputs(seed=0):
    out = dict(first_inputs(seed))
    for name, value in second_inputs(seed + 1).items():
        if name != "x":
            out[name + "_2"] = value
    return out


def reference(
    x, norm_mix, w_in, conv_a_w, nsa_qk_gain, cmp_pe, cmp_w1, cmp_w2, gdn_conv_w, gdn_a_log,
    gdn_dt_bias, gdn_out_gain, w_branch, w_gate, b_gate, w_out, norm_ffn, w_router_group,
    b_router_group, w_router_expert, b_router_expert, w_expert_gate, w_expert_up, w_expert_down,
    c_2, positions_2, ada_w_2, ada_b_2, norm_g_2, mla_w_in_2, mla_q_norm_2, mla_kv_norm_2,
    mla_w_uq_2, mla_w_ukv_2, mla_w_out_2, ssm_w_in_2, ssm_conv_w_2, ssm_conv_b_2, ssm_dt_bias_2,
    ssm_a_log_2, ssm_d_2, ssm_norm_2, ssm_w_out_2, ffn_w_gate_2, ffn_w_up_2, ffn_w_down_2,
    moe_w_router_2, moe_w_gate_2, moe_w_up_2, moe_w_down_2, final_norm_2,
):
    x = first_block(
        x, norm_mix, w_in, conv_a_w, nsa_qk_gain, cmp_pe, cmp_w1, cmp_w2, gdn_conv_w, gdn_a_log,
        gdn_dt_bias, gdn_out_gain, w_branch, w_gate, b_gate, w_out, norm_ffn, w_router_group,
        b_router_group, w_router_expert, b_router_expert, w_expert_gate, w_expert_up,
        w_expert_down,
    )
    return second_block(
        x, c_2, positions_2, ada_w_2, ada_b_2, norm_g_2, mla_w_in_2, mla_q_norm_2,
        mla_kv_norm_2, mla_w_uq_2, mla_w_ukv_2, mla_w_out_2, ssm_w_in_2, ssm_conv_w_2,
        ssm_conv_b_2, ssm_dt_bias_2, ssm_a_log_2, ssm_d_2, ssm_norm_2, ssm_w_out_2,
        ffn_w_gate_2, ffn_w_up_2, ffn_w_down_2, moe_w_router_2, moe_w_gate_2, moe_w_up_2,
        moe_w_down_2, final_norm_2,
    )


_drawn_inputs = setup_inputs


def setup_inputs(seed=0):
    import zlib

    import numpy as np

    out = dict(_drawn_inputs(seed))
    spreads = {}
    factors = {'nsa_qk_gain': 6.034,
     'cmp_pe': 8.0,
     'gdn_out_gain': 4.513,
     'b_gate': 8.0,
     'b_router_group': 5.425,
     'b_router_expert': 4.423,
     'mla_q_norm_2': 8.0,
     'mla_kv_norm_2': 4.15,
     'ssm_conv_b_2': 15.08,
     'ssm_d_2': 10.47,
     'ssm_norm_2': 3.048}
    for name, (base, spread) in spreads.items():
        noise = np.random.default_rng([zlib.crc32(name.encode()), seed]).standard_normal(out[name].shape)
        drawn = base * np.exp(spread * noise) if base else spread * noise
        out[name] = __import__('jax').numpy.asarray(drawn.astype(out[name].dtype))
    for name, factor in factors.items():
        out[name] = (out[name] * factor).astype(out[name].dtype)
    return out
```

```python
import math
from contextlib import ExitStack, contextmanager

import concourse.bass as bass
import numpy as np
from concourse import mybir

F32 = mybir.dt.float32
U32 = mybir.dt.uint32
ALU = mybir.AluOpType
ACT = mybir.ActivationFunctionType
AX = mybir.AxisListType

P = 128
T = 256
NT = T // P
D = 1024
KD = D // P
UNIT = 4096
SLOTS = 4
EPS = 1e-6
BIG = 1e30


class At:

    def __init__(self, f):
        self.f = f


def at(x, i):
    return x.f(i) if isinstance(x, At) else x


class Loop:
    def __init__(self, count):
        self.count, self.step = count, {}


class Mark:

    def __init__(self, counter, n, loop, back=0):
        self.counter, self.n, self.loop, self.back = counter, n, loop, back

    def value(self, i, loop):
        if self.loop is None:
            return self.n
        step = self.loop.step[self.counter]
        if loop is not self.loop:
            return self.n + (self.loop.count - 1) * step
        least = self.n - self.back * step
        assert least > 0
        return least if step == 0 else i * step + least


class Later:

    def __init__(self, back=0):
        self.marks, self.back = [], back

    def all(self):
        return [Mark(m.counter, m.n, m.loop, self.back) for m in self.marks]


class Counter:

    def __init__(self, sem):
        self.sem, self.n, self.loop = sem, 0, None

    def mark(self):
        return Mark(self, self.n, self.loop)


class Step:
    def __init__(self, op, args, kw, waits):
        self.op, self.args, self.kw, self.waits, self.raises = op, args, kw, waits, []


class Engine(Counter):

    def __init__(self, sem):
        super().__init__(sem)
        self.queue, self.waits, self.before_raise, self.registers = [], [], lambda: None, {}

    def wait(self, *marks):
        self.waits += [m for m in marks if m is not None]

    def put(self, op, *args, **kw):
        step = Step(op, args, kw, self.waits)
        self.waits = []
        self.queue.append(step)
        return step

    def wait_here(self):
        if self.waits:
            self.put(None)

    def raised(self, step, counter=None, by=1):
        if counter is None:
            counter = self
            self.before_raise()
        step.raises.append((counter.sem, by))
        counter.n += by
        return counter.mark()

    def __call__(self, op, *args, after=(), chain=True, **kw):
        if chain and self.n:
            self.wait(self.mark())
        self.wait(*after)
        return self.raised(self.put(op, *args, **kw))

    def play(self, eng, queue=None, i=None, loop=None):
        for step in self.queue if queue is None else queue:
            if isinstance(step, Load):
                for m in [x for w in step.waits for x in (w.all() if isinstance(w, Later) else [w])]:
                    eng.wait_ge(m.counter.sem, m.value(i, loop))
                self.registers[step.name] = eng.value_load(step.ap, min_val=step.low, max_val=step.high)
                continue
            if isinstance(step, Case):
                with eng.If(self.registers[step.number] > step.least):
                    self.play(eng, step.queue, self.registers[step.index], None)
                with eng.Else():
                    for sem, reached, by in step.raises:
                        eng.wait_ge(sem, reached)
                        eng.sem_inc(sem, by)
                continue
            if isinstance(step, tuple):
                with eng.Fori(0, step[0].count) as j:
                    self.play(eng, step[1], j, step[0])
                continue
            best = {}
            for m in [x for w in step.waits for x in (w.all() if isinstance(w, Later) else [w])]:
                key = (m.counter, m.loop is loop, m.back)
                if key not in best or m.n > best[key].n:
                    best[key] = m
            for m in best.values():
                eng.wait_ge(m.counter.sem, m.value(i, loop))
            if step.op is None:
                continue
            ins = step.op(*[at(a, i) for a in step.args], **{k: at(v, i) for k, v in step.kw.items()})
            for sem, by in step.raises:
                ins.then_inc(sem, by)


class Load:

    def __init__(self, name, ap, low, high, waits):
        self.name, self.ap, self.low, self.high, self.waits = name, ap, low, high, waits


class Case:

    def __init__(self, number, least, index, queue, raises):
        self.number, self.least, self.index, self.queue, self.raises = number, least, index, queue, raises


@contextmanager
def repeat(count, engines, counters=()):
    loop = Loop(count)
    kept = {}
    for e in engines:
        e.wait_here()
        kept[e] = (e.queue, e.n)
        e.queue, e.loop = [], loop
    for c in counters:
        kept[c] = (None, c.n)
        c.loop = loop
    yield loop
    for c, (queue, n) in kept.items():
        loop.step[c] = c.n - n
        c.n = n + count * (c.n - n)
        c.loop = None
        if queue is not None:
            queue.append((loop, c.queue))
            c.queue = queue


def block(nc, A, out):
    ctx = ExitStack()
    V, S, G, PE_ = nc.vector, nc.scalar, nc.gpsimd, nc.tensor

    def semaphore(name):
        return ctx.enter_context(nc.semaphore(name))

    dve, act, pool, pe, sp = (Engine(semaphore("steps_" + n)) for n in ("dve", "act", "pool", "pe", "sp"))
    everyone = (dve, act, pool, pe)
    small_loads = Counter(semaphore("small_loads"))
    slot_loaded = [semaphore(f"slot_loaded{n}") for n in range(SLOTS)]
    unit_used = Counter(semaphore("unit_used"))
    stored = Counter(semaphore("stored"))

    def sb(name, shape, dt=F32, where=None):
        return (where or ctx).enter_context(nc.sbuf_tensor(name, shape, dt))

    ring = sb("ring", [P, SLOTS, UNIT])
    sent = [0, None]
    used = [0, None]

    def unit_value(n, loop_of, add):
        loop = loop_of[1]
        if loop is None:
            return n + add
        return At(lambda i: i * loop.units + n + add)

    def send(src, columns):
        n, slot = sent[0], sent[0] % SLOTS
        dst = ring[:, slot, 0:columns]
        if n >= SLOTS or sent[1] is not None:
            sp.put(nc.sync.wait_ge, unit_used.sem, unit_value(n, sent, 1 - SLOTS))
        shape = at(src, 0).shape
        if len(shape) == 3:
            dst = dst.rearrange("p (k n) -> p k n", k=shape[1])
        step = sp.put(nc.sync.dma_start, dst, src)
        step.raises.append((slot_loaded[slot], 16))
        sent[0] += 1

    sp_skipped = [0] * SLOTS

    def skip_to_slot_0():
        for slot in range(sent[0] % SLOTS, SLOTS):
            sp_skipped[slot] += 1
        sent[0] += SLOTS - sent[0] % SLOTS

    def take(eng=pe):
        n, slot = used[0], used[0] % SLOTS
        loads = 16 * (n // SLOTS + 1 - skipped[slot])
        loop = used[1]
        value = loads if loop is None else At(lambda i: i * (16 * loop.units // SLOTS) + loads)
        eng.put(wait_op[eng], slot_loaded[slot], value)
        used[0] += 1
        return ring[:, slot, :]

    wait_op = {pe: nc.tensor.wait_ge, dve: nc.vector.wait_ge, act: nc.scalar.wait_ge}
    skipped = [0] * SLOTS

    pending = [0, 0]

    def give():
        signal_used()
        pending[0] += 1
        pending[1] = len(pe.queue)

    def signal_now(more=0):
        if pending[0] + more:
            pe.wait(pe.mark())
            pe.put(nc.tensor.sem_inc, unit_used.sem, pending[0] + more)
            unit_used.n += pending[0] + more
            pending[0] = 0

    def signal_used():
        if pending[0]:
            for step in pe.queue[pending[1]:-1]:
                if isinstance(step, Step) and step.op in (PE_.matmul, PE_.transpose) and not step.raises:
                    pe.raised(step, unit_used, pending[0])
                    pending[0] = 0
                    return

    pe.before_raise = signal_used

    def rows(w, k0=0, k1=None):
        return w.rearrange("(k p) n -> p k n", p=P)[:, k0:k1, :]

    MOST_OVER = NT * P * 2 // (P + 1)
    E_OF = {"a": 32, "b": 8}
    tables = {tag: sb("table_" + tag, [1, 4], mybir.dt.int32) for tag in "ab"}
    table_ready = {tag: Later() for tag in "ab"}

    def columns_of(w, c0, n):
        kt = w.shape[0] // P
        send(rows(w[:, c0:c0 + n]), kt * n)

    def mlp_units(gate, up, down, F):
        for c0 in range(0, F, 512):
            n = min(512, F - c0)
            for w in (gate, up):
                send(At(lambda i, w=w, c0=c0, n=n: rows(w(i)[:, c0:c0 + n])), KD * n)
        for r0 in range(0, F, 512):
            n = min(512, F - r0)
            send(At(lambda i, r0=r0, n=n: rows(down(i)[r0:r0 + n, :])), (n // P) * D)

    w_in = A["w_in"][0]
    w_branch, w_gate, w_out = A["w_branch"][0], A["w_gate"][0], A["w_out"][0]
    ssm_in, ssm_out = A["ssm_w_in_2"][0], A["ssm_w_out_2"][0]
    O_Q, O_KV, O_NG, O_GQ, O_GZ, O_GB = 1536, 2048, 2816, 2840, 4376, 4888

    ADA = 6144 // 16
    ada_loaded = [semaphore(f"ada_loaded{b}") for b in range(2)]
    ada_used = Counter(semaphore("ada_used"))

    def send_ada(j):
        sp.put(nc.sync.wait_ge, ada_used.sem, At(lambda i: 4 * i + j + 1))
        step = sp.put(nc.sync.dma_start, At(lambda i: ada_place[0][:, j % 2, :, :]),
                      At(lambda i: rows(A["ada_w_2"][j // 2][:, bass.ds((2 * i + j % 2) * ADA, ADA)])))
        step.raises.append((ada_loaded[j % 2], 16))

    ada_place = []

    def start_loop(count, units):
        loop = Loop(count)
        loop.units = units
        return loop

    def stream():
        for c0 in (0, 512, 1024, O_GQ, O_GQ + 512, O_GQ + 1024, O_GZ, O_Q, O_KV):
            columns_of(w_in, c0, 512)
        columns_of(w_in, O_KV + 512, 256)
        for j in range(2):
            columns_of(A["cmp_w1"][0][j], 0, 256)
        for r in range(3):
            columns_of(w_branch[r], 0, 1024)
            for half in range(2):
                columns_of(w_gate, 1024 * r + 512 * half, 512)
        for half in range(2):
            columns_of(w_out, 512 * half, 512)
        first_moe_units()
        columns_of(A["mla_w_in_2"][0], 0, 512)
        columns_of(A["mla_w_in_2"][0], 512, 160)
        for c in range(2):
            columns_of(A["mla_w_uq_2"][0], 768 * c, 768)
        columns_of(A["mla_w_ukv_2"][0], 0, 2048)
        for half in range(2):
            columns_of(A["mla_w_out_2"][0], 512 * half, 512)
        mlp_units(lambda i: A["ffn_w_gate_2"][0], lambda i: A["ffn_w_up_2"][0],
                  lambda i: A["ffn_w_down_2"][0], 2816)
        for c in range(10):
            columns_of(ssm_in, 512 * c, 512)
        for q in range(4):
            send(rows(ssm_out, 4 * q, 4 * q + 4), 4096)
        second_moe_units()

    def first_moe_units():
        skip_to_slot_0()
        count, units = 8, 12
        names = ("w_expert_gate", "w_expert_up", "w_expert_down")
        with repeat(count, [sp]) as loop:
            loop.units, sent[1] = units, loop
            for j in range(4):
                mlp_units(*(lambda i, w=w, j=j: A[w][0][4 * i + j] for w in names), 512)
                send_ada(j)
        sent[0] += (count - 1) * units
        sent[1] = None
        overflow_units("a", names, 512)

    def second_moe_units():
        skip_to_slot_0()
        count, units = 4, 36
        names = ("moe_w_gate_2", "moe_w_up_2", "moe_w_down_2")
        with repeat(count, [sp]) as loop:
            loop.units, sent[1] = units, loop
            for j in range(2):
                mlp_units(*(lambda i, w=w, j=j: A[w][0][2 * i + j] for w in names), 2816)
        sent[0] += (count - 1) * units
        sent[1] = None
        overflow_units("b", names, 2816)

    def overflow_units(tag, names, F):
        sp.wait(table_ready[tag])
        load_table(sp, tag)
        for k in range(MOST_OVER):
            first = sent[0]
            with case(tag, k, [sp]) as raises:
                mlp_units(*(lambda i, w=w: A[w][0][i] for w in names), F)
                for slot in range(SLOTS):
                    units_in = [n for n in range(first, sent[0]) if n % SLOTS == slot]
                    if units_in:
                        reached = 16 * (units_in[0] // SLOTS - sp_skipped[slot])
                        raises[sp].append((slot_loaded[slot], reached, 16 * len(units_in)))

    def load_table(e, tag):
        for n in range(1 + MOST_OVER):
            e.queue.append(Load(f"{tag}{n}", tables[tag][0:1, n:n + 1], 0, MOST_OVER if n == 0 else E_OF[tag] - 1, e.waits))
            e.waits = []

    @contextmanager
    def case(tag, k, engines):
        for e in engines:
            e.wait_here()
        kept = {e: (e.queue, e.n) for e in engines}
        raises = {e: [] for e in engines}
        for e in engines:
            e.queue = []
        yield raises
        for e in engines:
            e.wait_here()
            queue, n = kept[e]
            if e.n > n:
                raises[e].append((e.sem, n, e.n - n))
            queue.append(Case(f"{tag}0", k, f"{tag}{k + 1}", e.queue, raises[e]))
            e.queue = queue

    @contextmanager
    def unit_loop(count, units, counters=()):
        gap = SLOTS - used[0] % SLOTS
        for s in range(SLOTS - gap, SLOTS):
            skipped[s] += 1
        used[0] += gap
        signal_now(gap - 1)
        pending[0] = 1
        with repeat(count, [pe, act, dve], [unit_used, *counters]) as loop:
            loop.units, used[1] = units, loop
            assert pending[0] == 1
            pending[1], first = 0, used[0]
            yield loop
            assert pending[0] == 1 and used[0] - first == units
        pending[1] = len(pe.queue)
        used[0] += (count - 1) * units
        used[1] = None

    stream()

    psum = ctx.enter_context(nc.psum_tensor("psum", [P, 4, 1024], F32))
    pair_free = [[] for _ in range(4)]
    turn = [0]
    held = []

    def pair():
        while turn[0] % 4 in held:
            turn[0] += 1
        n = turn[0] % 4
        turn[0] += 1
        pe.wait(*pair_free[n])
        pair_free[n] = []
        return psum[:, n, :], pair_free[n]

    def product(o, terms):
        for n, (l, r) in enumerate(terms):
            step = pe.put(PE_.matmul, o, l, r, start=n == 0, stop=n == len(terms) - 1)
        return step

    def phase():
        marks = [e.mark() for e in everyone]
        for e in everyone:
            e.wait(*marks)
        return ExitStack()

    def load(dst, src):
        act.raised(act.put(nc.scalar.dma_start, dst, src), small_loads, 16)

    ident = sb("ident", [P, P])
    x = sb("x", [P, NT, D])
    hT = sb("hT", [P, KD, T])
    NCOL = 4 * P
    cols = sb("cols", [P, NCOL])
    eps = sb("eps", [P, 1])
    rows512 = sb("rows512", [6, 512])
    w_thin = sb("w_thin", [P, KD, 64])
    w_rout = sb("w_rout", [P, KD, 44])
    b_rout = sb("b_rout", [P, 36])
    cmp_w2 = sb("cmp_w2", [P, 2, 2, 64])
    gains = sb("gains", [P, 4, 64])
    gdn_ab = sb("gdn_ab", [P, 8])
    ssm_v = sb("ssm_v", [P, 3, 32])
    upper = sb("upper", [P, P])
    ones = sb("ones", [P, P])

    load(x[:, :, :], A["x"][0].rearrange("(t p) n -> p t n", p=P))
    start = ExitStack()
    staged = sb("staged", [P, 4, P], where=start)
    row = [0, 0]
    where = {}

    def stage(name, src, n):
        g, r = row
        load(staged[r:r + n, g, :], src)
        where[name] = g * P + r
        row[1] += n

    def flat(a):
        dims = " ".join("abcd"[:len(a.shape)])
        return a.rearrange(f"{dims} -> ({dims})").rearrange("(r p) -> r p", p=P)

    for name, n in (("norm_mix", 8), ("norm_ffn", 8), ("norm_g_2", 32), ("conv_a_w", 12),
                    ("gdn_conv_w", 48), ("gdn_out_gain", 1), ("mla_q_norm_2", 3), ("mla_kv_norm_2", 2)):
        stage(name, flat(A[name]), n)
    row[:] = [1, 0]
    for name, n in (("cmp_pe", 32), ("ssm_norm_2", 16), ("ssm_conv_b_2", 24), ("c_2", 8)):
        stage(name, flat(A[name]), n)
    row[:] = [2, 0]
    stage("ssm_conv_w_2", flat(A["ssm_conv_w_2"]), 96)
    row[:] = [3, 0]
    stage("ada_b_2", flat(A["ada_b_2"]), 96)

    def col(name, n=0):
        return cols[:, where[name] + n:where[name] + n + 1]

    def colrange(name, n0, n1):
        return cols[:, where[name] + n0:where[name] + n1]

    load(rows512[:, :], A["b_gate"].rearrange("l (r n) -> (l r) n", n=512))
    load(w_thin[:, :, 0:24], rows(w_in[:, O_NG:O_NG + 24]))
    load(w_thin[:, :, 24:32], rows(w_in[:, O_GB:O_GB + 8]))
    load(w_thin[:, :, 32:64], rows(ssm_in[:, 5120:5152]))
    load(w_rout[:, :, 0:4], rows(A["w_router_group"][0]))
    load(w_rout[:, :, 4:36], rows(A["w_router_expert"][0]))
    load(w_rout[:, :, 36:44], rows(A["moe_w_router_2"][0]))
    load(b_rout[:, 0:4], A["b_router_group"][0].partition_broadcast(P))
    load(b_rout[:, 4:36], A["b_router_expert"][0].partition_broadcast(P))
    load(cmp_w2[:, 0, :, :], rows(A["cmp_w2"][0][0]))
    load(cmp_w2[:, 1, :, :], rows(A["cmp_w2"][0][1]))
    load(gains[:, :, :].rearrange("p a b -> p (a b)"),
         A["nsa_qk_gain"][0].rearrange("a b -> (a b)").partition_broadcast(P))
    load(gdn_ab[:, 0:4], A["gdn_a_log"][0].partition_broadcast(P))
    load(gdn_ab[:, 4:8], A["gdn_dt_bias"][0].partition_broadcast(P))
    for n, name in enumerate(("ssm_dt_bias_2", "ssm_a_log_2", "ssm_d_2")):
        load(ssm_v[:, n, :], A[name][0].partition_broadcast(P))
    all_small = small_loads.mark()

    pool(G.memset, ident[:, :], 0.0)
    ident_ready = pool(G.affine_select, out=ident[:, :], in_=ident[:, :], compare_op=ALU.not_equal,
                       fill=1.0, base=0, pattern=[[-1, P]], channel_multiplier=1)
    pool(G.memset, eps[:, :], EPS)
    pool(G.memset, upper[:, :], 1.0)
    pool(G.affine_select, out=upper[:, :], in_=upper[:, :], compare_op=ALU.is_ge, fill=0.0,
         base=0, pattern=[[1, P]], channel_multiplier=-1)
    pool(G.memset, ones[:, :], 1.0)
    consts = pool.mark()

    dve.wait(ident_ready)
    pe.wait(ident_ready, all_small)
    ps, free = pair()
    for g, n in ((0, 114), (1, 80), (2, 96), (3, 96)):
        step = pe.put(PE_.transpose, ps[:, g * P:g * P + n], staged[0:n, g, :], ident[0:n, 0:n])
    m = pe.raised(step)
    for g, n in ((0, 114), (1, 80), (2, 96), (3, 96)):
        m = dve(V.tensor_copy, cols[:, g * P:g * P + n], ps[:, g * P:g * P + n], after=[m])
    free.append(m)
    cols_ready = m
    for e in everyone:
        e.wait(all_small, consts, cols_ready)
    start_marks = phase()
    start.close()

    def rsqrt(dst, src, scale, after=()):
        act(S.activation, dst, src, ACT.Ln, bias=eps[0:dst.shape[0], :], scale=scale, after=after)
        return act(S.activation, dst, dst, ACT.Exp, scale=-0.5)

    def norm_transposed(gain, shift, where, tag):
        xn = sb("xn" + tag, [P, NT, D], where=where)
        ss = sb("ss" + tag, [P, NT], where=where)
        for t in range(NT):
            act(S.activation, xn[:, t, :], x[:, t, :], ACT.Square, accum_out=ss[:, t:t + 1], after=[dve.mark()])
        m = rsqrt(ss[:, :], ss[:, :], 1.0 / D)
        for t in range(NT):
            m = dve(V.tensor_scalar, xn[:, t, :], x[:, t, :], ss[:, t:t + 1], None, ALU.mult, after=[m])
        pe.wait(m)
        for k4 in range(0, KD, 4):
            ps, free = pair()
            for k in range(4):
                for t in range(NT):
                    step = pe.put(PE_.transpose, ps[:, k * T + t * P:k * T + t * P + P],
                                  xn[:, t, (k4 + k) * P:(k4 + k + 1) * P], ident[:, :])
            m = pe.raised(step)
            for k in range(4):
                src = ps[:, k * T:(k + 1) * T]
                if shift is None:
                    last = dve(V.tensor_scalar, hT[:, k4 + k, :], src, gain(k4 + k), None, ALU.mult, after=[m])
                else:
                    last = dve(V.tensor_scalar, hT[:, k4 + k, :], src, gain(k4 + k), shift(k4 + k),
                               ALU.mult, ALU.add, after=[m])
            free.append(last)
        return last, xn

    def by_feature(w, f, o):
        return product(o, [(w[:, k, f * P:(f + 1) * P], hT[:, k, :]) for k in range(KD)])

    def unit_by_feature(evacuate, n_tiles=4):
        w = take().rearrange("p (k n) -> p k n", k=KD)
        ps, free = pair()
        for f in range(n_tiles):
            step = by_feature(w, f, ps[:, f * T:(f + 1) * T])
        give()
        m = pe.raised(step)
        free.append(evacuate(ps.rearrange("p (f t) -> p f t", f=4), m))

    def unit_by_token(n, evacuate, src=None, kt=KD):
        src = hT if src is None else src
        w = take()[:, 0:kt * n].rearrange("p (k n) -> p k n", k=kt)
        ps, free = pair()
        for t in range(NT):
            step = product(ps[:, t * 512:t * 512 + n],
                           [(src[:, k, t * P:(t + 1) * P], w[:, k, 0:n]) for k in range(kt)])
        give()
        m = pe.raised(step)
        free.append(evacuate(ps.rearrange("p (t n) -> p t n", t=NT)[:, :, 0:n], m))

    def by_token_rows(dst, c0, n, kt=KD):
        return lambda ps, m: act(S.copy, dst[:, :, c0:c0 + n], ps, after=[m])

    def transposed(jobs, copy_out):
        for n0 in range(0, len(jobs), 8):
            ps, free = pair()
            part = jobs[n0:n0 + 8]
            for n, src in enumerate(part):
                r, c = src.shape[0], src.shape[1]
                step = pe.put(PE_.transpose, ps[0:c, n * P:n * P + r], src, ident[0:r, 0:r])
            m = pe.raised(step)
            free.append(copy_out(n0, len(part), ps, m))

    def attention(name, jobs, n_keys, scale, where):
        AHEAD = 2
        s = [sb(f"{name}_s{b}", [P, 4, n_keys], where=where) for b in range(AHEAD + 1)]
        pT = [sb(f"{name}_pT{b}", [P, 8, P], where=where) for b in range(2)]
        mx = sb(f"{name}_mx", [P, len(jobs), 4], where=where)
        den = sb(f"{name}_den", [P, len(jobs), 4], where=where)
        shown, probs, out_done = {}, {}, {}

        def scores(n):
            job = jobs[n]
            nk = job["n_keys"]
            if job.get("prepare"):
                job["prepare"]()
            ps, free = pair()
            for j in range(4):
                step = product(ps[:, j * 256:j * 256 + nk], [(job["queries"](j), job["keys"](j)[:, 0:nk])])
            job["multiplied"] = m = pe.raised(step)
            psv = ps.rearrange("p (h k) -> p h k", h=4)[:, :, 0:nk]
            sv = s[n % (AHEAD + 1)][:, :, 0:nk]
            free.append(job["score"](psv, sv, [m, shown.get(n - AHEAD - 1)]))
            dve(V.tensor_reduce, mx[:, n, :], sv, AX.X, ALU.max)
            m = dve(V.tensor_scalar, mx[:, n, :], mx[:, n, :], -scale, None, ALU.mult)
            for j in range(4):
                m2 = act(S.activation, sv[:, j, :], sv[:, j, :], ACT.Exp, bias=mx[:, n, j:j + 1],
                         scale=scale, accum_out=den[:, n, j:j + 1], after=[m], chain=False)
            probs[n] = m2

        def values(n):
            job = jobs[n]
            nk = job["n_keys"]
            parts = [(k0, min(P, nk - k0)) for k0 in range(0, nk, P)]
            pe.wait(probs[n])
            ps, free = pair()
            for j in range(4):
                for kt, (k0, kn) in enumerate(parts):
                    step = pe.put(PE_.transpose, ps[0:kn, (2 * j + kt) * P:(2 * j + kt + 1) * P],
                                  s[n % (AHEAD + 1)][:, j, k0:k0 + kn], ident[:, :])
            shown[n] = pe.raised(step)
            kn = parts[0][1]
            src = ps.rearrange("p (j c q) -> p j c q", j=4, c=2)[0:kn, :, 0:len(parts), :]
            dst = pT[n % 2][:, :, :].rearrange("p (j c) q -> p j c q", j=4)[0:kn, :, 0:len(parts), :]
            m = act(S.copy, dst, src, after=[shown[n], out_done.get(n - 2)], chain=False)
            free.append(m)
            pe.wait(m)
            ps, free = pair()
            for j in range(4):
                step = product(ps[:, j * 64:(j + 1) * 64],
                               [(pT[n % 2][0:kn, 2 * j + c, :], job["values"](j, c)) for c in range(len(parts))])
            out_done[n] = m = pe.raised(step)
            free.append(job["finish"](ps[:, 0:256].rearrange("p (h d) -> p h d", h=4), den[:, n, :], m))

        for n in range(len(jobs) + AHEAD):
            if n < len(jobs):
                scores(n)
            if n >= AHEAD:
                values(n - AHEAD)

    def conv_silu(padded, out_, f, w_cols, taps, bias=None, after=()):
        m = dve(V.tensor_scalar, out_, padded[:, f, 0:T], w_cols(0), None, ALU.mult, after=after)
        for j in range(1, taps):
            m = dve(V.scalar_tensor_tensor, out_, padded[:, f, j:j + T], w_cols(j), out_, ALU.mult, ALU.add)
        return m

    def softplus(dst, tmp, src, after=()):
        y, w, l = tmp
        dve(V.tensor_scalar, w, src, -1.0, None, ALU.mult, after=after)
        m = dve(V.tensor_tensor, w, w, src, ALU.min)
        m = act(S.activation, y, w, ACT.Exp, after=[m])
        m = dve(V.tensor_scalar, w, y, 1.0, None, ALU.add, after=[m])
        m = act(S.activation, l, w, ACT.Ln, after=[m])
        dve(V.tensor_scalar, w, w, -1.0, 1e-30, ALU.add, ALU.max, after=[m])
        dve(V.reciprocal, w, w)
        dve(V.tensor_tensor, w, w, y, ALU.mult)
        dve(V.tensor_tensor, l, l, w, ALU.mult)
        return dve(V.scalar_tensor_tensor, dst, src, 0.0, l, ALU.max, ALU.add)

    mix = ExitStack()
    tmp = ExitStack()
    m, _ = norm_transposed(lambda k: col("norm_mix", k), None, tmp, "a")
    phase()
    tmp.close()
    pe.wait(m)
    yT = sb("yT", [P, 3, 4, T], where=mix)
    thin = sb("thin", [P, NT, 32], where=mix)
    gates = sb("gates", [P, NT, 24], where=mix)

    cv = ExitStack()
    bT = sb("bT", [P, 4, T], where=cv)
    cT = sb("cT", [P, 4, T + 2], where=cv)
    m_pad = dve(V.memset, cT[:, :, 0:2], 0.0)
    unit_by_feature(lambda ps, m: act(S.copy, bT[:, :, :], ps, after=[m]))
    unit_by_feature(lambda ps, m: act(S.copy, cT[:, :, 2:T + 2], ps, after=[m, m_pad]))
    unit_by_feature(lambda ps, m: dve(V.tensor_tensor, cT[:, :, 2:T + 2], cT[:, :, 2:T + 2], ps, ALU.mult,
                                      after=[m, act.mark()]))
    for f in range(4):
        conv_silu(cT, yT[:, 0, f, :], f, lambda j, f=f: col("conv_a_w", 4 * j + f), 3)
    dve(V.tensor_tensor, yT[:, 0, :, :], yT[:, 0, :, :], bT[:, :, :], ALU.mult)
    phase()
    cv.close()

    gd = ExitStack()
    qkvT = sb("qkvT", [P, 12, T], where=gd)
    zT = sb("zT", [P, 4, T], where=gd)
    pad = ExitStack()
    upad = sb("upad", [P, 2, 4, T + 3], where=pad)
    m_pad = dve(V.memset, upad[:, :, :, 0:3], 0.0)
    act.wait(m_pad)
    conv_done = {}
    for u in range(3):
        buf = upad[:, u % 2, :, :]
        def evacuate(ps, m, buf=buf, u=u):
            return act(S.copy, buf[:, :, 3:T + 3], ps, after=[m, conv_done.get(u - 2)])
        unit_by_feature(evacuate)
        for f in range(4):
            c = 4 * u + f
            conv_done[u] = conv_silu(buf, qkvT[:, c, :], f, lambda j, c=c: col("gdn_conv_w", 12 * j + c), 4,
                                     after=[act.mark()])
    unit_by_feature(lambda ps, m: act(S.activation, zT[:, :, :], ps, ACT.Silu, after=[m]))
    silu_done = act(S.activation, qkvT[:, :, :], qkvT[:, :, :], ACT.Silu, after=[dve.mark()])
    phase()
    pad.close()

    ps, free = pair()
    for t in range(NT):
        step = product(ps[:, t * 512:t * 512 + 32],
                       [(hT[:, k, t * P:(t + 1) * P], w_thin[:, k, 0:32]) for k in range(KD)])
    m = pe.raised(step)
    free.append(act(S.copy, thin[:, :, :], ps.rearrange("p (t n) -> p t n", t=NT)[:, :, 0:32], after=[m]))

    shared = sb("shared", [P, 4, 8, P], where=gd)
    sq = shared[:, 0:2, :, :].rearrange("p a n c -> p (a n c)").rearrange("p (n t) -> p n t", t=T)
    act(S.activation, sq[:, :, :], qkvT[:, 0:8, :], ACT.Square)
    rs = shared[:, 2:4, :, :].rearrange("p a n c -> p (a n c)").rearrange("p (n t) -> p n t", t=T)
    pe.wait(act.mark())
    for half in range(2):
        ps, free = pair()
        for n in range(2):
            s0 = 4 * half + 2 * n
            step = product(ps[:, n * 512:(n + 1) * 512], [(ones[:, :], sq[:, s0:s0 + 2, :].rearrange("p a t -> p (a t)"))])
        m = pe.raised(step)
        free.append(rsqrt(rs[:, 4 * half:4 * half + 4, :], ps.rearrange("p (a t) -> p a t", a=4), 1.0, after=[m]))
    m = act.mark()
    dve(V.scalar_tensor_tensor, qkvT[:, 0:4, :], qkvT[:, 0:4, :], 128.0 ** -0.5, rs[:, 0:4, :], ALU.mult, ALU.mult,
        after=[m])
    dve(V.tensor_tensor, qkvT[:, 4:8, :], qkvT[:, 4:8, :], rs[:, 4:8, :], ALU.mult)
    beta = sb("beta", [P, NT, 4], where=gd)
    g = sb("g", [P, NT, 4], where=gd)
    t3 = sb("t3", [P, 3, NT, 4], where=gd)
    ea = sb("ea", [P, 4], where=gd)
    act(S.activation, beta[:, :, :], thin[:, :, 24:28], ACT.Sigmoid)
    act(S.activation, gates[:, :, :], thin[:, :, 0:24], ACT.Sigmoid)
    act(S.activation, ea[:, :], gdn_ab[:, 0:4], ACT.Exp)
    for t in range(NT):
        dve(V.tensor_tensor, g[:, t, :], thin[:, t, 28:32], gdn_ab[:, 4:8], ALU.add, after=[act.mark()])
    softplus(g[:, :, :], [t3[:, n, :, :] for n in range(3)], g[:, :, :])
    for t in range(NT):
        m = dve(V.scalar_tensor_tensor, g[:, t, :], g[:, t, :], -1.0, ea[:, :], ALU.mult, ALU.mult)
    gc = sb("gc", [P, 2, NT * 4], where=gd)
    g8 = g[:, :, :].rearrange("p t h -> p (t h)")
    pe.wait(m)
    ps, free = pair()
    product(ps[:, 0:8], [(upper[:, :], g8)])
    step = product(ps[:, 8:16], [(ones[:, :], g8)])
    m = pe.raised(step)
    m = dve(V.tensor_copy, gc[:, :, :], ps[:, 0:16].rearrange("p (a b) -> p a b", a=2), after=[m])
    free.append(m)
    ps, free = pair()
    for n in range(8):
        step = product(ps[:, n * P:(n + 1) * P], [(g8[:, n:n + 1].to_broadcast([P, P]), upper[:, :])])
    m = pe.raised(step)
    dec = sb("dec", [P, 8, P], where=gd)
    decT = sb("decT", [P, 8, P], where=gd)
    gcc = gc[:, 0, :].unsqueeze(2).to_broadcast([P, 8, P])
    psn = ps.rearrange("p (n c) -> p n c", n=8)
    dve(V.tensor_tensor, decT[:, :, :], psn, gcc, ALU.subtract, after=[m])
    free.append(dve.mark())
    dve(V.tensor_scalar, dec[:, :, :], decT[:, :, :], -1.0, 0.0, ALU.mult, ALU.min)
    m = dve(V.tensor_scalar, decT[:, :, :], decT[:, :, :], 0.0, None, ALU.min)
    act(S.activation, dec[:, :, :], dec[:, :, :], ACT.Exp, after=[m])
    act(S.activation, decT[:, :, :], decT[:, :, :], ACT.Exp)
    eg = sb("eg", [P, 2, 8], where=gd)
    m = dve(V.tensor_tensor, eg[:, 1, :], gc[:, 1, :], gc[:, 0, :], ALU.subtract)
    act(S.activation, eg[:, 1, :], eg[:, 1, :], ACT.Exp, after=[m])
    act(S.activation, eg[:, 0, :], gc[:, 0, :], ACT.Exp)
    slow = sb("slow", [P, P], where=gd)
    pool(G.memset, slow[:, :], 1.0)
    pool(G.affine_select, out=slow[:, :], in_=slow[:, :], compare_op=ALU.is_ge, fill=0.0, base=-1,
         pattern=[[-1, P]], channel_multiplier=1)
    levels = [1 << n for n in range(7)]
    lev = sb("lev", [P, 7, P], where=gd)
    for n, b in enumerate(levels):
        v = lev[:, n, :].rearrange("p (j h r) -> p j h r", h=2, r=b)
        pool(G.memset, v[:, :, 0, :], 0.0)
        pool(G.memset, v[:, :, 1, :], 1.0)
        nj = P // (2 * b)
        v1 = v[:, :, 1, :]
        pool(G.affine_select, out=v1, in_=v1, compare_op=ALU.is_ge, fill=0.0, base=0,
             pattern=[[-2 * b, nj], [0, b]], channel_multiplier=1)
        pool(G.affine_select, out=v1, in_=v1, compare_op=ALU.is_ge, fill=0.0, base=b - 1,
             pattern=[[2 * b, nj], [0, b]], channel_multiplier=-1)
    masks_ready = pool.mark()

    def over8(a):
        return a.unsqueeze(1).to_broadcast([P, 8, P])

    dve(V.tensor_tensor, dec[:, :, :], dec[:, :, :], over8(slow[:, :]), ALU.mult, after=[act.mark(), masks_ready])
    m = dve(V.tensor_tensor, decT[:, :, :], decT[:, :, :], over8(upper[:, :]), ALU.mult)

    def qT(h, t):
        return qkvT[:, h, t * P:(t + 1) * P]

    def kT(h, t):
        return qkvT[:, 4 + h, t * P:(t + 1) * P]

    L, LT, X, XT = (shared[:, n, :, :] for n in range(4))
    atT = sb("atT", [P, 8, P], where=gd)
    pe.wait(m)
    ps, free = pair()
    for n in range(8):
        step = product(ps[:, n * P:(n + 1) * P], [(kT(n % 4, n // 4), kT(n % 4, n // 4))])
    m = pe.raised(step)
    dve(V.tensor_tensor, L[:, :, :], dec[:, :, :], ps.rearrange("p (n c) -> p n c", n=8), ALU.mult, after=[m])
    free.append(dve.mark())
    b8 = beta[:, :, :].rearrange("p t h -> p (t h)")
    m_L = dve(V.tensor_tensor, L[:, :, :], L[:, :, :], b8.unsqueeze(2).to_broadcast([P, 8, P]), ALU.mult)
    ps, free = pair()
    for n in range(8):
        step = product(ps[:, n * P:(n + 1) * P], [(kT(n % 4, n // 4), qT(n % 4, n // 4))])
    m = pe.raised(step)
    dve(V.tensor_tensor, atT[:, :, :], decT[:, :, :], ps.rearrange("p (n c) -> p n c", n=8), ALU.mult, after=[m])
    free.append(dve.mark())
    pe.wait(m_L)
    transposed([L[:, n, :] for n in range(8)],
               lambda n0, k, ps, m: act(S.copy, LT[:, :, :], ps.rearrange("p (n c) -> p n c", n=8), after=[m]))
    kb = sb("kb", [P, 8, P], where=gd)
    kd = sb("kd", [P, 8, P], where=gd)
    vb = sb("vb", [P, 8, P], where=gd)
    m = dve(V.tensor_tensor, gc[:, 0, :], b8, eg[:, 0, :], ALU.mult, after=[act.mark()])

    def k_out(n0, k, ps, m):
        src = ps.rearrange("p (n c) -> p n c", n=8)
        dve(V.tensor_tensor, kb[:, :, :], src, gc[:, 0, :].unsqueeze(2).to_broadcast([P, 8, P]), ALU.mult, after=[m])
        return dve(V.tensor_tensor, kd[:, :, :], src, eg[:, 1, :].unsqueeze(2).to_broadcast([P, 8, P]), ALU.mult)

    def v_out(n0, k, ps, m):
        src = ps.rearrange("p (n c) -> p n c", n=8)
        return dve(V.tensor_tensor, vb[:, :, :], src, b8.unsqueeze(2).to_broadcast([P, 8, P]), ALU.mult, after=[m])

    transposed([kT(n % 4, n // 4) for n in range(8)], k_out)
    transposed([qkvT[:, 8 + n % 4, (n // 4) * P:(n // 4 + 1) * P] for n in range(8)], v_out)

    Z = sb("Z", [P, 8, P], where=gd)
    LbT = dec
    dve(V.tensor_tensor, XT[:, :, :], LT[:, :, :], over8(lev[:, 0, :]), ALU.mult, after=[act.mark()])
    m = dve(V.tensor_tensor, XT[:, :, :], over8(ident[:, :]), XT[:, :, :], ALU.subtract)
    pe.wait(m)
    transposed([XT[:, n, :] for n in range(8)],
               lambda n0, k, ps, m: act(S.copy, X[:, :, :], ps.rearrange("p (n c) -> p n c", n=8), after=[m]))
    m_x = act.mark()
    for lv in range(1, 7):
        m = dve(V.tensor_tensor, LbT[:, :, :], LT[:, :, :], over8(lev[:, lv, :]), ALU.mult, after=[pe.mark()])
        pe.wait(m, m_x)
        ps, free = pair()
        for n in range(8):
            step = product(ps[:, n * P:(n + 1) * P], [(LbT[:, n, :], X[:, n, :])])
        m = pe.raised(step)
        m = act(S.copy, Z[:, :, :], ps.rearrange("p (n c) -> p n c", n=8), after=[m])
        free.append(m)
        pe.wait(m)
        last = lv == 6
        if not last:
            ps, free = pair()
            for n in range(8):
                step = product(ps[:, n * P:(n + 1) * P], [(XT[:, n, :], Z[:, n, :])])
            m = pe.raised(step)
            free_x, ps_x = free, ps
        ps, free = pair()
        for n in range(8):
            step = product(ps[:, n * P:(n + 1) * P], [(Z[:, n, :], XT[:, n, :])])
        m = pe.raised(step)
        if not last:
            m_x = dve(V.tensor_tensor, X[:, :, :], X[:, :, :], ps_x.rearrange("p (n c) -> p n c", n=8), ALU.subtract,
                      after=[m])
            free_x.append(m_x)
        m_x = dve(V.tensor_tensor, XT[:, :, :], XT[:, :, :], ps.rearrange("p (n c) -> p n c", n=8), ALU.subtract,
                  after=[m])
        free.append(m_x)
    U, WT, ST = L, LT, Z
    pe.wait(m_x)
    ps, free = pair()
    for n in range(8):
        step = product(ps[:, n * P:(n + 1) * P], [(XT[:, n, :], vb[:, n, :])])
    m = pe.raised(step)
    m_u = act(S.copy, U[:, :, :], ps.rearrange("p (n c) -> p n c", n=8), after=[m])
    free.append(m_u)
    ps, free = pair()
    for h in range(4):
        step = product(ps[:, h * P:(h + 1) * P], [(kb[:, 4 + h, :], XT[:, 4 + h, :])])
    m = pe.raised(step)
    free.append(act(S.copy, WT[:, 0:4, :], ps[:, 0:512].rearrange("p (n c) -> p n c", n=4), after=[m]))
    pe.wait(act.mark())
    ps, free = pair()
    for h in range(4):
        step = product(ps[:, h * P:(h + 1) * P], [(kd[:, h, :], U[:, h, :])])
    m = pe.raised(step)
    m = act(S.copy, ST[:, 0:4, :], ps[:, 0:512].rearrange("p (n c) -> p n c", n=4), after=[m])
    free.append(m)
    pe.wait(m)
    ps, free = pair()
    for h in range(4):
        product(ps[:, h * P:(h + 1) * P], [(WT[:, h, :], ST[:, h, :])])
    for h in range(4):
        step = product(ps[:, 512 + h * P:512 + (h + 1) * P], [(qT(h, 1), ST[:, h, :])])
    m = pe.raised(step)
    ps4 = ps.rearrange("p (a n c) -> p a n c", a=2, n=4)
    m = dve(V.tensor_tensor, U[:, 4:8, :], U[:, 4:8, :], ps4[:, 0, :, :], ALU.subtract, after=[m])
    o = X
    m2 = dve(V.tensor_tensor, o[:, 4:8, :], ps4[:, 1, :, :], eg[:, 0, 4:8].unsqueeze(2).to_broadcast([P, 4, P]), ALU.mult)
    free.append(m2)
    pe.wait(m)
    ps, free = pair()
    for n in range(8):
        step = product(ps[:, n * P:(n + 1) * P], [(atT[:, n, :], U[:, n, :])])
    m = pe.raised(step)
    ps8 = ps.rearrange("p (n c) -> p n c", n=8)
    dve(V.tensor_copy, o[:, 0:4, :], ps8[:, 0:4, :], after=[m])
    m = dve(V.tensor_tensor, o[:, 4:8, :], o[:, 4:8, :], ps8[:, 4:8, :], ALU.add)
    free.append(m)
    os_ = sb("os", [P, 8], where=gd)
    dve(V.tensor_tensor, XT[:, :, :], o[:, :, :], o[:, :, :], ALU.mult)
    m = dve(V.tensor_reduce, os_[:, :], XT[:, :, :], AX.X, ALU.add)
    m = rsqrt(os_[:, :], os_[:, :], 1.0 / 128, after=[m])
    m = dve(V.tensor_tensor, o[:, :, :], o[:, :, :], os_[:, :].unsqueeze(2).to_broadcast([P, 8, P]), ALU.mult,
            after=[m])
    pe.wait(m)

    def o_out(n0, k, ps, m):
        for t in range(NT):
            last = dve(V.scalar_tensor_tensor, yT[:, 2, :, t * P:(t + 1) * P],
                       ps.rearrange("p (t h c) -> p t h c", t=NT, h=4)[:, t, :, :], col("gdn_out_gain"),
                       zT[:, :, t * P:(t + 1) * P], ALU.mult, ALU.mult, after=[m])
        return last

    transposed([o[:, n, :] for n in range(8)], o_out)
    phase()
    gd.close()

    ns = ExitStack()
    q = sb("q", [P, NT, 512], where=ns)
    kv = sb("kv", [P, NT, 768], where=ns)
    unit_by_token(512, by_token_rows(q, 0, 512))
    unit_by_token(512, by_token_rows(kv, 0, 512))
    unit_by_token(256, by_token_rows(kv, 512, 256))
    dist = sb("dist", [P, NT, T], where=ns)
    distc = sb("distc", [P, NT, 15], where=ns)
    seen = sb("seen", [P, NT], where=ns)
    pool(G.iota, dist[:, :, :], pattern=[[P, NT], [-1, T]], base=0, channel_multiplier=1,
         allow_small_or_imprecise_dtypes=True)
    pool(G.affine_select, out=dist[:, :, :], in_=dist[:, :, :], compare_op=ALU.is_ge, fill=BIG, base=0,
         pattern=[[P, NT], [-1, T]], channel_multiplier=1)
    pool(G.iota, distc[:, :, :], pattern=[[P, NT], [-16, 15]], base=-31, channel_multiplier=1,
         allow_small_or_imprecise_dtypes=True)
    pool(G.affine_select, out=distc[:, :, :], in_=distc[:, :, :], compare_op=ALU.is_ge, fill=BIG, base=-31,
         pattern=[[P, NT], [-16, 15]], channel_multiplier=1)
    pool(G.memset, seen[:, :], 1.0)
    dist_ready = pool(G.affine_select, out=seen[:, :], in_=seen[:, :], compare_op=ALU.is_ge, fill=0.0, base=-31,
                      pattern=[[P, NT]], channel_multiplier=1)
    sq = sb("nsq", [P, NT, 1024], where=ns)
    rn = sb("nrn", [P, NT, 16], where=ns)

    def head_norm(buf, c0, n, gain, scale, k0):
        v = buf[:, :, c0:c0 + 64 * n]
        w = sq[:, :, 0:64 * n]
        dve(V.tensor_tensor, w, v, v, ALU.mult, after=[act.mark()])
        for t in range(NT):
            m = dve(V.tensor_reduce, rn[:, t, k0:k0 + n], w[:, t, :].rearrange("p (n d) -> p n d", d=64), AX.X, ALU.add)
        m = rsqrt(rn[:, :, k0:k0 + n], rn[:, :, k0:k0 + n], 1.0 / 64, after=[m])
        for t in range(NT):
            vt = v[:, t, :].rearrange("p (n d) -> p n d", d=64)
            dve(V.tensor_tensor, vt, vt, rn[:, t, k0:k0 + n].unsqueeze(2).to_broadcast([P, n, 64]), ALU.mult, after=[m])
            if scale != 1.0:
                dve(V.tensor_scalar, vt, vt, scale, None, ALU.mult)
            last = dve(V.tensor_tensor, vt, vt, gain.unsqueeze(1).to_broadcast([P, n, 64]), ALU.mult)
        return last

    head_norm(q, 0, 8, gains[:, 0, :], 64.0 ** -0.5, 0)
    head_norm(kv, 256, 2, gains[:, 2, :], 1.0, 8)
    m = head_norm(kv, 512, 2, gains[:, 3, :], 1.0, 10)
    nqT = sb("nqT", [64, 8, T], where=ns)
    nkT = sb("nkT", [64, 4, T], where=ns)
    pe.wait(m)
    for h0 in range(0, 8, 4):
        transposed([q[:, t, 64 * h:64 * h + 64] for h in range(h0, h0 + 4) for t in range(NT)],
                   lambda n0, k, ps, m, h0=h0: act(S.copy, nqT[:, h0:h0 + 4, :].rearrange("p h t -> p (h t)"),
                                                   ps[0:64, :], after=[m]))
    transposed([kv[:, t, 256 + 256 * b + 64 * gr_:256 + 256 * b + 64 * gr_ + 64]
                for b in range(2) for gr_ in range(2) for t in range(NT)],
               lambda n0, k, ps, m: act(S.copy, nkT[:, :, :].rearrange("p h t -> p (h t)"), ps[0:64, :], after=[m]))
    dup = sb("dup", [P, 4, NT, P], where=ns)
    for jg in range(4):
        for c in range(2):
            dve(V.tensor_copy, dup[:, jg, :, 64 * c:64 * c + 64], kv[:, :, 64 * jg:64 * jg + 64])
    kcT = sb("kcT", [P, 4, T], where=ns)
    pe.wait(dve.mark())
    transposed([dup[:, jg, t, :] for jg in range(4) for t in range(NT)],
               lambda n0, k, ps, m: act(S.copy, kcT[:, :, :].rearrange("p h t -> p (h t)"), ps, after=[m]))
    fl = sb("fl", [P, 2, 16, 2, 15], where=ns)
    for j in range(2):
        for g_ in range(2):
            toks = kcT[:, 2 * j + g_, :].rearrange("p (c s) -> p s c", s=16)
            for odd in range(2):
                r = slice(64 * odd, 64 * odd + 64)
                for half in range(2):
                    pe_cols = colrange("cmp_pe", 16 * j + 8 * half, 16 * j + 8 * half + 8)[r, :]
                    dve(V.tensor_tensor, fl[r, j, 8 * half:8 * half + 8, g_, :],
                        toks[r, odd:16:2, half:half + 15], pe_cols.unsqueeze(2).to_broadcast([64, 8, 15]), ALU.add,
                        after=[act.mark()])
    pe.wait(dve.mark())
    h1 = sb("h1", [30, 2, 256], where=ns)
    h2 = sb("h2", [30, 2, 256], where=ns)
    for j in range(2):
        w = take().rearrange("p (k n) -> p k n", k=16)
        ps, free = pair()
        step = product(ps[0:30, 0:256], [(fl[:, j, k, :, :].rearrange("p g c -> p (g c)"), w[:, k, :]) for k in range(16)])
        give()
        m = pe.raised(step)
        free.append(act(S.copy, h1[:, j, :], ps[0:30, 0:256], after=[m]))
    dve(V.tensor_tensor, h2[:, :, :], h1[:, :, :], h1[:, :, :], ALU.mult, after=[act.mark()])
    dve(V.tensor_scalar, h2[:, :, :], h2[:, :, :], 0.044715, 1.0, ALU.mult, ALU.add)
    m = dve(V.tensor_tensor, h2[:, :, :], h2[:, :, :], h1[:, :, :], ALU.mult)
    m = act(S.activation, h2[:, :, :], h2[:, :, :], ACT.Sigmoid, scale=2.0 * math.sqrt(2.0 / math.pi), after=[m])
    m = dve(V.tensor_tensor, h1[:, :, :], h1[:, :, :], h2[:, :, :], ALU.mult, after=[m])
    pe.wait(m)
    h1T = sb("h1T", [P, 4, 30], where=ns)
    transposed([h1[:, j, P * c:P * c + P] for j in range(2) for c in range(2)],
               lambda n0, k, ps, m: act(S.copy, h1T[:, :, :], ps[:, 0:512].rearrange("p (n c) -> p n c", n=4)[:, :, 0:30],
                                        after=[m]))
    pe.wait(act.mark())
    kc = sb("kc", [30, 4, 64], where=ns)
    vcT = sb("vcT", [64, 30], where=ns)
    rc = sb("rc", [30, 1], where=ns)
    ps, free = pair()
    product(ps[0:30, 0:64], [(h1T[:, c, :], cmp_w2[:, 0, c, :]) for c in range(2)])
    step = product(ps[0:64, 512:542], [(cmp_w2[:, 1, c, :], h1T[:, 2 + c, :]) for c in range(2)])
    m = pe.raised(step)
    act(S.copy, vcT[:, :], ps[0:64, 512:542], after=[m])
    act(S.copy, kc[:, 0, :], ps[0:30, 0:64])
    m = act(S.activation, kc[:, 1, :], kc[:, 0, :], ACT.Square, accum_out=rc[:, :])
    free.append(m)
    m = rsqrt(rc[:, :], rc[:, :], 1.0 / 64)
    dve(V.tensor_scalar, kc[:, 0, :], kc[:, 0, :], rc[:, :], None, ALU.mult, after=[m])
    m = dve(V.tensor_tensor, kc[:, 0, :], kc[:, 0, :], gains[0:30, 1, :], ALU.mult)
    pe.wait(m)
    kcT2 = sb("kcT2", [64, 30], where=ns)
    vc = sb("vc", [15, 2, 64], where=ns)
    ps, free = pair()
    pe.put(PE_.transpose, ps[0:64, 0:30], kc[:, 0, :], ident[0:30, 0:30])
    pe.put(PE_.transpose, ps[0:15, 128:192], vcT[:, 0:15], ident[0:64, 0:64])
    step = pe.put(PE_.transpose, ps[0:15, 256:320], vcT[:, 15:30], ident[0:64, 0:64])
    m = pe.raised(step)
    act(S.copy, kcT2[:, :], ps[0:64, 0:30], after=[m])
    act(S.copy, vc[:, 0, :], ps[0:15, 128:192])
    free.append(act(S.copy, vc[:, 1, :], ps[0:15, 256:320]))
    pe.wait(act.mark())

    yn = sb("yn", [P, NT, 512], where=ns)
    wgt = sb("wgt", [P, 4], where=ns)
    slopes = [2.0 ** (-8.0 * (h + 1) / 8) for h in range(8)]

    def branch_jobs(br, d, keys_of, k_of, v_of):
        def job(t, h0):
            def score(ps_, s_, marks):
                for j in range(4):
                    last = dve(V.scalar_tensor_tensor, s_[:, j, :], d[:, t, 0:s_.shape[2]], -slopes[h0 + j], ps_[:, j, :],
                               ALU.mult, ALU.add, after=marks + [dist_ready], chain=False)
                return last

            def finish(ps_, den, m):
                dve(V.reciprocal, wgt[:, :], den, after=[m])
                dve(V.tensor_tensor, wgt[:, :], wgt[:, :], gates[:, t, 8 * br + h0:8 * br + h0 + 4], ALU.mult)
                if br == 0:
                    dve(V.tensor_scalar, wgt[:, :], wgt[:, :], seen[:, t:t + 1], None, ALU.mult)
                for j in range(4):
                    y = yn[:, t, 64 * (h0 + j):64 * (h0 + j) + 64]
                    if br == 0:
                        last = dve(V.tensor_scalar, y, ps_[:, j, :], wgt[:, j:j + 1], None, ALU.mult, chain=j == 0)
                    else:
                        last = dve(V.scalar_tensor_tensor, y, ps_[:, j, :], wgt[:, j:j + 1], y, ALU.mult, ALU.add,
                                   chain=j == 0)
                return last

            return dict(n_keys=keys_of(t), queries=lambda j: nqT[:, h0 + j, t * P:(t + 1) * P],
                        keys=lambda j: k_of(h0 + j), values=lambda j, c: v_of(h0 + j, c), score=score, finish=finish)
        return [job(t, h0) for t in range(NT) for h0 in (0, 4)]

    jobs = branch_jobs(0, distc, lambda t: 15, lambda h: kcT2[:, 15 * (h // 4):15 * (h // 4) + 15],
                       lambda h, c: vc[:, h // 4, :])
    for b in range(2):
        jobs += branch_jobs(1 + b, dist, lambda t: (t + 1) * P, lambda h, b=b: nkT[:, 2 * b + h // 4, :],
                            lambda h, c, b=b: kv[:, c, 384 + 256 * b + 64 * (h // 4):384 + 256 * b + 64 * (h // 4) + 64])
    at_ctx = ExitStack()
    attention("nsa", jobs, T, 1.0, at_ctx)
    phase()
    at_ctx.close()
    def yn_out(n0, k, ps, m):
        return act(S.copy, yT[:, 1, :, :].rearrange("p f t -> p (f t)"), ps, after=[m])
    transposed([yn[:, t, f * P:(f + 1) * P] for f in range(4) for t in range(NT)], yn_out)
    phase()
    ns.close()

    mg = ExitStack()
    merged = sb("merged", [P, NT, D], where=mg)
    sg = [sb(f"sg{b}", [P, NT, 512], where=mg) for b in range(2)]
    sg_free = [None, None]
    for r in range(3):
        w = take().rearrange("p (k n) -> p k n", k=4)
        halves = []
        for half in range(2):
            ps, free = pair()
            for t in range(NT):
                step = product(ps[:, t * 512:(t + 1) * 512],
                               [(yT[:, r, k, t * P:(t + 1) * P], w[:, k, 512 * half:512 * half + 512]) for k in range(4)])
            halves.append((ps, free, pe.raised(step)))
        give()
        for half in range(2):
            wg = take().rearrange("p (k n) -> p k n", k=KD)
            ps, free = pair()
            n = 2 * r + half
            for t in range(NT):
                step = product(ps[:, t * 512:(t + 1) * 512],
                               [(hT[:, k, t * P:(t + 1) * P], wg[:, k, :]) for k in range(KD)]
                               + [(ident[0:6, n:n + 1].to_broadcast([6, P]), rows512[:, :])])
            give()
            m = pe.raised(step)
            b = half
            s3 = sg[b][:, :, :]
            m = act(S.activation, s3, ps.rearrange("p (t n) -> p t n", t=NT), ACT.Sigmoid, after=[m, sg_free[b]])
            free.append(m)
            br_ps, br_free, br_m = halves[half]
            dst = merged[:, :, 512 * half:512 * half + 512]
            brv = br_ps.rearrange("p (t n) -> p t n", t=NT)
            if r == 0:
                m = dve(V.tensor_tensor, dst, s3, brv, ALU.mult, after=[m, br_m])
                br_free.append(m)
            else:
                m = dve(V.tensor_tensor, s3, s3, brv, ALU.mult, after=[m, br_m])
                br_free.append(m)
                m = dve(V.tensor_tensor, dst, dst, s3, ALU.add)
            sg_free[b] = m
    mT = sb("mT", [P, KD, T], where=mg)

    def token_tiles_transposed(src, dstT, n_f, after):
        pe.wait(*after)
        for f0 in range(0, n_f, 4):
            transposed([src[:, t, f * P:(f + 1) * P] for f in range(f0, f0 + 4) for t in range(NT)],
                       lambda n0, k, ps, m, f0=f0: act(S.copy, dstT[:, f0:f0 + 4, :].rearrange("p f t -> p (f t)"), ps,
                                                       after=[m]))
        pe.wait(act.mark())

    token_tiles_transposed(merged, mT, KD, [dve.mark()])
    for half in range(2):
        dst = x[:, :, 512 * half:512 * half + 512]
        unit_by_token(512, lambda ps, m, dst=dst: dve(V.tensor_tensor, dst, dst, ps, ALU.add, after=[m]), src=mT)
    phase()
    mg.close()
    mix.close()

    def mlp(F, down_out, where, tag, loop_marks=()):
        mid = mids[tag]
        sil = silus[tag]
        mark = list(loop_marks)
        for c, c0 in enumerate(range(0, F, 512)):
            nf = min(512, F - c0) // P
            wg = take()[:, 0:KD * nf * P].rearrange("p (k n) -> p k n", k=KD)
            psg, free_g = pair()
            for f in range(nf):
                step = by_feature(wg, f, psg[:, f * T:(f + 1) * T])
            give()
            m_g = pe.raised(step)
            wu = take()[:, 0:KD * nf * P].rearrange("p (k n) -> p k n", k=KD)
            psu, free_u = pair()
            for f in range(nf):
                step = by_feature(wu, f, psu[:, f * T:(f + 1) * T])
            give()
            m_u = pe.raised(step)
            s3 = sil[:, c % 2, 0:nf * T]
            m = act(S.activation, s3, psg[:, 0:nf * T], ACT.Silu, after=[m_g] + mark, chain=False)
            free_g.append(m)
            m = dve(V.tensor_tensor, mid[:, 4 * c:4 * c + nf, :].rearrange("p f t -> p (f t)"), s3, psu[:, 0:nf * T],
                    ALU.mult, after=[m, m_u] + mark, chain=False)
            free_u.append(m)
            mark = [m]
        n_k = F // P
        pe.wait(m)
        (ps0, free0), (ps1, free1) = pair(), pair()
        halves = [(ps0, free0), (ps1, free1)]
        last = []
        for k0 in range(0, n_k, 4):
            wd = take().rearrange("p (k n) -> p k n", k=4)
            kn = min(4, n_k - k0)
            for half in range(2):
                for t in range(NT):
                    for k in range(kn):
                        step = pe.put(PE_.matmul, halves[half][0][:, t * 512:(t + 1) * 512],
                                      mid[:, k0 + k, t * P:(t + 1) * P], wd[:, k, 512 * half:512 * half + 512],
                                      start=k0 + k == 0, stop=k0 + k == n_k - 1)
                if k0 + kn == n_k and half == 0:
                    last.append(pe.raised(step))
            give()
        last.append(pe.raised(step))
        for half in range(2):
            free = halves[half][1]
            free.append(down_out(half, halves[half][0].rearrange("p (t n) -> p t n", t=NT), last[half]))

    mids, silus = {}, {}

    def mlp_buffers(F, where, tag):
        mids[tag] = sb("mid" + tag, [P, F // P, T], where=where)
        silus[tag] = sb("sil" + tag, [P, 2, 1024], where=where)

    def expert_gates(logits, n, where, tag, after):
        best = sb("best" + tag, [P, NT, 8], where=where)
        index = sb("index" + tag, [P, NT, 8], U32, where=where)
        idx = sb("idx" + tag, [P, NT, 8], where=where)
        gate = sb("gate" + tag, [P, NT, n], where=where)
        one = sb("one" + tag, [P, NT, n], where=where)
        iota = sb("iota" + tag, [P, n], where=where)
        wts = sb("wts" + tag, [P, NT, 4], where=where)
        m_i = pool(G.iota, iota[:, :], pattern=[[1, n]], base=0, channel_multiplier=0,
                   allow_small_or_imprecise_dtypes=True)
        for t in range(NT):
            dve(V.max, best[:, t, :], logits[:, t, :], after=after)
            dve(V.max_index, index[:, t, :], best[:, t, :], logits[:, t, :])
        dve(V.tensor_copy, idx[:, :, :], index[:, :, :])
        m = dve(V.tensor_tensor, wts[:, :, 0:1], best[:, :, 1:2], best[:, :, 0:1], ALU.subtract)
        m = act(S.activation, wts[:, :, 0:1], wts[:, :, 0:1], ACT.Exp, after=[m])
        dve(V.tensor_scalar, wts[:, :, 1:2], wts[:, :, 0:1], 1.0, None, ALU.add, after=[m])
        dve(V.reciprocal, wts[:, :, 1:2], wts[:, :, 1:2])
        dve(V.tensor_tensor, wts[:, :, 2:3], wts[:, :, 0:1], wts[:, :, 1:2], ALU.mult)
        for t in range(NT):
            dve(V.tensor_scalar, gate[:, t, :], iota[:, :], idx[:, t, 0:1], wts[:, t, 1:2], ALU.is_equal, ALU.mult,
                after=[m_i])
            dve(V.tensor_scalar, one[:, t, :], iota[:, :], idx[:, t, 1:2], wts[:, t, 2:3], ALU.is_equal, ALU.mult)
        return gate, dve(V.tensor_tensor, gate[:, :, :], gate[:, :, :], one[:, :, :], ALU.add)

    class Carry(dict):

        def __missing__(self, name):
            self[name] = self.open[name] = Later(back=1)
            return self[name]

    def expert_tools(n_exp, F, gate, xn, gain8, shift8, acc, where, tag, after):
        pos = sb("pos" + tag, [P, NT, n_exp + 1], where=where)
        some = sb("some" + tag, [P, NT, n_exp], where=where)
        iota = sb("slots" + tag, [P, 2, P], where=where)
        sel = sb("sel" + tag, [P, NT, P], where=where)
        selg = sb("selg" + tag, [P, NT, P], where=where)
        selgT = sb("selgT" + tag, [P, NT * P], where=where)
        xg = sb("xg" + tag, [P, KD, P], where=where)
        sil = sb("sil" + tag, [P, 2, 512], where=where)
        mid = sb("mid" + tag, [P, 2, 512], where=where)
        midT = sb("midT" + tag, [P, F // P, P], where=where)
        ysb = sb("ysb" + tag, [P, D], where=where)
        m_i = pool(G.iota, iota[:, :, :], pattern=[[P, 2], [1, P]], base=0, channel_multiplier=0,
                   allow_small_or_imprecise_dtypes=True)
        m = dve(V.tensor_scalar, some[:, :, :], gate[:, :, 0:n_exp], 0.0, None, ALU.is_gt, after=[after])
        pe.wait(m)
        ps, free = pair()
        product(ps[:, 0:n_exp], [(upper[:, :], some[:, 0, :])])
        product(ps[:, n_exp:2 * n_exp], [(ones[:, :], some[:, 0, :]), (upper[:, :], some[:, 1, :])])
        step = product(ps[:, 512:512 + n_exp], [(ones[:, :], some[:, 0, :]), (ones[:, :], some[:, 1, :])])
        m = pe.raised(step)
        dve(V.memset, pos[:, :, n_exp:n_exp + 1], -1.0)
        dve(V.tensor_tensor, pos[:, :, 0:n_exp], ps[:, 0:2 * n_exp].rearrange("p (t n) -> p t n", t=NT),
            some[:, :, :], ALU.mult, after=[m])
        dve(V.tensor_scalar, pos[:, :, 0:n_exp], pos[:, :, 0:n_exp], -1.0, None, ALU.add)
        over = sb("over" + tag, [1, n_exp], where=where)
        rank = sb("rank" + tag, [1, n_exp], where=where)
        num = sb("num" + tag, [1, n_exp], where=where)
        tf = sb("tf" + tag, [1, 4], where=where)
        m = dve(V.tensor_scalar, over[:, :], ps[0:1, 512:512 + n_exp], float(P), None, ALU.is_gt)
        free.append(m)
        dve(V.tensor_tensor_scan, rank[:, :], ones[0:1, 0:n_exp], over[:, :], 0.0, ALU.mult, ALU.add)
        dve(V.tensor_copy, tf[:, 0:1], rank[:, n_exp - 1:n_exp])
        dve(V.tensor_tensor, over[:, :], over[:, :], iota[0:1, 0, 0:n_exp], ALU.mult, after=[m_i])
        for k in range(MOST_OVER):
            dve(V.tensor_scalar, num[:, :], rank[:, :], float(k + 1), None, ALU.is_equal)
            dve(V.tensor_tensor, num[:, :], num[:, :], over[:, :], ALU.mult)
            dve(V.tensor_reduce, tf[:, k + 1:k + 2], num[:, :], AX.X, ALU.max)
        table_ready[tag].marks.append(dve(V.tensor_copy, tables[tag][:, :], tf[:, :]))
        dve(V.memset, ysb[:, :], 0.0)
        m = dve(V.memset, selgT[:, :], 0.0)

        def column(table, t, e):
            return At(lambda i: table[:, t, bass.ds(e(i), 1)])

        def gather(c, e, b):
            for t in range(NT):
                m = dve(V.tensor_scalar, sel[:, t, :], iota[:, b, :], column(pos, t, e), None, ALU.is_equal,
                        after=[c["gathered"]], chain=False)
            pe.wait(m)
            ps, free = pair()
            for k in range(KD):
                step = product(ps[:, k * P:(k + 1) * P], [(xn[:, t, k * P:(k + 1) * P], sel[:, t, :]) for t in range(NT)])
            c["gathered"] = m = pe.raised(step)
            m = dve(V.tensor_tensor, xg[:, :, :], ps.rearrange("p (k c) -> p k c", k=KD),
                    gain8.unsqueeze(2).to_broadcast([P, KD, P]), ALU.mult, after=[m, c["up"]], chain=False)
            free.append(m)
            if shift8 is not None:
                m = dve(V.tensor_tensor, xg[:, :, :], xg[:, :, :], shift8.unsqueeze(2).to_broadcast([P, KD, P]),
                        ALU.add)
            c["xg"] = m

        def scatter(c):
            pe.wait(c["y"], c["selgT"])
            for t in range(NT):
                ps, free = pair()
                for half in range(2):
                    step = product(ps[:, half * 512:(half + 1) * 512],
                                   [(selgT[:, t * P:(t + 1) * P], ysb[:, half * 512:(half + 1) * 512])])
                c["scattered"] = m = pe.raised(step)
                free.append(dve(V.tensor_tensor, acc[:, t, :], acc[:, t, :], ps, ALU.add, after=[m]))

        def turn_mid(c, ch, nf):
            pe.wait(c["mid", ch % 2])
            ps, free = pair()
            for f in range(nf):
                step = pe.put(PE_.transpose, ps[:, f * P:(f + 1) * P], mid[:, ch % 2, f * P:(f + 1) * P], ident[:, :])
            c["turned", ch % 2] = m = pe.raised(step)
            m = act(S.copy, midT[:, 4 * ch:4 * ch + nf, :].rearrange("p f c -> p (f c)"), ps[:, 0:nf * P],
                    after=[m, c["down"]], chain=False)
            free.append(m)
            c["midT"] = m

        def layers(c, e, b, after_gate, after_up):
            for t in range(NT):
                m_selg = dve(V.tensor_scalar, selg[:, t, :], iota[:, b, :], column(pos, t, e), column(gate, t, e),
                             ALU.is_equal, ALU.mult, after=[c["selg_read"]], chain=False)
            chunks = [min(512, F - c0) for c0 in range(0, F, 512)]
            for ch, n in enumerate(chunks):
                pe.wait(c["xg"])
                ps, free = pair()
                marks = []
                for g_ in range(2):
                    w = take()[:, 0:KD * n].rearrange("p (k n) -> p k n", k=KD)
                    step = product(ps[:, g_ * 512:g_ * 512 + n], [(xg[:, k, :], w[:, k, :]) for k in range(KD)])
                    marks.append(pe.raised(step))
                    give()
                    if g_ == 0:
                        m = act(S.activation, sil[:, ch % 2, 0:n], ps[:, 0:n], ACT.Silu,
                                after=[marks[0], c["mid", ch % 2]], chain=False)
                        if ch == 0:
                            after_gate()
                        else:
                            turn_mid(c, ch - 1, chunks[ch - 1] // P)
                c["mid", ch % 2] = m = dve(V.tensor_tensor, mid[:, ch % 2, 0:n], sil[:, ch % 2, 0:n],
                                           ps[:, 512:512 + n], ALU.mult,
                                           after=[m, marks[1], c["turned", ch % 2]], chain=False)
                free.append(m)
            c["up"] = marks[1]
            after_up()
            turn_mid(c, len(chunks) - 1, chunks[-1] // P)
            pe.wait(m_selg)
            ps, free = pair()
            for t in range(NT):
                step = pe.put(PE_.transpose, ps[:, t * P:(t + 1) * P], selg[:, t, :], ident[:, :])
            c["selg_read"] = m = pe.raised(step)
            c["selgT"] = m = act(S.copy, selgT[:, :], ps[:, 0:NT * P], after=[m, c["scattered"]], chain=False)
            free.append(m)
            pe.wait(c["midT"])
            ps, free = pair()
            n_k = F // P
            for k0 in range(0, n_k, 4):
                wd = take().rearrange("p (k n) -> p k n", k=4)
                for k in range(min(4, n_k - k0)):
                    for half in range(2):
                        step = pe.put(PE_.matmul, ps[:, half * 512:(half + 1) * 512], midT[:, k0 + k, :],
                                      wd[:, k, 512 * half:512 * half + 512], start=k0 + k == 0, stop=k0 + k == n_k - 1)
                if k0 + 4 >= n_k:
                    c["down"] = m = pe.raised(step)
                give()
            c["y"] = m = act(S.copy, ysb[:, :], ps, after=[m, c["scattered"]], chain=False)
            free.append(m)

        return gather, scatter, layers

    def run_experts(turns, per_turn, units, gather, scatter, layers, tag, beside=None):
        engines = [pe, act, dve]
        flat = Carry()
        flat.open = {}
        for name in ("gathered", "up"):
            flat[name] = None
        gather(flat, lambda i: 0, 0)
        marks = [e.mark() for e in everyone]
        for e in everyone:
            e.wait(*marks)
        with unit_loop(turns, units, [ada_used] if beside else []):
            turn_first = turn[0] % 4
            c = Carry()
            c.open = {}
            banks = [Later(back=1) for _ in range(4)]
            for n in range(4):
                pair_free[n] = [banks[n]]
            for j in range(per_turn):
                e = lambda i, j=j: per_turn * i + j
                def after_gate(j=j):
                    scatter(c)
                    if beside:
                        beside[0](c, j)

                def after_up(j=j):
                    gather(c, lambda i: per_turn * i + j + 1, 0)
                    if beside:
                        beside[1](c, j)

                layers(c, e, 0, after_gate, after_up)
            for name, later in c.open.items():
                later.marks.append(c[name])
            for n in range(4):
                banks[n].marks += [m for m in pair_free[n] if m is not banks[n]]
        marks = [e.mark() for e in everyone]
        for e in everyone:
            e.wait(*marks)
        for n in range(4):
            pair_free[n] = []
        flat = Carry()
        flat.open = {}
        for name in ("gathered", "up", "y", "selgT", "scattered", "selg_read", ("mid", 0), ("mid", 1), ("turned", 0),
                     ("turned", 1), "down", "xg", "midT"):
            flat[name] = None
        scatter(flat)
        signal_now()
        for e in engines:
            e.wait(table_ready[tag])
            load_table(e, tag)
        for k in range(MOST_OVER):
            phase()
            with case(tag, k, engines) as raises:
                first = unit_used.n
                own = Carry(flat)
                own.open = {}
                gather(own, lambda i: i, 1)
                layers(own, lambda i: i, 1, lambda: None, lambda: None)
                scatter(own)
                signal_now()
                raises[pe].append((unit_used.sem, first, unit_used.n - first))
            for n in range(4):
                pair_free[n] = [e.mark() for e in engines]
        phase()

    cond = sb("cond", [P, 8])
    cond_ready = act(S.activation, cond[:, :], colrange("c_2", 0, 8), ACT.Silu)
    mod_all = sb("mod_all", [P, 96])
    fe = ExitStack()
    ada_place.append(sb("ada_buf", [P, 2, KD, ADA], where=fe))
    ada_sum = sb("ada_sum", [P, 2, ADA], where=fe)
    dve.put(nc.vector.sem_inc, ada_used.sem, 2)
    ada_used.n += 2

    def ada_chunk(c, j):
        b = j % 2
        buf = ada_place[0]
        dve.put(nc.vector.wait_ge, ada_loaded[b], At(lambda i: i * 32 + 16 * (j // 2 + 1)))
        dve(V.tensor_scalar, ada_sum[:, b, :], buf[:, b, 0, :], cond[:, 0:1], None, ALU.mult,
            after=[cond_ready, c["ada_read", b]])
        for k in range(1, KD):
            dve.wait(dve.mark())
            step = dve.put(V.scalar_tensor_tensor, ada_sum[:, b, :], buf[:, b, k, :], cond[:, k:k + 1],
                           ada_sum[:, b, :], ALU.mult, ALU.add)
            m = dve.raised(step, ada_used) if k == KD - 1 else dve.raised(step)
        c["ada_sum", b] = m

    def ada_columns(c, j):
        b = j % 2
        pe.wait(c["ada_sum", b])
        ps, free = pair()
        for f in range(3):
            step = product(ps[:, f:f + 1], [(ada_sum[:, b, f * P:(f + 1) * P], ones[:, 0:1])])
        c["ada_read", b] = m = pe.raised(step)
        free.append(dve(V.tensor_copy, At(lambda i: mod_all[:, bass.ds(48 * (j // 2) + 3 * (j % 2) + 6 * i, 3)]),
                        ps[:, 0:3], after=[m], chain=False))

    tmp = ExitStack()
    m, xn = norm_transposed(lambda k: col("norm_ffn", k), None, fe, "b")
    logits = sb("logits", [P, NT, 36], where=fe)
    lg8 = sb("lg8", [P, NT, 8], where=fe)
    pe.wait(m)
    ps, free = pair()
    for t in range(NT):
        step = product(ps[:, t * 512:t * 512 + 36], [(hT[:, k, t * P:(t + 1) * P], w_rout[:, k, 0:36]) for k in range(KD)])
    m = pe.raised(step)
    m = dve(V.tensor_tensor, logits[:, :, :], ps.rearrange("p (t n) -> p t n", t=NT)[:, :, 0:36],
            b_rout[:, :].unsqueeze(1).to_broadcast([P, NT, 36]), ALU.add, after=[m])
    free.append(m)
    dve(V.memset, lg8[:, :, 4:8], -BIG)
    dve(V.tensor_copy, lg8[:, :, 0:4], logits[:, :, 0:4])
    gb = sb("gbest", [P, NT, 8], where=fe)
    gi = sb("gindex", [P, NT, 8], U32, where=fe)
    gf = sb("gf", [P, NT, 1], where=fe)
    pg = sb("pg", [P, NT, 8], where=fe)
    gs = sb("gs", [P, NT], where=fe)
    for t in range(NT):
        dve(V.max, gb[:, t, :], lg8[:, t, :])
        m = dve(V.max_index, gi[:, t, :], gb[:, t, :], lg8[:, t, :])
    m = dve(V.tensor_scalar, gb[:, :, 1:2], gb[:, :, 0:1], -1.0, None, ALU.mult)
    for t in range(NT):
        m = act(S.activation, pg[:, t, :], lg8[:, t, :], ACT.Exp, bias=gb[:, t, 1:2], accum_out=gs[:, t:t + 1], after=[m])
    dve(V.reciprocal, gs[:, :], gs[:, :], after=[m])
    dve(V.tensor_copy, gf[:, :, :], gi[:, :, 0:1])
    grp_of = sb("grp_of", [P, 32], where=fe)
    m = pool(G.iota, grp_of[:, :].rearrange("p (g e) -> p g e", g=4), pattern=[[1, 4], [0, 8]], base=0,
             channel_multiplier=0, allow_small_or_imprecise_dtypes=True)
    inside = sb("inside", [P, NT, 32], where=fe)
    le = logits[:, :, 4:36]
    for t in range(NT):
        dve(V.tensor_scalar, inside[:, t, :], grp_of[:, :], gf[:, t, :], None, ALU.is_equal, after=[m])
    dve(V.tensor_tensor, le, le, inside[:, :, :], ALU.mult)
    dve(V.tensor_scalar, inside[:, :, :], inside[:, :, :], -1.0, BIG, ALU.add, ALU.mult)
    m = dve(V.tensor_tensor, le, le, inside[:, :, :], ALU.add)
    gate, m = expert_gates(le, 32, fe, "a", [m])
    for t in range(NT):
        m = dve(V.tensor_scalar, gate[:, t, :], gate[:, t, :], gs[:, t:t + 1], None, ALU.mult)
    tools = expert_tools(32, 512, gate, xn, colrange("norm_ffn", 0, 8), None, x, fe, "a", m)
    run_experts(8, 4, 12, *tools, "a", (ada_chunk, ada_columns))
    fe.close()

    mod = sb("mod", [P, 48])
    gate_b = sb("gate_b", [P, 2, D])
    fgain = sb("fgain", [P, 2, KD])

    def modulation(layer):
        ad = ExitStack()
        spread = sb(f"spread{layer}", [P, 2, 8, P], where=ad)
        dve(V.tensor_tensor, mod[:, :], mod_all[:, 48 * layer:48 * layer + 48], colrange("ada_b_2", 48 * layer, 48 * layer + 48),
            ALU.add)
        for s_ in range(2):
            g0 = 16 * layer + 8 * s_
            dve(V.scalar_tensor_tensor, fgain[:, s_, :], mod[:, 24 * s_ + 8:24 * s_ + 16], 1.0,
                colrange("norm_g_2", g0, g0 + 8), ALU.add, ALU.mult)
            m = dve(V.tensor_tensor, spread[:, s_, :, :], ident[:, :].unsqueeze(1).to_broadcast([P, 8, P]),
                    mod[:, 24 * s_ + 16:24 * s_ + 24].unsqueeze(2).to_broadcast([P, 8, P]), ALU.mult)
            pe.wait(m)
            ps, free = pair()
            for half in range(2):
                step = product(ps[:, half * 512:(half + 1) * 512],
                               [(ones[:, :], spread[:, s_, 4 * half:4 * half + 4, :].rearrange("p a b -> p (a b)"))])
            m = pe.raised(step)
            free.append(act(S.copy, gate_b[:, s_, :], ps, after=[m]))
        phase()
        ad.close()

    def modulated(s_, tag):
        tmp = ExitStack()
        m, _ = norm_transposed(lambda k: fgain[:, s_, k:k + 1], lambda k: mod[:, 24 * s_ + k:24 * s_ + k + 1], tmp, tag)
        phase()
        tmp.close()
        pe.wait(m)

    def gated_add(half, s_, ps, m, tmp_, free_mark):
        dst = x[:, :, 512 * half:512 * half + 512]
        gv = gate_b[:, s_, 512 * half:512 * half + 512].unsqueeze(1).to_broadcast([P, NT, 512])
        m = dve(V.tensor_tensor, tmp_[:, :, :], ps, gv, ALU.mult, after=[m])
        dve(V.tensor_tensor, dst, dst, tmp_[:, :, :], ALU.add)
        return m

    modulation(0)
    modulated(0, "c")
    ml = ExitStack()
    lat = sb("lat", [P, NT, 672], where=ml)
    unit_by_token(512, by_token_rows(lat, 0, 512))
    unit_by_token(160, by_token_rows(lat, 512, 160))
    pos_i = sb("pos_i", [NT, P], mybir.dt.int32, where=ml)
    lsq = sb("lsq", [P, 384], where=ml)
    pos_f = lsq[0:NT, 0:P]
    load(pos_i[:, :], A["positions_2"][0].rearrange("(t p) -> t p", p=P))
    pos = sb("pos", [P, NT], where=ml)
    ang = sb("ang", [P, 2, NT, 16], where=ml)
    kq = sb("kq", [P, 2, NT, 16], where=ml)
    m = dve(V.tensor_copy, pos_f, pos_i[:, :], after=[small_loads.mark()])
    pe.wait(m)
    ps, free = pair()
    m = pe.raised(pe.put(PE_.transpose, ps[:, 0:NT], pos_f, ident[0:NT, 0:NT]))
    free.append(dve(V.tensor_copy, pos[:, :], ps[:, 0:NT], after=[m]))
    freq = sb("freq", [P, 16], where=ml)
    for n in range(16):
        f = float(np.float32(10000.0) ** np.float32(-2.0 * n / 32))
        pool(G.memset, freq[:, n:n + 1], f)
    for t in range(NT):
        dve(V.tensor_scalar, ang[:, 1, t, :], freq[:, :], pos[:, t:t + 1], None, ALU.mult, after=[pool.mark()])
    magic = 1.5 * 2.0 ** 23
    c1 = 6.28125
    c2 = float(np.float32(np.floor((2 * math.pi - c1) * 2 ** 21) / 2 ** 21))
    c3 = 2 * math.pi - c1 - c2
    dve(V.tensor_copy, ang[:, 0, :, :], ang[:, 1, :, :])
    dve(V.tensor_scalar, kq[:, 1, :, :], ang[:, 1, :, :], 1.0 / (2 * math.pi), None, ALU.mult)
    dve(V.tensor_scalar, kq[:, 0, :, :], ang[:, 0, :, :], 1.0 / (2 * math.pi), 0.25, ALU.mult, ALU.add)
    dve(V.tensor_scalar, kq[:, :, :, :], kq[:, :, :, :], magic, None, ALU.add)
    dve(V.tensor_scalar, kq[:, :, :, :], kq[:, :, :, :], -magic, None, ALU.add)
    for c in (c1, c2, c3):
        dve(V.scalar_tensor_tensor, ang[:, :, :, :].rearrange("p a t n -> p (a t n)"),
            kq[:, :, :, :].rearrange("p a t n -> p (a t n)"), -c,
            ang[:, :, :, :].rearrange("p a t n -> p (a t n)"), ALU.mult, ALU.add)
    dve(V.tensor_scalar, ang[:, 0, :, :], ang[:, 0, :, :], math.pi / 2, None, ALU.add)
    pi_in = float(np.nextafter(np.float32(math.pi), np.float32(0)))
    m = dve(V.tensor_scalar, ang[:, :, :, :], ang[:, :, :, :], pi_in, -pi_in, ALU.min, ALU.max)
    act(S.activation, ang[:, :, :, :], ang[:, :, :, :], ACT.Sin, after=[m])
    cos, sin = ang[:, 0, :, :], ang[:, 1, :, :]

    ls = sb("ls", [P, NT, 2], where=ml)
    lT = sb("lT", [P, 5, T], where=ml)
    for t in range(NT):
        act(S.activation, lsq[:, :], lat[:, t, 0:384], ACT.Square, accum_out=ls[:, t, 0:1])
        act(S.activation, lsq[:, 0:256], lat[:, t, 384:640], ACT.Square, accum_out=ls[:, t, 1:2])
    rsqrt(ls[:, :, 0:1], ls[:, :, 0:1], 1.0 / 384)
    m = rsqrt(ls[:, :, 1:2], ls[:, :, 1:2], 1.0 / 256)
    for t in range(NT):
        dve(V.tensor_scalar, lat[:, t, 0:384], lat[:, t, 0:384], ls[:, t, 0:1], None, ALU.mult, after=[m])
        m2 = dve(V.tensor_scalar, lat[:, t, 384:640], lat[:, t, 384:640], ls[:, t, 1:2], None, ALU.mult)
    pe.wait(m2)
    for f0 in (0, 4):
        fs = range(f0, min(f0 + 4, 5))
        def lat_out(n0, k, ps, m, fs=fs):
            for f in fs:
                c = col("mla_q_norm_2", f) if f < 3 else col("mla_kv_norm_2", f - 3)
                last = dve(V.tensor_scalar, lT[:, f, :], ps[:, (f - fs[0]) * T:(f - fs[0] + 1) * T], c, None, ALU.mult,
                           after=[m])
            return last
        transposed([lat[:, t, f * P:(f + 1) * P] for f in fs for t in range(NT)], lat_out)
    pe.wait(dve.mark())
    mq = sb("mq", [P, NT, 1536], where=ml)
    mkv = sb("mkv", [P, NT, 2048], where=ml)
    for c in range(2):
        w = take()[:, 0:2304].rearrange("p (k n) -> p k n", k=3)
        for c0, n in ((0, 512), (512, 256)):
            ps, free = pair()
            for t in range(NT):
                step = product(ps[:, t * 512:t * 512 + n], [(lT[:, k, t * P:(t + 1) * P], w[:, k, c0:c0 + n]) for k in range(3)])
            if c0:
                give()
            m = pe.raised(step)
            free.append(act(S.copy, mq[:, :, 768 * c + c0:768 * c + c0 + n],
                            ps.rearrange("p (t n) -> p t n", t=NT)[:, :, 0:n], after=[m]))
    w = take().rearrange("p (k n) -> p k n", k=2)
    for c in range(4):
        ps, free = pair()
        for t in range(NT):
            step = product(ps[:, t * 512:(t + 1) * 512],
                           [(lT[:, 3 + k, t * P:(t + 1) * P], w[:, k, 512 * c:512 * c + 512]) for k in range(2)])
        if c == 3:
            give()
        m = pe.raised(step)
        free.append(act(S.copy, mkv[:, :, 512 * c:512 * c + 512], ps.rearrange("p (t n) -> p t n", t=NT), after=[m]))

    mout = sb("mout", [P, NT, D], where=ml)
    rt = mout[:, 0, :].rearrange("p (k h n) -> p k h n", k=4, h=16)

    def rope(v, t, n):
        c_ = cos[:, t, :].unsqueeze(1).to_broadcast([P, n, 16])
        s_ = sin[:, t, :].unsqueeze(1).to_broadcast([P, n, 16])
        a, b = v[:, :, 0:16], v[:, :, 16:32]
        r = [rt[:, k, 0:n, :] for k in range(4)]
        dve(V.tensor_tensor, r[0], a, c_, ALU.mult, after=[act.mark()])
        dve(V.tensor_tensor, r[1], b, s_, ALU.mult)
        dve(V.tensor_tensor, r[2], a, s_, ALU.mult)
        dve(V.tensor_tensor, r[3], b, c_, ALU.mult)
        dve(V.tensor_tensor, a, r[0], r[1], ALU.subtract)
        return dve(V.tensor_tensor, b, r[2], r[3], ALU.add)

    for t in range(NT):
        rope(mq[:, t, :].rearrange("p (h d) -> p h d", d=96)[:, :, 64:96], t, 16)
        rope(lat[:, t, 640:672].unsqueeze(1), t, 1)
    mqT = sb("mqT", [96, 2, 4, T], where=ml)
    mkT = sb("mkT", [96, 2, 4, T], where=ml)
    diag = sb("diag", [P, P], where=ml)
    pool(G.memset, diag[:, :], 0.0)
    m_diag = pool(G.memset, diag[0:64, 64:128], -BIG)
    wgt2 = sb("wgt2", [P, 4], where=ml)
    kcat = sb("kcat", [P, NT, 4, 96], where=ml)
    heads_ready = dve.mark()
    jobs, kcat_read = [], [None]

    def latent_job(g4, t):
        h4, buf = 4 * g4, g4 % 2

        def prepare():
            for t_ in range(NT):
                dve(V.tensor_copy, kcat[:, t_, :, 0:64],
                    mkv[:, t_, :].rearrange("p (h d) -> p h d", d=128)[:, h4:h4 + 4, 0:64], after=[act.mark(), kcat_read[0]])
                m = dve(V.tensor_copy, kcat[:, t_, :, 64:96], lat[:, t_, 640:672].unsqueeze(1).to_broadcast([P, 4, 32]))
            before = [jobs[2 * (g4 - 2) + 1]["multiplied"]] if g4 >= 2 else []
            pe.wait(m, heads_ready)
            transposed([mq[:, t_, 96 * (h4 + j):96 * (h4 + j) + 96] for j in range(4) for t_ in range(NT)],
                       lambda n0, k, ps, m: act(S.copy, mqT[:, buf, :, :].rearrange("p h t -> p (h t)"), ps[0:96, :],
                                                after=[m] + before))
            transposed([kcat[:, t_, j, :] for j in range(4) for t_ in range(NT)],
                       lambda n0, k, ps, m: act(S.copy, mkT[:, buf, :, :].rearrange("p h t -> p (h t)"), ps[0:96, :],
                                                after=[m] + before))
            kcat_read[0] = pe.mark()
            pe.wait(act.mark())

        def score(ps_, s_, marks):
            if t:
                dve(V.tensor_copy, s_[:, :, 0:P], ps_[:, :, 0:P], after=marks, chain=False)
            return dve(V.tensor_tensor, s_[:, :, t * P:(t + 1) * P], ps_[:, :, t * P:(t + 1) * P],
                       diag[:, :].unsqueeze(1).to_broadcast([P, 4, P]), ALU.add, after=marks + [m_diag], chain=False)

        def finish(ps_, den, m):
            dve(V.reciprocal, wgt2[:, :], den, after=[m])
            dst = mout[:, t, 64 * h4:64 * h4 + 256].rearrange("p (h d) -> p h d", d=64)
            return dve(V.tensor_tensor, dst, ps_, wgt2[:, :].unsqueeze(2).to_broadcast([P, 4, 64]), ALU.mult)

        return dict(n_keys=(t + 1) * P, queries=lambda j: mqT[:, buf, j, t * P:(t + 1) * P],
                    keys=lambda j: mkT[:, buf, j, :],
                    values=lambda j, c: mkv[:, c, 128 * (h4 + j) + 64:128 * (h4 + j) + 128],
                    score=score, finish=finish, prepare=prepare if t == 0 else None)

    jobs += [latent_job(g4, t) for g4 in range(4) for t in range(NT)]
    ac = ExitStack()
    attention("mla", jobs, T, 96.0 ** -0.5, ac)
    phase()
    ac.close()
    oT = mq[:, :, :].rearrange("p t n -> p (t n)")[:, 0:KD * T].rearrange("p (k t) -> p k t", k=KD)
    token_tiles_transposed(mout, oT, KD, [dve.mark()])
    ga = mkv[:, 0, 0:NT * 512].rearrange("p (t n) -> p t n", t=NT)
    for half in range(2):
        unit_by_token(512, lambda ps, m, half=half: gated_add(half, 0, ps, m, ga, None), src=oT)
    phase()
    ml.close()

    modulated(1, "d")
    ff = ExitStack()
    mlp_buffers(2816, ff, "f")
    ga = sb("gb_", [P, NT, 512], where=ff)
    mlp(2816, lambda half, ps, m: gated_add(half, 1, ps, m, ga, None), ff, "f", [pe.mark()])
    phase()
    ff.close()

    modulation(1)
    modulated(0, "e")
    sm = ExitStack()
    z = sb("z", [P, NT, 2048], where=sm)
    for c in range(4):
        unit_by_token(512, lambda ps, m, c=c: act(S.activation, z[:, :, 512 * c:512 * c + 512], ps, ACT.Silu, after=[m]))
    xbc = sb("xbc", [P, 24, T], where=sm)
    pad = ExitStack()
    upad = sb("upad2", [P, 2, 4, T + 3], where=pad)
    m_pad = dve(V.memset, upad[:, :, :, 0:3], 0.0)
    act.wait(m_pad)
    conv_done = {}
    for u in range(6):
        buf = upad[:, u % 2, :, :]
        def evacuate(ps, m, buf=buf, u=u):
            return act(S.copy, buf[:, :, 3:T + 3], ps, after=[m, conv_done.get(u - 2)])
        unit_by_feature(evacuate)
        m_in = act.mark()
        for f in range(4):
            c = 4 * u + f
            conv_done[u] = conv_silu(buf, xbc[:, c, :], f, lambda j, c=c: col("ssm_conv_w_2", 24 * j + c), 4,
                                     after=[m_in])
    for c in range(24):
        m = act(S.activation, xbc[:, c, :], xbc[:, c, :], ACT.Silu, bias=col("ssm_conv_b_2", c),
                after=[conv_done[c // 4]])
    phase()
    pad.close()
    dt = sb("dt", [P, NT, 32], where=sm)
    da = sb("da", [P, NT, 32], where=sm)
    t3 = sb("t3b", [P, 3, NT, 32], where=sm)
    ps, free = pair()
    for t in range(NT):
        step = product(ps[:, t * 512:t * 512 + 32], [(hT[:, k, t * P:(t + 1) * P], w_thin[:, k, 32:64]) for k in range(KD)])
    m = pe.raised(step)

    def over_tiles(v):
        return v.unsqueeze(1).to_broadcast([P, NT, 32])

    m = dve(V.tensor_tensor, dt[:, :, :], ps.rearrange("p (t n) -> p t n", t=NT)[:, :, 0:32], over_tiles(ssm_v[:, 0, :]),
            ALU.add, after=[m])
    free.append(m)
    m = softplus(dt[:, :, :], [t3[:, n, :, :] for n in range(3)], dt[:, :, :])
    act(S.activation, ssm_v[:, 1, :], ssm_v[:, 1, :], ACT.Exp)
    m = dve(V.scalar_tensor_tensor, da[:, 0, :], dt[:, 0, :], -1.0, ssm_v[:, 1, :], ALU.mult, ALU.mult, after=[act.mark()])
    m = dve(V.scalar_tensor_tensor, da[:, 1, :], dt[:, 1, :], -1.0, ssm_v[:, 1, :], ALU.mult, ALU.mult)
    pe.wait(m)
    daT = sb("daT", [32, T], where=sm)
    csT = sb("csT", [32, T], where=sm)
    cs = sb("cs", [P, NT, 32], where=sm)
    on32 = sb("on32", [32, T], where=sm)
    transposed([da[:, t, :] for t in range(NT)],
               lambda n0, k, ps, m: dve(V.tensor_copy, daT[:, :], ps[0:32, 0:T], after=[m]))
    dve(V.memset, on32[:, :], 1.0)
    m = dve(V.tensor_tensor_scan, csT[:, :], on32[:, :], daT[:, :], 0.0, ALU.mult, ALU.add)
    pe.wait(m)
    ps, free = pair()
    for t in range(NT):
        step = pe.put(PE_.transpose, ps[:, t * 32:t * 32 + 32], csT[:, t * P:(t + 1) * P], ident[0:32, 0:32])
    m = pe.raised(step)
    free.append(dve(V.tensor_copy, cs[:, :, :].rearrange("p t h -> p (t h)"), ps[:, 0:64], after=[m]))
    xs = sb("xs", [P, NT, 2048], where=sm)
    pe.wait(act.mark())
    for f0 in range(0, 16, 4):
        transposed([xbc[:, f, t * P:(t + 1) * P] for t in range(NT) for f in range(f0, f0 + 4)],
                   lambda n0, k, ps, m, f0=f0: act(S.copy, xs[:, :, f0 * P:(f0 + 4) * P],
                                                   ps.rearrange("p (t n) -> p t n", t=NT), after=[m]))
    cb = sb("cb", [P, 4, 3, P], where=sm)
    for g0 in range(0, 4, 2):
        ps, free = pair()
        for g_ in range(g0, g0 + 2):
            o_ = (g_ - g0) * 512
            product(ps[:, o_:o_ + T], [(xbc[:, 16 + g_, 0:P], xbc[:, 20 + g_, :])])
            step = product(ps[:, o_ + T:o_ + T + P], [(xbc[:, 16 + g_, P:T], xbc[:, 20 + g_, P:T])])
        m = pe.raised(step)
        for g_ in range(g0, g0 + 2):
            o_ = (g_ - g0) * 512
            v = ps[:, o_:o_ + 3 * P].rearrange("p (a c) -> p a c", a=3)
            dve(V.tensor_tensor, cb[:, g_, 0:3:2, :], v[:, 0:3:2, :], upper[:, :].unsqueeze(1).to_broadcast([P, 2, P]),
                ALU.mult, after=[m])
            last = dve(V.tensor_copy, cb[:, g_, 1, :], v[:, 1, :])
        free.append(last)
    NM = 4
    Mt = [sb(f"Mt{b}", [P, 3 * P], where=sm) for b in range(NM)]
    Mfree = [None] * NM
    y = hT[:, 0:4, :].rearrange("p k t -> p (k t)").rearrange("p (t n) -> p t n", t=NT)
    tmpy = sb("tmpy", [P, NT, 512], where=sm)
    ys = sb("ys", [P, NT, 4], where=sm)
    pe.wait(dve.mark(), act.mark())
    state = {}

    def decays(h):
        b = h % NM
        ps, free = pair()
        step = product(ps[:, 0:T], [(ident[0:32, h:h + 1].to_broadcast([32, P]), csT[:, :])])
        m = pe.raised(step)
        dve(V.tensor_scalar, Mt[b][:, 0:T], ps[:, 0:T], cs[:, 0, h:h + 1], 0.0, ALU.subtract, ALU.min,
            after=[m, Mfree[b]], chain=False)
        m = dve(V.tensor_scalar, Mt[b][:, T:T + P], ps[:, P:T], cs[:, 1, h:h + 1], 0.0, ALU.subtract, ALU.min,
                chain=False)
        free.append(m)
        state[h] = act(S.activation, Mt[b][:, :], Mt[b][:, :], ACT.Exp, after=[m], chain=False)

    def weigh(h):
        b = h % NM
        cbv = cb[:, h // 8, :, :].rearrange("p a c -> p (a c)")
        dve(V.scalar_tensor_tensor, Mt[b][:, 0:T], Mt[b][:, 0:T], dt[:, 0, h:h + 1], cbv[:, 0:T], ALU.mult, ALU.mult,
            after=[state[h]])
        state[h] = dve(V.scalar_tensor_tensor, Mt[b][:, T:T + P], Mt[b][:, T:T + P], dt[:, 1, h:h + 1],
                       cbv[:, T:T + P], ALU.mult, ALU.mult, chain=False)

    for g_ in range(4):
        if g_ == 0:
            decays(0)
            decays(1)
        ysum, yfree = pair()
        held.append((turn[0] - 1) % 4)
        for hh in range(8):
            h = 8 * g_ + hh
            weigh(h)
            if h + 2 < 32:
                decays(h + 2)
            pe.wait(state[h])
            b = h % NM
            xv = [xs[:, s_, 64 * h:64 * h + 64] for s_ in range(2)]
            product(ysum[:, 64 * hh:64 * hh + 64], [(Mt[b][:, 0:P], xv[0])])
            step = product(ysum[:, 512 + 64 * hh:512 + 64 * hh + 64], [(Mt[b][:, P:T], xv[0]), (Mt[b][:, T:T + P], xv[1])])
            Mfree[b] = pe.raised(step)
        yv = ysum.rearrange("p (t n) -> p t n", t=NT)
        gx = slice(512 * g_, 512 * g_ + 512)
        m = dve(V.tensor_tensor, tmpy[:, :, :].rearrange("p t (h d) -> p t h d", d=64),
                xs[:, :, gx].rearrange("p t (h d) -> p t h d", d=64),
                ssm_v[:, 2, 8 * g_:8 * g_ + 8].unsqueeze(1).unsqueeze(3).to_broadcast([P, NT, 8, 64]), ALU.mult,
                after=Mfree)
        m = dve(V.tensor_tensor, tmpy[:, :, :], tmpy[:, :, :], yv, ALU.add)
        yfree.append(m)
        held.clear()
        m = dve(V.tensor_tensor, z[:, :, gx], z[:, :, gx], tmpy[:, :, :], ALU.mult)
        for t in range(NT):
            m = act(S.activation, y[:, t, :], z[:, t, gx], ACT.Square, accum_out=ys[:, t, g_:g_ + 1], after=[m])
    m = rsqrt(ys[:, :, :], ys[:, :, :], 1.0 / 512)
    for t in range(NT):
        zt = z[:, t, :].rearrange("p (g n) -> p g n", g=4)
        m2 = dve(V.tensor_tensor, zt, zt, ys[:, t, :].unsqueeze(2).to_broadcast([P, 4, 512]), ALU.mult, after=[m])
    pe.wait(m2)
    zTt = xbc
    m_b = [pe.mark()]
    for f0 in range(0, 16, 4):
        def z_out(n0, k, ps, m, f0=f0):
            for f in range(f0, f0 + 4):
                last = dve(V.tensor_scalar, zTt[:, f, :], ps[:, (f - f0) * T:(f - f0 + 1) * T], col("ssm_norm_2", f), None,
                           ALU.mult, after=[m])
            return last
        transposed([z[:, t, f * P:(f + 1) * P] for f in range(f0, f0 + 4) for t in range(NT)], z_out)
    pe.wait(dve.mark())
    acc = [pair(), pair()]
    for q4 in range(4):
        w = take().rearrange("p (k n) -> p k n", k=4)
        for half in range(2):
            for t in range(NT):
                for k in range(4):
                    kk = 4 * q4 + k
                    step = pe.put(PE_.matmul, acc[half][0][:, t * 512:(t + 1) * 512], zTt[:, kk, t * P:(t + 1) * P],
                                  w[:, k, 512 * half:512 * half + 512], start=kk == 0, stop=kk == 15)
        give()
    m = pe.raised(step)
    for half in range(2):
        acc[half][1].append(gated_add(half, 0, acc[half][0].rearrange("p (t n) -> p t n", t=NT), m, tmpy, None))
    phase()
    sm.close()

    me = ExitStack()
    fg = gate_b[:, 0, :]
    load(fg, A["final_norm_2"].partition_broadcast(P))
    m, xn = norm_transposed(lambda k: fgain[:, 1, k:k + 1], lambda k: mod[:, 24 + k:24 + k + 1], me, "g")
    pe.wait(m)
    lo2 = sb("lo2", [P, NT, 8], where=me)
    ps, free = pair()
    for t in range(NT):
        step = product(ps[:, t * 512:t * 512 + 8], [(hT[:, k, t * P:(t + 1) * P], w_rout[:, k, 36:44]) for k in range(KD)])
    m = pe.raised(step)
    m = act(S.copy, lo2[:, :, :], ps.rearrange("p (t n) -> p t n", t=NT)[:, :, 0:8], after=[m])
    free.append(m)
    gate2, m = expert_gates(lo2, 8, me, "b", [m])
    total = sb("total", [P, NT, D], where=me)
    m = dve(V.memset, total[:, :, :], 0.0)
    tools = expert_tools(8, 2816, gate2, xn, fgain[:, 1, :], mod[:, 24:32], total, me, "b", m)
    run_experts(4, 2, 36, *tools, "b")
    dve(V.tensor_tensor, total[:, :, :], total[:, :, :], gate_b[:, 1, :].unsqueeze(1).to_broadcast([P, NT, D]), ALU.mult)
    m = dve(V.tensor_tensor, x[:, :, :], x[:, :, :], total[:, :, :], ALU.add)
    fs = sb("fs", [P, NT], where=me)
    for t in range(NT):
        act(S.activation, total[:, t, :], x[:, t, :], ACT.Square, accum_out=fs[:, t:t + 1], after=[m])
    m = rsqrt(fs[:, :], fs[:, :], 1.0 / D)
    for t in range(NT):
        m = dve(V.scalar_tensor_tensor, total[:, t, :], x[:, t, :], fs[:, t:t + 1], fg, ALU.mult, ALU.mult,
                after=[m, small_loads.mark()])
    sp.wait(m)
    sp.raised(sp.put(nc.sync.dma_start, out[0].rearrange("(t p) n -> p t n", p=P), total[:, :, :]), stored, 16)
    sp.put(nc.sync.wait_ge, stored.sem, stored.n)
    me.close()

    with ctx, nc.Block() as blk:
        blk.sync(lambda eng: sp.play(eng))
        blk.gpsimd(lambda eng: pool.play(eng))
        blk.scalar(lambda eng: act.play(eng))
        blk.vector(lambda eng: dve.play(eng))
        blk.tensor(lambda eng: pe.play(eng))



def kernel(**inputs):
    import concourse.bacc as bacc
    from concourse.bass_utils import run_bass_kernel_spmd

    nc = bacc.Bacc("TRN2", target_bir_lowering=False, num_devices=1)
    arrays, A = {}, {}
    for name, value in inputs.items():
        a = np.ascontiguousarray(value)
        arrays["in_" + name] = a
        A[name] = nc.dram_tensor("in_" + name, a.shape, mybir.dt.from_np(a.dtype), kind="ExternalInput").ap()
    out = nc.dram_tensor("out", (1, T, D), F32, kind="ExternalOutput").ap()
    block(nc, A, out)
    result = run_bass_kernel_spmd(nc, [arrays], core_ids=[0])
    return result.results[0]["out"]
```

```python
import math
from contextlib import ExitStack, contextmanager

import concourse.bass as bass
import numpy as np
from concourse import mybir

F32 = mybir.dt.float32
F32R = mybir.dt.float32r
U32 = mybir.dt.uint32
ALU = mybir.AluOpType
ACT = mybir.ActivationFunctionType
AX = mybir.AxisListType

P = 128
T = 256
NT = T // P
D = 1024
KD = D // P
UNIT = 4096
SLOTS = 4
EPS = 1e-6
BIG = 1e30


class At:

    def __init__(self, f):
        self.f = f


def at(x, i):
    return x.f(i) if isinstance(x, At) else x


class Loop:
    def __init__(self, count):
        self.count, self.step = count, {}


class Mark:

    def __init__(self, counter, n, loop, back=0):
        self.counter, self.n, self.loop, self.back = counter, n, loop, back

    def value(self, i, loop):
        if self.loop is None:
            return self.n
        step = self.loop.step[self.counter]
        if loop is not self.loop:
            return self.n + (self.loop.count - 1) * step
        least = self.n - self.back * step
        assert least > 0
        return least if step == 0 else i * step + least


class Later:

    def __init__(self, back=0):
        self.marks, self.back = [], back

    def all(self):
        return [Mark(m.counter, m.n, m.loop, self.back) for m in self.marks]


class Counter:

    def __init__(self, sem):
        self.sem, self.n, self.loop = sem, 0, None

    def mark(self):
        return Mark(self, self.n, self.loop)


class Step:
    def __init__(self, op, args, kw, waits):
        self.op, self.args, self.kw, self.waits, self.raises = op, args, kw, waits, []


class Engine(Counter):

    def __init__(self, sem):
        super().__init__(sem)
        self.queue, self.waits, self.before_raise, self.registers = [], [], lambda: None, {}

    def wait(self, *marks):
        self.waits += [m for m in marks if m is not None]

    def put(self, op, *args, **kw):
        step = Step(op, args, kw, self.waits)
        self.waits = []
        self.queue.append(step)
        return step

    def wait_here(self):
        if self.waits:
            self.put(None)

    def raised(self, step, counter=None, by=1):
        if counter is None:
            counter = self
            self.before_raise()
        step.raises.append((counter.sem, by))
        counter.n += by
        return counter.mark()

    def __call__(self, op, *args, after=(), chain=True, **kw):
        if chain and self.n:
            self.wait(self.mark())
        self.wait(*after)
        return self.raised(self.put(op, *args, **kw))

    def play(self, eng, queue=None, i=None, loop=None):
        for step in self.queue if queue is None else queue:
            if isinstance(step, Load):
                for m in [x for w in step.waits for x in (w.all() if isinstance(w, Later) else [w])]:
                    eng.wait_ge(m.counter.sem, m.value(i, loop))
                self.registers[step.name] = eng.value_load(step.ap, min_val=step.low, max_val=step.high)
                continue
            if isinstance(step, Case):
                with eng.If(self.registers[step.number] > step.least):
                    self.play(eng, step.queue, self.registers[step.index], None)
                with eng.Else():
                    for sem, reached, by in step.raises:
                        eng.wait_ge(sem, reached)
                        eng.sem_inc(sem, by)
                continue
            if isinstance(step, tuple):
                with eng.Fori(0, step[0].count) as j:
                    self.play(eng, step[1], j, step[0])
                continue
            best = {}
            for m in [x for w in step.waits for x in (w.all() if isinstance(w, Later) else [w])]:
                key = (m.counter, m.loop is loop, m.back)
                if key not in best or m.n > best[key].n:
                    best[key] = m
            for m in best.values():
                eng.wait_ge(m.counter.sem, m.value(i, loop))
            if step.op is None:
                continue
            ins = step.op(*[at(a, i) for a in step.args], **{k: at(v, i) for k, v in step.kw.items()})
            for sem, by in step.raises:
                ins.then_inc(sem, by)


class Load:

    def __init__(self, name, ap, low, high, waits):
        self.name, self.ap, self.low, self.high, self.waits = name, ap, low, high, waits


class Case:

    def __init__(self, number, least, index, queue, raises):
        self.number, self.least, self.index, self.queue, self.raises = number, least, index, queue, raises


@contextmanager
def repeat(count, engines, counters=()):
    loop = Loop(count)
    kept = {}
    for e in engines:
        e.wait_here()
        kept[e] = (e.queue, e.n)
        e.queue, e.loop = [], loop
    for c in counters:
        kept[c] = (None, c.n)
        c.loop = loop
    yield loop
    for c, (queue, n) in kept.items():
        loop.step[c] = c.n - n
        c.n = n + count * (c.n - n)
        c.loop = None
        if queue is not None:
            queue.append((loop, c.queue))
            c.queue = queue


def block(nc, A, out):
    ctx = ExitStack()
    V, S, G, PE_ = nc.vector, nc.scalar, nc.gpsimd, nc.tensor

    def semaphore(name):
        return ctx.enter_context(nc.semaphore(name))

    dve, act, pool, pe, sp = (Engine(semaphore("steps_" + n)) for n in ("dve", "act", "pool", "pe", "sp"))
    everyone = (dve, act, pool, pe)
    small_loads = Counter(semaphore("small_loads"))
    slot_loaded = [semaphore(f"slot_loaded{n}") for n in range(SLOTS)]
    unit_used = Counter(semaphore("unit_used"))
    stored = Counter(semaphore("stored"))

    def sb(name, shape, dt=F32, where=None):
        return (where or ctx).enter_context(nc.sbuf_tensor(name, shape, dt))

    ring = sb("ring", [P, SLOTS, UNIT])
    sent = [0, None]
    used = [0, None]

    def unit_value(n, loop_of, add):
        loop = loop_of[1]
        if loop is None:
            return n + add
        return At(lambda i: i * loop.units + n + add)

    def send(src, columns):
        n, slot = sent[0], sent[0] % SLOTS
        dst = ring[:, slot, 0:columns]
        if n >= SLOTS or sent[1] is not None:
            sp.put(nc.sync.wait_ge, unit_used.sem, unit_value(n, sent, 1 - SLOTS))
        shape = at(src, 0).shape
        if len(shape) == 3:
            dst = dst.rearrange("p (k n) -> p k n", k=shape[1])
        step = sp.put(nc.sync.dma_start, dst, src)
        step.raises.append((slot_loaded[slot], 16))
        sent[0] += 1

    sp_skipped = [0] * SLOTS

    def skip_to_slot_0():
        for slot in range(sent[0] % SLOTS, SLOTS):
            sp_skipped[slot] += 1
        sent[0] += SLOTS - sent[0] % SLOTS

    def take(eng=pe, count=True):
        n, slot = used[0], used[0] % SLOTS
        loads = 16 * (n // SLOTS + 1 - skipped[slot])
        loop = used[1]
        value = loads if loop is None else At(lambda i: i * (16 * loop.units // SLOTS) + loads)
        eng.put(wait_op[eng], slot_loaded[slot], value)
        used[0] += count
        return ring[:, slot, :]

    wait_op = {pe: nc.tensor.wait_ge, dve: nc.vector.wait_ge, act: nc.scalar.wait_ge}
    skipped = [0] * SLOTS

    pending = [0, 0]

    def give():
        signal_used()
        pending[0] += 1
        pending[1] = len(pe.queue)

    def signal_now(more=0):
        if pending[0] + more:
            pe.wait(pe.mark())
            pe.put(nc.tensor.sem_inc, unit_used.sem, pending[0] + more)
            unit_used.n += pending[0] + more
            pending[0] = 0

    def signal_used():
        if pending[0]:
            for step in pe.queue[pending[1]:-1]:
                if isinstance(step, Step) and step.op in (PE_.matmul, PE_.transpose) and not step.raises:
                    pe.raised(step, unit_used, pending[0])
                    pending[0] = 0
                    return

    pe.before_raise = signal_used

    def rows(w, k0=0, k1=None):
        return w.rearrange("(k p) n -> p k n", p=P)[:, k0:k1, :]

    MOST_OVER = NT * P * 2 // (P + 1)
    E_OF = {"a": 32, "b": 8}
    tables = {tag: sb("table_" + tag, [1, 4], mybir.dt.int32) for tag in "ab"}
    table_ready = {tag: Later() for tag in "ab"}

    def columns_of(w, c0, n):
        kt = w.shape[0] // P
        send(rows(w[:, c0:c0 + n]), kt * n)

    def mlp_units(gate, up, down, F):
        for c0 in range(0, F, 512):
            n = min(512, F - c0)
            for w in (gate, up):
                send(At(lambda i, w=w, c0=c0, n=n: rows(w(i)[:, c0:c0 + n])), KD * n)
        for r0 in range(0, F, 512):
            n = min(512, F - r0)
            send(At(lambda i, r0=r0, n=n: rows(down(i)[r0:r0 + n, :])), (n // P) * D)

    w_in = A["w_in"][0]
    w_branch, w_gate, w_out = A["w_branch"][0], A["w_gate"][0], A["w_out"][0]
    ssm_in, ssm_out = A["ssm_w_in_2"][0], A["ssm_w_out_2"][0]
    O_Q, O_KV, O_NG, O_GQ, O_GZ, O_GB = 1536, 2048, 2816, 2840, 4376, 4888

    ADA = 6144 // 16
    ada_loaded = [semaphore(f"ada_loaded{b}") for b in range(2)]
    ada_used = Counter(semaphore("ada_used"))

    def send_ada(j):
        sp.put(nc.sync.wait_ge, ada_used.sem, At(lambda i: 4 * i + j + 1))
        step = sp.put(nc.sync.dma_start, At(lambda i: ada_place[0][:, j % 2, :, :]),
                      At(lambda i: rows(A["ada_w_2"][j // 2][:, bass.ds((2 * i + j % 2) * ADA, ADA)])))
        step.raises.append((ada_loaded[j % 2], 16))

    ada_place = []

    def start_loop(count, units):
        loop = Loop(count)
        loop.units = units
        return loop

    def stream():
        for c0 in (0, 512, 1024, O_GQ, O_GQ + 512, O_GQ + 1024, O_GZ, O_Q, O_KV):
            columns_of(w_in, c0, 512)
        columns_of(w_in, O_KV + 512, 256)
        for j in range(2):
            columns_of(A["cmp_w1"][0][j], 0, 256)
        for r in range(3):
            columns_of(w_branch[r], 0, 1024)
            for half in range(2):
                columns_of(w_gate, 1024 * r + 512 * half, 512)
        for half in range(2):
            columns_of(w_out, 512 * half, 512)
        first_moe_units()
        columns_of(A["mla_w_in_2"][0], 0, 512)
        columns_of(A["mla_w_in_2"][0], 512, 160)
        for c in range(2):
            columns_of(A["mla_w_uq_2"][0], 768 * c, 768)
        columns_of(A["mla_w_ukv_2"][0], 0, 2048)
        for half in range(2):
            columns_of(A["mla_w_out_2"][0], 512 * half, 512)
        mlp_units(lambda i: A["ffn_w_gate_2"][0], lambda i: A["ffn_w_up_2"][0],
                  lambda i: A["ffn_w_down_2"][0], 2816)
        for c in range(10):
            columns_of(ssm_in, 512 * c, 512)
        for q in range(4):
            send(rows(ssm_out, 4 * q, 4 * q + 4), 4096)
        second_moe_units()

    def first_moe_units():
        skip_to_slot_0()
        count, units = 8, 12
        names = ("w_expert_gate", "w_expert_up", "w_expert_down")
        with repeat(count, [sp]) as loop:
            loop.units, sent[1] = units, loop
            for j in range(4):
                send_ada(j)
                mlp_units(*(lambda i, w=w, j=j: A[w][0][4 * i + j] for w in names), 512)
        sent[0] += (count - 1) * units
        sent[1] = None
        overflow_units("a", names, 512)

    def second_moe_units():
        skip_to_slot_0()
        count, units = 4, 36
        names = ("moe_w_gate_2", "moe_w_up_2", "moe_w_down_2")
        with repeat(count, [sp]) as loop:
            loop.units, sent[1] = units, loop
            for j in range(2):
                mlp_units(*(lambda i, w=w, j=j: A[w][0][2 * i + j] for w in names), 2816)
        sent[0] += (count - 1) * units
        sent[1] = None
        overflow_units("b", names, 2816)

    def overflow_units(tag, names, F):
        sp.wait(table_ready[tag])
        load_table(sp, tag)
        for k in range(MOST_OVER):
            first = sent[0]
            with case(tag, k, [sp]) as raises:
                mlp_units(*(lambda i, w=w: A[w][0][i] for w in names), F)
                for slot in range(SLOTS):
                    units_in = [n for n in range(first, sent[0]) if n % SLOTS == slot]
                    if units_in:
                        reached = 16 * (units_in[0] // SLOTS - sp_skipped[slot])
                        raises[sp].append((slot_loaded[slot], reached, 16 * len(units_in)))

    def load_table(e, tag):
        for n in range(1 + MOST_OVER):
            e.queue.append(Load(f"{tag}{n}", tables[tag][0:1, n:n + 1], 0, MOST_OVER if n == 0 else E_OF[tag] - 1, e.waits))
            e.waits = []

    @contextmanager
    def case(tag, k, engines):
        for e in engines:
            e.wait_here()
        kept = {e: (e.queue, e.n) for e in engines}
        raises = {e: [] for e in engines}
        for e in engines:
            e.queue = []
        yield raises
        for e in engines:
            e.wait_here()
            queue, n = kept[e]
            if e.n > n:
                raises[e].append((e.sem, n, e.n - n))
            queue.append(Case(f"{tag}0", k, f"{tag}{k + 1}", e.queue, raises[e]))
            e.queue = queue

    @contextmanager
    def unit_loop(count, units, counters=()):
        gap = SLOTS - used[0] % SLOTS
        for s in range(SLOTS - gap, SLOTS):
            skipped[s] += 1
        used[0] += gap
        signal_now(gap - 1)
        pending[0] = 1
        with repeat(count, [pe, act, dve], [unit_used, *counters]) as loop:
            loop.units, used[1] = units, loop
            assert pending[0] == 1
            pending[1], first = 0, used[0]
            yield loop
            assert pending[0] == 1 and used[0] - first == units
        pending[1] = len(pe.queue)
        used[0] += (count - 1) * units
        used[1] = None

    stream()

    psum = ctx.enter_context(nc.psum_tensor("psum", [P, 4, 1024], F32))
    pair_free = [[] for _ in range(4)]
    turn = [0]
    held = []

    def pair():
        while turn[0] % 4 in held:
            turn[0] += 1
        n = turn[0] % 4
        turn[0] += 1
        pe.wait(*pair_free[n])
        pair_free[n] = []
        return psum[:, n, :], pair_free[n]

    def product(o, terms):
        for n, (l, r) in enumerate(terms):
            step = pe.put(PE_.matmul, o, l, r, start=n == 0, stop=n == len(terms) - 1)
        return step

    def phase():
        marks = [e.mark() for e in everyone]
        for e in everyone:
            e.wait(*marks)
        return ExitStack()

    def load(dst, src):
        act.raised(act.put(nc.scalar.dma_start, dst, src), small_loads, 16)

    ident = sb("ident", [P, P])
    x = sb("x", [P, NT, D])
    hT = sb("hT", [P, KD, T])
    NCOL = 4 * P
    cols = sb("cols", [P, NCOL])
    eps = sb("eps", [P, 1])
    rows512 = sb("rows512", [6, 512])
    w_thin = sb("w_thin", [P, KD, 64])
    w_rout = sb("w_rout", [P, KD, 44])
    b_rout = sb("b_rout", [P, 36])
    cmp_w2 = sb("cmp_w2", [P, 2, 2, 64])
    gains = sb("gains", [P, 4, 64])
    gdn_ab = sb("gdn_ab", [P, 8])
    ssm_v = sb("ssm_v", [P, 3, 32])
    upper = sb("upper", [P, P])
    ones = sb("ones", [P, P])

    load(x[:, :, :], A["x"][0].rearrange("(t p) n -> p t n", p=P))
    start = ExitStack()
    staged = sb("staged", [P, 4, P], where=start)
    row = [0, 0]
    where = {}

    def stage(name, src, n):
        g, r = row
        load(staged[r:r + n, g, :], src)
        where[name] = g * P + r
        row[1] += n

    def flat(a):
        dims = " ".join("abcd"[:len(a.shape)])
        return a.rearrange(f"{dims} -> ({dims})").rearrange("(r p) -> r p", p=P)

    for name, n in (("norm_mix", 8), ("norm_ffn", 8), ("norm_g_2", 32), ("conv_a_w", 12),
                    ("gdn_conv_w", 48), ("gdn_out_gain", 1), ("mla_q_norm_2", 3), ("mla_kv_norm_2", 2)):
        stage(name, flat(A[name]), n)
    row[:] = [1, 0]
    for name, n in (("cmp_pe", 32), ("ssm_norm_2", 16), ("ssm_conv_b_2", 24), ("c_2", 8)):
        stage(name, flat(A[name]), n)
    row[:] = [2, 0]
    stage("ssm_conv_w_2", flat(A["ssm_conv_w_2"]), 96)
    row[:] = [3, 0]
    stage("ada_b_2", flat(A["ada_b_2"]), 96)

    def col(name, n=0):
        return cols[:, where[name] + n:where[name] + n + 1]

    def colrange(name, n0, n1):
        return cols[:, where[name] + n0:where[name] + n1]

    load(rows512[:, :], A["b_gate"].rearrange("l (r n) -> (l r) n", n=512))
    load(w_thin[:, :, 0:24], rows(w_in[:, O_NG:O_NG + 24]))
    load(w_thin[:, :, 24:32], rows(w_in[:, O_GB:O_GB + 8]))
    load(w_thin[:, :, 32:64], rows(ssm_in[:, 5120:5152]))
    load(w_rout[:, :, 0:4], rows(A["w_router_group"][0]))
    load(w_rout[:, :, 4:36], rows(A["w_router_expert"][0]))
    load(w_rout[:, :, 36:44], rows(A["moe_w_router_2"][0]))
    load(b_rout[:, 0:4], A["b_router_group"][0].partition_broadcast(P))
    load(b_rout[:, 4:36], A["b_router_expert"][0].partition_broadcast(P))
    load(cmp_w2[:, 0, :, :], rows(A["cmp_w2"][0][0]))
    load(cmp_w2[:, 1, :, :], rows(A["cmp_w2"][0][1]))
    load(gains[:, :, :].rearrange("p a b -> p (a b)"),
         A["nsa_qk_gain"][0].rearrange("a b -> (a b)").partition_broadcast(P))
    load(gdn_ab[:, 0:4], A["gdn_a_log"][0].partition_broadcast(P))
    load(gdn_ab[:, 4:8], A["gdn_dt_bias"][0].partition_broadcast(P))
    for n, name in enumerate(("ssm_dt_bias_2", "ssm_a_log_2", "ssm_d_2")):
        load(ssm_v[:, n, :], A[name][0].partition_broadcast(P))
    all_small = small_loads.mark()

    pool(G.memset, ident[:, :], 0.0)
    ident_ready = pool(G.affine_select, out=ident[:, :], in_=ident[:, :], compare_op=ALU.not_equal,
                       fill=1.0, base=0, pattern=[[-1, P]], channel_multiplier=1)
    pool(G.memset, eps[:, :], EPS)
    pool(G.memset, upper[:, :], 1.0)
    pool(G.affine_select, out=upper[:, :], in_=upper[:, :], compare_op=ALU.is_ge, fill=0.0,
         base=0, pattern=[[1, P]], channel_multiplier=-1)
    pool(G.memset, ones[:, :], 1.0)
    consts = pool.mark()

    dve.wait(ident_ready)
    pe.wait(ident_ready, all_small)
    ps, free = pair()
    for g, n in ((0, 114), (1, 80), (2, 96), (3, 96)):
        step = pe.put(PE_.transpose, ps[:, g * P:g * P + n], staged[0:n, g, :], ident[0:n, 0:n])
    m = pe.raised(step)
    for g, n in ((0, 114), (1, 80), (2, 96), (3, 96)):
        m = dve(V.tensor_copy, cols[:, g * P:g * P + n], ps[:, g * P:g * P + n], after=[m])
    free.append(m)
    cols_ready = m
    for e in everyone:
        e.wait(all_small, consts, cols_ready)
    start_marks = phase()
    start.close()

    def rsqrt(dst, src, scale, after=()):
        act(S.activation, dst, src, ACT.Ln, bias=eps[0:dst.shape[0], :], scale=scale, after=after)
        return act(S.activation, dst, dst, ACT.Exp, scale=-0.5)

    def norm_transposed(gain, shift, where, tag, h=None):
        xn = sb("xn" + tag, [P, NT, D], where=where)
        ss = sb("ss" + tag, [P, NT], where=where)
        for t in range(NT):
            act(S.activation, xn[:, t, :], x[:, t, :], ACT.Square, accum_out=ss[:, t:t + 1], after=[dve.mark()])
        m = rsqrt(ss[:, :], ss[:, :], 1.0 / D)
        for t in range(NT):
            m = dve(V.tensor_scalar, xn[:, t, :], x[:, t, :], ss[:, t:t + 1], None, ALU.mult, after=[m])
        pe.wait(m)
        for k4 in range(0, KD, 4):
            ps, free = pair()
            for k in range(4):
                for t in range(NT):
                    step = pe.put(PE_.transpose, ps[:, k * T + t * P:k * T + t * P + P],
                                  xn[:, t, (k4 + k) * P:(k4 + k + 1) * P], ident[:, :])
            m = pe.raised(step)
            for k in range(4):
                src = ps[:, k * T:(k + 1) * T]
                if shift is None:
                    last = dve(V.tensor_scalar, hT[:, k4 + k, :], src, gain(k4 + k), None, ALU.mult, after=[m])
                else:
                    last = dve(V.tensor_scalar, hT[:, k4 + k, :], src, gain(k4 + k), shift(k4 + k),
                               ALU.mult, ALU.add, after=[m])
            free.append(last)
            if h is not None:
                last = split_into(tiles(h, slice(k4, k4 + 4)), hT[:, k4:k4 + 4, :], [last])
        return last, xn

    PARTS, PART = 4, 1024

    def feature_parts(n_tiles=4):
        return [lambda slot, f=f: slot[:, 0:KD * n_tiles * P].rearrange("p (k n) -> p k n", k=KD)[:, :, f * P:(f + 1) * P]
                for f in range(n_tiles)]

    def row_parts(n, kt=KD):
        step = PART // n
        return [lambda slot, k=k: slot[:, 0:kt * n].rearrange("p (k n) -> p k n", k=kt)[:, k:min(k + step, kt), :]
                for k in range(0, kt, step)]

    class Split:

        def __init__(self, name, units, where):
            self.hi = sb(f"w_hi_{name}", [P, PARTS, PART], F32R, where=where)
            self.lo = sb(f"w_lo_{name}", [P, PARTS, PART], F32R, where=where)
            self.todo = [(part, n == 0) for unit in units for n, part in enumerate(unit)]
            self.made, self.read = [], []
            for _ in range(min(PARTS, len(self.todo))):
                self.split()

        def part(self, n, shape):
            return [t[:, n % PARTS, 0:shape[1] * shape[2]].rearrange("p (k n) -> p k n", k=shape[1])
                    for t in (self.hi, self.lo)]

        def split(self):
            n = len(self.made)
            if n == len(self.todo):
                return
            view, new_unit = self.todo[n]
            if new_unit:
                self.slot = take(act)
            src = view(self.slot)
            hi, lo = self.part(n, src.shape)
            before = self.read[n - PARTS:n - PARTS + 1] if n >= PARTS else []
            m = act(S.copy, hi, src, after=before, chain=False)
            m = dve(V.tensor_tensor, lo, src, hi.bitcast(F32), ALU.subtract, after=[m] + before, chain=False)
            self.made.append((m, src.shape))

        def use(self, multiply):
            n = len(self.read)
            m, shape = self.made[n]
            pe.wait(m)
            m = pe.raised(multiply(*self.part(n, shape)))
            self.read.append(m)
            if n + 1 == len(self.todo) or self.todo[n + 1][1]:
                give()
            self.split()
            return m

    def split_product(o, l, r, start, stop):
        pe.put(PE_.matmul, o, l[0], r[0], start=start, stop=False)
        pe.put(PE_.matmul, o, l[1], r[0], start=False, stop=False)
        return pe.put(PE_.matmul, o, l[0], r[1], start=False, stop=stop)

    def split_buffers(name, shape, where):
        return sb(name + "_hi", shape, F32R, where=where), sb(name + "_lo", shape, F32R, where=where)

    def split_into(dst, src, after):
        m = act(S.copy, dst[0], src, after=after, chain=False)
        return dve(V.tensor_tensor, dst[1], src, dst[0].bitcast(F32), ALU.subtract, after=[m] + list(after), chain=False)

    def tiles(pair_, *index):
        return [t[(slice(None),) + index] for t in pair_]

    def by_feature(split, h, f, o):
        def multiply(hi, lo):
            for k in range(KD):
                step = split_product(o, (hi[:, k, :], lo[:, k, :]), tiles(h, k), k == 0, k == KD - 1)
            return step
        return split.use(multiply)

    def unit_by_feature(split, h, evacuate, n_tiles=4):
        ps, free = pair()
        for f in range(n_tiles):
            m = by_feature(split, h, f, ps[:, f * T:(f + 1) * T])
        free.append(evacuate(ps.rearrange("p (f t) -> p f t", f=4), m))

    def rows_by_token(split, h, n_parts, outs, first=0, kt=KD, more=()):
        k0 = [first]
        for part in range(n_parts):
            def multiply(hi, lo):
                kn = hi.shape[1]
                for half, out_ in enumerate(outs):
                    for t in range(NT):
                        n = out_[t].shape[-1]
                        for k in range(kn):
                            w = slice(half * n, half * n + n)
                            last = k0[0] + k == kt - 1
                            step = split_product(out_[t], tiles(h, k0[0] + k, slice(t * P, (t + 1) * P)),
                                                 (hi[:, k, w], lo[:, k, w]), k0[0] + k == 0, last and not more)
                        if last and more:
                            step = more(out_[t])
                k0[0] += kn
                return step
            m = split.use(multiply)
        return m

    def unit_by_token(split, h, n, evacuate, kt=KD, more=()):
        ps, free = pair()
        m = rows_by_token(split, h, len(row_parts(n, kt)), [[ps[:, t * 512:t * 512 + n] for t in range(NT)]], kt=kt,
                          more=more)
        free.append(evacuate(ps.rearrange("p (t n) -> p t n", t=NT)[:, :, 0:n], m))

    def by_token_rows(dst, c0, n, kt=KD):
        return lambda ps, m: act(S.copy, dst[:, :, c0:c0 + n], ps, after=[m])

    def transposed(jobs, copy_out):
        for n0 in range(0, len(jobs), 8):
            ps, free = pair()
            part = jobs[n0:n0 + 8]
            for n, src in enumerate(part):
                r, c = src.shape[0], src.shape[1]
                step = pe.put(PE_.transpose, ps[0:c, n * P:n * P + r], src, ident[0:r, 0:r])
            m = pe.raised(step)
            free.append(copy_out(n0, len(part), ps, m))

    def attention(name, jobs, n_keys, scale, where):
        AHEAD = 2
        s = [sb(f"{name}_s{b}", [P, 4, n_keys], where=where) for b in range(AHEAD + 1)]
        pT = [sb(f"{name}_pT{b}", [P, 8, P], where=where) for b in range(2)]
        mx = sb(f"{name}_mx", [P, len(jobs), 4], where=where)
        den = sb(f"{name}_den", [P, len(jobs), 4], where=where)
        shown, probs, out_done = {}, {}, {}

        def scores(n):
            job = jobs[n]
            nk = job["n_keys"]
            if job.get("prepare"):
                job["prepare"]()
            ps, free = pair()
            for j in range(4):
                step = product(ps[:, j * 256:j * 256 + nk], [(job["queries"](j), job["keys"](j)[:, 0:nk])])
            job["multiplied"] = m = pe.raised(step)
            psv = ps.rearrange("p (h k) -> p h k", h=4)[:, :, 0:nk]
            sv = s[n % (AHEAD + 1)][:, :, 0:nk]
            free.append(job["score"](psv, sv, [m, shown.get(n - AHEAD - 1)]))
            dve(V.tensor_reduce, mx[:, n, :], sv, AX.X, ALU.max)
            m = dve(V.tensor_scalar, mx[:, n, :], mx[:, n, :], -scale, None, ALU.mult)
            for j in range(4):
                m2 = act(S.activation, sv[:, j, :], sv[:, j, :], ACT.Exp, bias=mx[:, n, j:j + 1],
                         scale=scale, accum_out=den[:, n, j:j + 1], after=[m], chain=False)
            probs[n] = m2

        def values(n):
            job = jobs[n]
            nk = job["n_keys"]
            parts = [(k0, min(P, nk - k0)) for k0 in range(0, nk, P)]
            pe.wait(probs[n])
            ps, free = pair()
            for j in range(4):
                for kt, (k0, kn) in enumerate(parts):
                    step = pe.put(PE_.transpose, ps[0:kn, (2 * j + kt) * P:(2 * j + kt + 1) * P],
                                  s[n % (AHEAD + 1)][:, j, k0:k0 + kn], ident[:, :])
            shown[n] = pe.raised(step)
            kn = parts[0][1]
            src = ps.rearrange("p (j c q) -> p j c q", j=4, c=2)[0:kn, :, 0:len(parts), :]
            dst = pT[n % 2][:, :, :].rearrange("p (j c) q -> p j c q", j=4)[0:kn, :, 0:len(parts), :]
            m = act(S.copy, dst, src, after=[shown[n], out_done.get(n - 2)], chain=False)
            free.append(m)
            pe.wait(m)
            ps, free = pair()
            for j in range(4):
                step = product(ps[:, j * 64:(j + 1) * 64],
                               [(pT[n % 2][0:kn, 2 * j + c, :], job["values"](j, c)) for c in range(len(parts))])
            out_done[n] = m = pe.raised(step)
            free.append(job["finish"](ps[:, 0:256].rearrange("p (h d) -> p h d", h=4), den[:, n, :], m))

        for n in range(len(jobs) + AHEAD):
            if n < len(jobs):
                scores(n)
            if n >= AHEAD:
                values(n - AHEAD)

    def conv_silu(padded, out_, f, w_cols, taps, bias=None, after=()):
        m = dve(V.tensor_scalar, out_, padded[:, f, 0:T], w_cols(0), None, ALU.mult, after=after)
        for j in range(1, taps):
            m = dve(V.scalar_tensor_tensor, out_, padded[:, f, j:j + T], w_cols(j), out_, ALU.mult, ALU.add)
        return m

    def softplus(dst, tmp, src, after=()):
        y, w, l = tmp
        dve(V.tensor_scalar, w, src, -1.0, None, ALU.mult, after=after)
        m = dve(V.tensor_tensor, w, w, src, ALU.min)
        m = act(S.activation, y, w, ACT.Exp, after=[m])
        m = dve(V.tensor_scalar, w, y, 1.0, None, ALU.add, after=[m])
        m = act(S.activation, l, w, ACT.Ln, after=[m])
        dve(V.tensor_scalar, w, w, -1.0, 1e-30, ALU.add, ALU.max, after=[m])
        dve(V.reciprocal, w, w)
        dve(V.tensor_tensor, w, w, y, ALU.mult)
        dve(V.tensor_tensor, l, l, w, ALU.mult)
        return dve(V.scalar_tensor_tensor, dst, src, 0.0, l, ALU.max, ALU.add)

    mix = ExitStack()
    yT = sb("yT", [P, 3, 4, T], where=mix)
    thin = sb("thin", [P, NT, 32], where=mix)
    gates = sb("gates", [P, NT, 24], where=mix)
    h_mix = split_buffers("h_mix", [P, KD, T], mix)
    gd = ExitStack()
    qkvT = sb("qkvT", [P, 12, T], where=gd)
    zT = sb("zT", [P, 4, T], where=gd)
    pad = ExitStack()
    split = Split("c", [feature_parts()] * 7, pad)
    tmp = ExitStack()
    m, _ = norm_transposed(lambda k: col("norm_mix", k), None, tmp, "a", h_mix)
    pe.wait(m)
    phase()
    tmp.close()

    cv = ExitStack()
    bT = sb("bT", [P, 4, T], where=cv)
    cT = sb("cT", [P, 4, T + 2], where=cv)
    m_pad = dve(V.memset, cT[:, :, 0:2], 0.0)
    unit_by_feature(split, h_mix, lambda ps, m: act(S.copy, bT[:, :, :], ps, after=[m]))
    unit_by_feature(split, h_mix, lambda ps, m: act(S.copy, cT[:, :, 2:T + 2], ps, after=[m, m_pad]))
    unit_by_feature(split, h_mix, lambda ps, m: dve(V.tensor_tensor, cT[:, :, 2:T + 2], cT[:, :, 2:T + 2], ps, ALU.mult,
                                                after=[m, act.mark()]))
    for f in range(4):
        conv_silu(cT, yT[:, 0, f, :], f, lambda j, f=f: col("conv_a_w", 4 * j + f), 3)
    dve(V.tensor_tensor, yT[:, 0, :, :], yT[:, 0, :, :], bT[:, :, :], ALU.mult)
    phase()
    cv.close()

    upad = sb("upad", [P, 2, 4, T + 3], where=pad)
    m_pad = dve(V.memset, upad[:, :, :, 0:3], 0.0)
    act.wait(m_pad)
    conv_done = {}
    for u in range(3):
        buf = upad[:, u % 2, :, :]
        def evacuate(ps, m, buf=buf, u=u):
            return act(S.copy, buf[:, :, 3:T + 3], ps, after=[m, conv_done.get(u - 2)])
        unit_by_feature(split, h_mix, evacuate)
        for f in range(4):
            c = 4 * u + f
            conv_done[u] = conv_silu(buf, qkvT[:, c, :], f, lambda j, c=c: col("gdn_conv_w", 12 * j + c), 4,
                                     after=[act.mark()])
    unit_by_feature(split, h_mix, lambda ps, m: act(S.activation, zT[:, :, :], ps, ACT.Silu, after=[m]))
    silu_done = act(S.activation, qkvT[:, :, :], qkvT[:, :, :], ACT.Silu, after=[dve.mark()])
    phase()
    pad.close()

    ps, free = pair()
    for t in range(NT):
        step = product(ps[:, t * 512:t * 512 + 32],
                       [(hT[:, k, t * P:(t + 1) * P], w_thin[:, k, 0:32]) for k in range(KD)])
    m = pe.raised(step)
    free.append(act(S.copy, thin[:, :, :], ps.rearrange("p (t n) -> p t n", t=NT)[:, :, 0:32], after=[m]))

    shared = sb("shared", [P, 4, 8, P], where=gd)
    sq = shared[:, 0:2, :, :].rearrange("p a n c -> p (a n c)").rearrange("p (n t) -> p n t", t=T)
    act(S.activation, sq[:, :, :], qkvT[:, 0:8, :], ACT.Square)
    rs = shared[:, 2:4, :, :].rearrange("p a n c -> p (a n c)").rearrange("p (n t) -> p n t", t=T)
    pe.wait(act.mark())
    for half in range(2):
        ps, free = pair()
        for n in range(2):
            s0 = 4 * half + 2 * n
            step = product(ps[:, n * 512:(n + 1) * 512], [(ones[:, :], sq[:, s0:s0 + 2, :].rearrange("p a t -> p (a t)"))])
        m = pe.raised(step)
        free.append(rsqrt(rs[:, 4 * half:4 * half + 4, :], ps.rearrange("p (a t) -> p a t", a=4), 1.0, after=[m]))
    m = act.mark()
    dve(V.scalar_tensor_tensor, qkvT[:, 0:4, :], qkvT[:, 0:4, :], 128.0 ** -0.5, rs[:, 0:4, :], ALU.mult, ALU.mult,
        after=[m])
    dve(V.tensor_tensor, qkvT[:, 4:8, :], qkvT[:, 4:8, :], rs[:, 4:8, :], ALU.mult)
    beta = sb("beta", [P, NT, 4], where=gd)
    g = sb("g", [P, NT, 4], where=gd)
    t3 = sb("t3", [P, 3, NT, 4], where=gd)
    ea = sb("ea", [P, 4], where=gd)
    act(S.activation, beta[:, :, :], thin[:, :, 24:28], ACT.Sigmoid)
    act(S.activation, gates[:, :, :], thin[:, :, 0:24], ACT.Sigmoid)
    act(S.activation, ea[:, :], gdn_ab[:, 0:4], ACT.Exp)
    for t in range(NT):
        dve(V.tensor_tensor, g[:, t, :], thin[:, t, 28:32], gdn_ab[:, 4:8], ALU.add, after=[act.mark()])
    softplus(g[:, :, :], [t3[:, n, :, :] for n in range(3)], g[:, :, :])
    for t in range(NT):
        m = dve(V.scalar_tensor_tensor, g[:, t, :], g[:, t, :], -1.0, ea[:, :], ALU.mult, ALU.mult)
    gc = sb("gc", [P, 2, NT * 4], where=gd)
    g8 = g[:, :, :].rearrange("p t h -> p (t h)")
    pe.wait(m)
    ps, free = pair()
    product(ps[:, 0:8], [(upper[:, :], g8)])
    step = product(ps[:, 8:16], [(ones[:, :], g8)])
    m = pe.raised(step)
    m = dve(V.tensor_copy, gc[:, :, :], ps[:, 0:16].rearrange("p (a b) -> p a b", a=2), after=[m])
    free.append(m)
    ps, free = pair()
    for n in range(8):
        step = product(ps[:, n * P:(n + 1) * P], [(g8[:, n:n + 1].to_broadcast([P, P]), upper[:, :])])
    m = pe.raised(step)
    dec = sb("dec", [P, 8, P], where=gd)
    decT = sb("decT", [P, 8, P], where=gd)
    gcc = gc[:, 0, :].unsqueeze(2).to_broadcast([P, 8, P])
    psn = ps.rearrange("p (n c) -> p n c", n=8)
    dve(V.tensor_tensor, decT[:, :, :], psn, gcc, ALU.subtract, after=[m])
    free.append(dve.mark())
    dve(V.tensor_scalar, dec[:, :, :], decT[:, :, :], -1.0, 0.0, ALU.mult, ALU.min)
    m = dve(V.tensor_scalar, decT[:, :, :], decT[:, :, :], 0.0, None, ALU.min)
    act(S.activation, dec[:, :, :], dec[:, :, :], ACT.Exp, after=[m])
    act(S.activation, decT[:, :, :], decT[:, :, :], ACT.Exp)
    eg = sb("eg", [P, 2, 8], where=gd)
    m = dve(V.tensor_tensor, eg[:, 1, :], gc[:, 1, :], gc[:, 0, :], ALU.subtract)
    act(S.activation, eg[:, 1, :], eg[:, 1, :], ACT.Exp, after=[m])
    act(S.activation, eg[:, 0, :], gc[:, 0, :], ACT.Exp)
    slow = sb("slow", [P, P], where=gd)
    pool(G.memset, slow[:, :], 1.0)
    pool(G.affine_select, out=slow[:, :], in_=slow[:, :], compare_op=ALU.is_ge, fill=0.0, base=-1,
         pattern=[[-1, P]], channel_multiplier=1)
    levels = [1 << n for n in range(7)]
    lev = sb("lev", [P, 7, P], where=gd)
    for n, b in enumerate(levels):
        v = lev[:, n, :].rearrange("p (j h r) -> p j h r", h=2, r=b)
        pool(G.memset, v[:, :, 0, :], 0.0)
        pool(G.memset, v[:, :, 1, :], 1.0)
        nj = P // (2 * b)
        v1 = v[:, :, 1, :]
        pool(G.affine_select, out=v1, in_=v1, compare_op=ALU.is_ge, fill=0.0, base=0,
             pattern=[[-2 * b, nj], [0, b]], channel_multiplier=1)
        pool(G.affine_select, out=v1, in_=v1, compare_op=ALU.is_ge, fill=0.0, base=b - 1,
             pattern=[[2 * b, nj], [0, b]], channel_multiplier=-1)
    masks_ready = pool.mark()

    def over8(a):
        return a.unsqueeze(1).to_broadcast([P, 8, P])

    dve(V.tensor_tensor, dec[:, :, :], dec[:, :, :], over8(slow[:, :]), ALU.mult, after=[act.mark(), masks_ready])
    m = dve(V.tensor_tensor, decT[:, :, :], decT[:, :, :], over8(upper[:, :]), ALU.mult)

    def qT(h, t):
        return qkvT[:, h, t * P:(t + 1) * P]

    def kT(h, t):
        return qkvT[:, 4 + h, t * P:(t + 1) * P]

    L, LT, X, XT = (shared[:, n, :, :] for n in range(4))
    atT = sb("atT", [P, 8, P], where=gd)
    pe.wait(m)
    ps, free = pair()
    for n in range(8):
        step = product(ps[:, n * P:(n + 1) * P], [(kT(n % 4, n // 4), kT(n % 4, n // 4))])
    m = pe.raised(step)
    dve(V.tensor_tensor, L[:, :, :], dec[:, :, :], ps.rearrange("p (n c) -> p n c", n=8), ALU.mult, after=[m])
    free.append(dve.mark())
    b8 = beta[:, :, :].rearrange("p t h -> p (t h)")
    m_L = dve(V.tensor_tensor, L[:, :, :], L[:, :, :], b8.unsqueeze(2).to_broadcast([P, 8, P]), ALU.mult)
    ps, free = pair()
    for n in range(8):
        step = product(ps[:, n * P:(n + 1) * P], [(kT(n % 4, n // 4), qT(n % 4, n // 4))])
    m = pe.raised(step)
    dve(V.tensor_tensor, atT[:, :, :], decT[:, :, :], ps.rearrange("p (n c) -> p n c", n=8), ALU.mult, after=[m])
    free.append(dve.mark())
    pe.wait(m_L)
    transposed([L[:, n, :] for n in range(8)],
               lambda n0, k, ps, m: act(S.copy, LT[:, :, :], ps.rearrange("p (n c) -> p n c", n=8), after=[m]))
    kb = sb("kb", [P, 8, P], where=gd)
    kd = sb("kd", [P, 8, P], where=gd)
    vb = sb("vb", [P, 8, P], where=gd)
    m = dve(V.tensor_tensor, gc[:, 0, :], b8, eg[:, 0, :], ALU.mult, after=[act.mark()])

    def k_out(n0, k, ps, m):
        src = ps.rearrange("p (n c) -> p n c", n=8)
        dve(V.tensor_tensor, kb[:, :, :], src, gc[:, 0, :].unsqueeze(2).to_broadcast([P, 8, P]), ALU.mult, after=[m])
        return dve(V.tensor_tensor, kd[:, :, :], src, eg[:, 1, :].unsqueeze(2).to_broadcast([P, 8, P]), ALU.mult)

    def v_out(n0, k, ps, m):
        src = ps.rearrange("p (n c) -> p n c", n=8)
        return dve(V.tensor_tensor, vb[:, :, :], src, b8.unsqueeze(2).to_broadcast([P, 8, P]), ALU.mult, after=[m])

    transposed([kT(n % 4, n // 4) for n in range(8)], k_out)
    transposed([qkvT[:, 8 + n % 4, (n // 4) * P:(n // 4 + 1) * P] for n in range(8)], v_out)

    Z = sb("Z", [P, 8, P], where=gd)
    LbT = dec
    dve(V.tensor_tensor, XT[:, :, :], LT[:, :, :], over8(lev[:, 0, :]), ALU.mult, after=[act.mark()])
    m = dve(V.tensor_tensor, XT[:, :, :], over8(ident[:, :]), XT[:, :, :], ALU.subtract)
    pe.wait(m)
    transposed([XT[:, n, :] for n in range(8)],
               lambda n0, k, ps, m: act(S.copy, X[:, :, :], ps.rearrange("p (n c) -> p n c", n=8), after=[m]))
    m_x = act.mark()
    for lv in range(1, 7):
        m = dve(V.tensor_tensor, LbT[:, :, :], LT[:, :, :], over8(lev[:, lv, :]), ALU.mult, after=[pe.mark()])
        pe.wait(m, m_x)
        ps, free = pair()
        for n in range(8):
            step = product(ps[:, n * P:(n + 1) * P], [(LbT[:, n, :], X[:, n, :])])
        m = pe.raised(step)
        m = act(S.copy, Z[:, :, :], ps.rearrange("p (n c) -> p n c", n=8), after=[m])
        free.append(m)
        pe.wait(m)
        last = lv == 6
        if not last:
            ps, free = pair()
            for n in range(8):
                step = product(ps[:, n * P:(n + 1) * P], [(XT[:, n, :], Z[:, n, :])])
            m = pe.raised(step)
            free_x, ps_x = free, ps
        ps, free = pair()
        for n in range(8):
            step = product(ps[:, n * P:(n + 1) * P], [(Z[:, n, :], XT[:, n, :])])
        m = pe.raised(step)
        if not last:
            m_x = dve(V.tensor_tensor, X[:, :, :], X[:, :, :], ps_x.rearrange("p (n c) -> p n c", n=8), ALU.subtract,
                      after=[m])
            free_x.append(m_x)
        m_x = dve(V.tensor_tensor, XT[:, :, :], XT[:, :, :], ps.rearrange("p (n c) -> p n c", n=8), ALU.subtract,
                  after=[m])
        free.append(m_x)
    U, WT, ST = L, LT, Z
    pe.wait(m_x)
    ps, free = pair()
    for n in range(8):
        step = product(ps[:, n * P:(n + 1) * P], [(XT[:, n, :], vb[:, n, :])])
    m = pe.raised(step)
    m_u = act(S.copy, U[:, :, :], ps.rearrange("p (n c) -> p n c", n=8), after=[m])
    free.append(m_u)
    ps, free = pair()
    for h in range(4):
        step = product(ps[:, h * P:(h + 1) * P], [(kb[:, 4 + h, :], XT[:, 4 + h, :])])
    m = pe.raised(step)
    free.append(act(S.copy, WT[:, 0:4, :], ps[:, 0:512].rearrange("p (n c) -> p n c", n=4), after=[m]))
    pe.wait(act.mark())
    ps, free = pair()
    for h in range(4):
        step = product(ps[:, h * P:(h + 1) * P], [(kd[:, h, :], U[:, h, :])])
    m = pe.raised(step)
    m = act(S.copy, ST[:, 0:4, :], ps[:, 0:512].rearrange("p (n c) -> p n c", n=4), after=[m])
    free.append(m)
    pe.wait(m)
    ps, free = pair()
    for h in range(4):
        product(ps[:, h * P:(h + 1) * P], [(WT[:, h, :], ST[:, h, :])])
    for h in range(4):
        step = product(ps[:, 512 + h * P:512 + (h + 1) * P], [(qT(h, 1), ST[:, h, :])])
    m = pe.raised(step)
    ps4 = ps.rearrange("p (a n c) -> p a n c", a=2, n=4)
    m = dve(V.tensor_tensor, U[:, 4:8, :], U[:, 4:8, :], ps4[:, 0, :, :], ALU.subtract, after=[m])
    o = X
    m2 = dve(V.tensor_tensor, o[:, 4:8, :], ps4[:, 1, :, :], eg[:, 0, 4:8].unsqueeze(2).to_broadcast([P, 4, P]), ALU.mult)
    free.append(m2)
    pe.wait(m)
    ps, free = pair()
    for n in range(8):
        step = product(ps[:, n * P:(n + 1) * P], [(atT[:, n, :], U[:, n, :])])
    m = pe.raised(step)
    ps8 = ps.rearrange("p (n c) -> p n c", n=8)
    dve(V.tensor_copy, o[:, 0:4, :], ps8[:, 0:4, :], after=[m])
    m = dve(V.tensor_tensor, o[:, 4:8, :], o[:, 4:8, :], ps8[:, 4:8, :], ALU.add)
    free.append(m)
    os_ = sb("os", [P, 8], where=gd)
    dve(V.tensor_tensor, XT[:, :, :], o[:, :, :], o[:, :, :], ALU.mult)
    m = dve(V.tensor_reduce, os_[:, :], XT[:, :, :], AX.X, ALU.add)
    m = rsqrt(os_[:, :], os_[:, :], 1.0 / 128, after=[m])
    m = dve(V.tensor_tensor, o[:, :, :], o[:, :, :], os_[:, :].unsqueeze(2).to_broadcast([P, 8, P]), ALU.mult,
            after=[m])
    pe.wait(m)

    def o_out(n0, k, ps, m):
        for t in range(NT):
            last = dve(V.scalar_tensor_tensor, yT[:, 2, :, t * P:(t + 1) * P],
                       ps.rearrange("p (t h c) -> p t h c", t=NT, h=4)[:, t, :, :], col("gdn_out_gain"),
                       zT[:, :, t * P:(t + 1) * P], ALU.mult, ALU.mult, after=[m])
        return last

    transposed([o[:, n, :] for n in range(8)], o_out)
    phase()
    gd.close()

    ns = ExitStack()
    q = sb("q", [P, NT, 512], where=ns)
    kv = sb("kv", [P, NT, 768], where=ns)
    sl = ExitStack()
    split = Split("n", [row_parts(512), row_parts(512), row_parts(256)], sl)
    unit_by_token(split, h_mix, 512, by_token_rows(q, 0, 512))
    unit_by_token(split, h_mix, 512, by_token_rows(kv, 0, 512))
    unit_by_token(split, h_mix, 256, by_token_rows(kv, 512, 256))
    phase()
    sl.close()
    dist = sb("dist", [P, NT, T], where=ns)
    distc = sb("distc", [P, NT, 15], where=ns)
    seen = sb("seen", [P, NT], where=ns)
    pool(G.iota, dist[:, :, :], pattern=[[P, NT], [-1, T]], base=0, channel_multiplier=1,
         allow_small_or_imprecise_dtypes=True)
    pool(G.affine_select, out=dist[:, :, :], in_=dist[:, :, :], compare_op=ALU.is_ge, fill=BIG, base=0,
         pattern=[[P, NT], [-1, T]], channel_multiplier=1)
    pool(G.iota, distc[:, :, :], pattern=[[P, NT], [-16, 15]], base=-31, channel_multiplier=1,
         allow_small_or_imprecise_dtypes=True)
    pool(G.affine_select, out=distc[:, :, :], in_=distc[:, :, :], compare_op=ALU.is_ge, fill=BIG, base=-31,
         pattern=[[P, NT], [-16, 15]], channel_multiplier=1)
    pool(G.memset, seen[:, :], 1.0)
    dist_ready = pool(G.affine_select, out=seen[:, :], in_=seen[:, :], compare_op=ALU.is_ge, fill=0.0, base=-31,
                      pattern=[[P, NT]], channel_multiplier=1)
    sq = sb("nsq", [P, NT, 1024], where=ns)
    rn = sb("nrn", [P, NT, 16], where=ns)

    def head_norm(buf, c0, n, gain, scale, k0):
        v = buf[:, :, c0:c0 + 64 * n]
        w = sq[:, :, 0:64 * n]
        dve(V.tensor_tensor, w, v, v, ALU.mult, after=[act.mark()])
        for t in range(NT):
            m = dve(V.tensor_reduce, rn[:, t, k0:k0 + n], w[:, t, :].rearrange("p (n d) -> p n d", d=64), AX.X, ALU.add)
        m = rsqrt(rn[:, :, k0:k0 + n], rn[:, :, k0:k0 + n], 1.0 / 64, after=[m])
        for t in range(NT):
            vt = v[:, t, :].rearrange("p (n d) -> p n d", d=64)
            dve(V.tensor_tensor, vt, vt, rn[:, t, k0:k0 + n].unsqueeze(2).to_broadcast([P, n, 64]), ALU.mult, after=[m])
            if scale != 1.0:
                dve(V.tensor_scalar, vt, vt, scale, None, ALU.mult)
            last = dve(V.tensor_tensor, vt, vt, gain.unsqueeze(1).to_broadcast([P, n, 64]), ALU.mult)
        return last

    head_norm(q, 0, 8, gains[:, 0, :], 64.0 ** -0.5, 0)
    head_norm(kv, 256, 2, gains[:, 2, :], 1.0, 8)
    m = head_norm(kv, 512, 2, gains[:, 3, :], 1.0, 10)
    nqT = sb("nqT", [64, 8, T], where=ns)
    nkT = sb("nkT", [64, 4, T], where=ns)
    pe.wait(m)
    for h0 in range(0, 8, 4):
        transposed([q[:, t, 64 * h:64 * h + 64] for h in range(h0, h0 + 4) for t in range(NT)],
                   lambda n0, k, ps, m, h0=h0: act(S.copy, nqT[:, h0:h0 + 4, :].rearrange("p h t -> p (h t)"),
                                                   ps[0:64, :], after=[m]))
    transposed([kv[:, t, 256 + 256 * b + 64 * gr_:256 + 256 * b + 64 * gr_ + 64]
                for b in range(2) for gr_ in range(2) for t in range(NT)],
               lambda n0, k, ps, m: act(S.copy, nkT[:, :, :].rearrange("p h t -> p (h t)"), ps[0:64, :], after=[m]))
    dup = sb("dup", [P, 4, NT, P], where=ns)
    for jg in range(4):
        for c in range(2):
            dve(V.tensor_copy, dup[:, jg, :, 64 * c:64 * c + 64], kv[:, :, 64 * jg:64 * jg + 64])
    kcT = sb("kcT", [P, 4, T], where=ns)
    pe.wait(dve.mark())
    transposed([dup[:, jg, t, :] for jg in range(4) for t in range(NT)],
               lambda n0, k, ps, m: act(S.copy, kcT[:, :, :].rearrange("p h t -> p (h t)"), ps, after=[m]))
    fl = sb("fl", [P, 2, 16, 2, 15], where=ns)
    for j in range(2):
        for g_ in range(2):
            toks = kcT[:, 2 * j + g_, :].rearrange("p (c s) -> p s c", s=16)
            for odd in range(2):
                r = slice(64 * odd, 64 * odd + 64)
                for half in range(2):
                    pe_cols = colrange("cmp_pe", 16 * j + 8 * half, 16 * j + 8 * half + 8)[r, :]
                    dve(V.tensor_tensor, fl[r, j, 8 * half:8 * half + 8, g_, :],
                        toks[r, odd:16:2, half:half + 15], pe_cols.unsqueeze(2).to_broadcast([64, 8, 15]), ALU.add,
                        after=[act.mark()])
    pe.wait(dve.mark())
    h1 = sb("h1", [30, 2, 256], where=ns)
    h2 = sb("h2", [30, 2, 256], where=ns)
    for j in range(2):
        w = take().rearrange("p (k n) -> p k n", k=16)
        ps, free = pair()
        step = product(ps[0:30, 0:256], [(fl[:, j, k, :, :].rearrange("p g c -> p (g c)"), w[:, k, :]) for k in range(16)])
        give()
        m = pe.raised(step)
        free.append(act(S.copy, h1[:, j, :], ps[0:30, 0:256], after=[m]))
    dve(V.tensor_tensor, h2[:, :, :], h1[:, :, :], h1[:, :, :], ALU.mult, after=[act.mark()])
    dve(V.tensor_scalar, h2[:, :, :], h2[:, :, :], 0.044715, 1.0, ALU.mult, ALU.add)
    m = dve(V.tensor_tensor, h2[:, :, :], h2[:, :, :], h1[:, :, :], ALU.mult)
    m = act(S.activation, h2[:, :, :], h2[:, :, :], ACT.Sigmoid, scale=2.0 * math.sqrt(2.0 / math.pi), after=[m])
    m = dve(V.tensor_tensor, h1[:, :, :], h1[:, :, :], h2[:, :, :], ALU.mult, after=[m])
    pe.wait(m)
    h1T = sb("h1T", [P, 4, 30], where=ns)
    transposed([h1[:, j, P * c:P * c + P] for j in range(2) for c in range(2)],
               lambda n0, k, ps, m: act(S.copy, h1T[:, :, :], ps[:, 0:512].rearrange("p (n c) -> p n c", n=4)[:, :, 0:30],
                                        after=[m]))
    pe.wait(act.mark())
    kc = sb("kc", [30, 4, 64], where=ns)
    vcT = sb("vcT", [64, 30], where=ns)
    rc = sb("rc", [30, 1], where=ns)
    ps, free = pair()
    product(ps[0:30, 0:64], [(h1T[:, c, :], cmp_w2[:, 0, c, :]) for c in range(2)])
    step = product(ps[0:64, 512:542], [(cmp_w2[:, 1, c, :], h1T[:, 2 + c, :]) for c in range(2)])
    m = pe.raised(step)
    act(S.copy, vcT[:, :], ps[0:64, 512:542], after=[m])
    act(S.copy, kc[:, 0, :], ps[0:30, 0:64])
    m = act(S.activation, kc[:, 1, :], kc[:, 0, :], ACT.Square, accum_out=rc[:, :])
    free.append(m)
    m = rsqrt(rc[:, :], rc[:, :], 1.0 / 64)
    dve(V.tensor_scalar, kc[:, 0, :], kc[:, 0, :], rc[:, :], None, ALU.mult, after=[m])
    m = dve(V.tensor_tensor, kc[:, 0, :], kc[:, 0, :], gains[0:30, 1, :], ALU.mult)
    pe.wait(m)
    kcT2 = sb("kcT2", [64, 30], where=ns)
    vc = sb("vc", [15, 2, 64], where=ns)
    ps, free = pair()
    pe.put(PE_.transpose, ps[0:64, 0:30], kc[:, 0, :], ident[0:30, 0:30])
    pe.put(PE_.transpose, ps[0:15, 128:192], vcT[:, 0:15], ident[0:64, 0:64])
    step = pe.put(PE_.transpose, ps[0:15, 256:320], vcT[:, 15:30], ident[0:64, 0:64])
    m = pe.raised(step)
    act(S.copy, kcT2[:, :], ps[0:64, 0:30], after=[m])
    act(S.copy, vc[:, 0, :], ps[0:15, 128:192])
    free.append(act(S.copy, vc[:, 1, :], ps[0:15, 256:320]))
    pe.wait(act.mark())

    yn = sb("yn", [P, NT, 512], where=ns)
    wgt = sb("wgt", [P, 4], where=ns)
    slopes = [2.0 ** (-8.0 * (h + 1) / 8) for h in range(8)]

    def branch_jobs(br, d, keys_of, k_of, v_of):
        def job(t, h0):
            def score(ps_, s_, marks):
                for j in range(4):
                    last = dve(V.scalar_tensor_tensor, s_[:, j, :], d[:, t, 0:s_.shape[2]], -slopes[h0 + j], ps_[:, j, :],
                               ALU.mult, ALU.add, after=marks + [dist_ready], chain=False)
                return last

            def finish(ps_, den, m):
                dve(V.reciprocal, wgt[:, :], den, after=[m])
                dve(V.tensor_tensor, wgt[:, :], wgt[:, :], gates[:, t, 8 * br + h0:8 * br + h0 + 4], ALU.mult)
                if br == 0:
                    dve(V.tensor_scalar, wgt[:, :], wgt[:, :], seen[:, t:t + 1], None, ALU.mult)
                for j in range(4):
                    y = yn[:, t, 64 * (h0 + j):64 * (h0 + j) + 64]
                    if br == 0:
                        last = dve(V.tensor_scalar, y, ps_[:, j, :], wgt[:, j:j + 1], None, ALU.mult, chain=j == 0)
                    else:
                        last = dve(V.scalar_tensor_tensor, y, ps_[:, j, :], wgt[:, j:j + 1], y, ALU.mult, ALU.add,
                                   chain=j == 0)
                return last

            return dict(n_keys=keys_of(t), queries=lambda j: nqT[:, h0 + j, t * P:(t + 1) * P],
                        keys=lambda j: k_of(h0 + j), values=lambda j, c: v_of(h0 + j, c), score=score, finish=finish)
        return [job(t, h0) for t in range(NT) for h0 in (0, 4)]

    jobs = branch_jobs(0, distc, lambda t: 15, lambda h: kcT2[:, 15 * (h // 4):15 * (h // 4) + 15],
                       lambda h, c: vc[:, h // 4, :])
    for b in range(2):
        jobs += branch_jobs(1 + b, dist, lambda t: (t + 1) * P, lambda h, b=b: nkT[:, 2 * b + h // 4, :],
                            lambda h, c, b=b: kv[:, c, 384 + 256 * b + 64 * (h // 4):384 + 256 * b + 64 * (h // 4) + 64])
    at_ctx = ExitStack()
    attention("nsa", jobs, T, 1.0, at_ctx)
    phase()
    at_ctx.close()
    def yn_out(n0, k, ps, m):
        return act(S.copy, yT[:, 1, :, :].rearrange("p f t -> p (f t)"), ps, after=[m])
    transposed([yn[:, t, f * P:(f + 1) * P] for f in range(4) for t in range(NT)], yn_out)
    phase()
    ns.close()

    mg = ExitStack()
    merged = sb("merged", [P, NT, D], where=mg)
    mg_in = ExitStack()
    sg = [sb(f"sg{b}", [P, NT, 512], where=mg_in) for b in range(2)]
    sg_free = [None, None]
    ys_ = split_buffers("ys", [P, 3, 4, T], mg_in)
    split = Split("m", ([row_parts(1024, 4)] + [row_parts(512)] * 2) * 3, mg_in)
    for r in range(3):
        pe.wait(split_into(tiles(ys_, r), yT[:, r, :, :], []))
    for r in range(3):
        halves = [pair(), pair()]
        m = rows_by_token(split, tiles(ys_, r), 4, [[ps[:, t * 512:(t + 1) * 512] for t in range(NT)] for ps, _ in halves],
                          kt=4)
        halves = [(ps, free, m) for ps, free in halves]
        for half in range(2):
            ps, free = pair()
            n = 2 * r + half

            def bias(o, n=n):
                return pe.put(PE_.matmul, o, ident[0:6, n:n + 1].to_broadcast([6, P]), rows512[:, :], start=False, stop=True)

            m = rows_by_token(split, h_mix, 4, [[ps[:, t * 512:(t + 1) * 512] for t in range(NT)]], more=bias)
            b = half
            s3 = sg[b][:, :, :]
            m = act(S.activation, s3, ps.rearrange("p (t n) -> p t n", t=NT), ACT.Sigmoid, after=[m, sg_free[b]])
            free.append(m)
            br_ps, br_free, br_m = halves[half]
            dst = merged[:, :, 512 * half:512 * half + 512]
            brv = br_ps.rearrange("p (t n) -> p t n", t=NT)
            if r == 0:
                m = dve(V.tensor_tensor, dst, s3, brv, ALU.mult, after=[m, br_m])
                br_free.append(m)
            else:
                m = dve(V.tensor_tensor, s3, s3, brv, ALU.mult, after=[m, br_m])
                br_free.append(m)
                m = dve(V.tensor_tensor, dst, dst, s3, ALU.add)
            sg_free[b] = m

    def token_tiles_transposed(src, dst, n_f, after):
        pe.wait(*after)
        for f0 in range(0, n_f, 4):
            transposed([src[:, t, f * P:(f + 1) * P] for f in range(f0, f0 + 4) for t in range(NT)],
                       lambda n0, k, ps, m, f0=f0: split_into(
                           [t[:, f0:f0 + 4, :].rearrange("p f t -> p (f t)") for t in dst], ps, [m]))
        pe.wait(dve.mark())

    phase()
    mg_in.close()
    mg_out = ExitStack()
    split = Split("o", [row_parts(512)] * 2, mg_out)
    mT = split_buffers("mT", [P, KD, T], mg_out)
    token_tiles_transposed(merged, mT, KD, [])
    for half in range(2):
        dst = x[:, :, 512 * half:512 * half + 512]
        unit_by_token(split, mT, 512, lambda ps, m, dst=dst: dve(V.tensor_tensor, dst, dst, ps, ALU.add, after=[m]))
    phase()
    mg_out.close()
    mg.close()
    mix.close()

    def mlp(F, down_out, where, tag):
        sil = sb("sil" + tag, [P, 2, 1024], where=where)
        gated = sb("gated" + tag, [P, 1024], where=where)
        chunks = [min(512, F - c0) // P for c0 in range(0, F, 512)]
        units = [feature_parts(nf) for nf in chunks for _ in range(2)]
        units += [row_parts(D, nf) for nf in chunks]
        split = Split(tag, units, where)
        h = split_buffers("h_" + tag, [P, KD, T], where)
        modulated(1, "d", h)
        mid = split_buffers("mid" + tag, [P, F // P, T], where)
        splits = {}
        for c, nf in enumerate(chunks):
            psg, free_g = pair()
            for f in range(nf):
                m_g = by_feature(split, h, f, psg[:, f * T:(f + 1) * T])
            s3, p3 = sil[:, c % 2, 0:nf * T], gated[:, 0:nf * T]
            m = act(S.activation, s3, psg[:, 0:nf * T], ACT.Silu, after=[m_g, splits.get(c - 2)], chain=False)
            free_g.append(m)
            psu, free_u = pair()
            for f in range(nf):
                m_u = by_feature(split, h, f, psu[:, f * T:(f + 1) * T])
            m = dve(V.tensor_tensor, p3, s3, psu[:, 0:nf * T], ALU.mult, after=[m, m_u, splits.get(c - 1)], chain=False)
            free_u.append(m)
            splits[c] = split_into([t[:, 4 * c:4 * c + nf, :].rearrange("p f t -> p (f t)") for t in mid], p3, [m])
        halves = [pair(), pair()]
        outs = [[ps[:, t * 512:(t + 1) * 512] for t in range(NT)] for ps, _ in halves]
        for c, nf in enumerate(chunks):
            pe.wait(splits[c])
            m = rows_by_token(split, mid, nf, outs, first=4 * c, kt=F // P)
        for half in range(2):
            ps, free = halves[half]
            free.append(down_out(half, ps.rearrange("p (t n) -> p t n", t=NT), m, sil[:, :, 0:512]))

    def expert_gates(logits, n, where, tag, after):
        best = sb("best" + tag, [P, NT, 8], where=where)
        index = sb("index" + tag, [P, NT, 8], U32, where=where)
        idx = sb("idx" + tag, [P, NT, 8], where=where)
        gate = sb("gate" + tag, [P, NT, n], where=where)
        one = sb("one" + tag, [P, NT, n], where=where)
        iota = sb("iota" + tag, [P, n], where=where)
        wts = sb("wts" + tag, [P, NT, 4], where=where)
        m_i = pool(G.iota, iota[:, :], pattern=[[1, n]], base=0, channel_multiplier=0,
                   allow_small_or_imprecise_dtypes=True)
        for t in range(NT):
            dve(V.max, best[:, t, :], logits[:, t, :], after=after)
            dve(V.max_index, index[:, t, :], best[:, t, :], logits[:, t, :])
        dve(V.tensor_copy, idx[:, :, :], index[:, :, :])
        m = dve(V.tensor_tensor, wts[:, :, 0:1], best[:, :, 1:2], best[:, :, 0:1], ALU.subtract)
        m = act(S.activation, wts[:, :, 0:1], wts[:, :, 0:1], ACT.Exp, after=[m])
        dve(V.tensor_scalar, wts[:, :, 1:2], wts[:, :, 0:1], 1.0, None, ALU.add, after=[m])
        dve(V.reciprocal, wts[:, :, 1:2], wts[:, :, 1:2])
        dve(V.tensor_tensor, wts[:, :, 2:3], wts[:, :, 0:1], wts[:, :, 1:2], ALU.mult)
        for t in range(NT):
            dve(V.tensor_scalar, gate[:, t, :], iota[:, :], idx[:, t, 0:1], wts[:, t, 1:2], ALU.is_equal, ALU.mult,
                after=[m_i])
            dve(V.tensor_scalar, one[:, t, :], iota[:, :], idx[:, t, 1:2], wts[:, t, 2:3], ALU.is_equal, ALU.mult)
        return gate, dve(V.tensor_tensor, gate[:, :, :], gate[:, :, :], one[:, :, :], ALU.add)

    class Carry(dict):

        def __missing__(self, name):
            self[name] = self.open[name] = Later(back=1)
            return self[name]

    def expert_tools(n_exp, F, gate, xn, gain8, shift8, acc, where, tag, after, in_three):
        pos = sb("pos" + tag, [P, NT, n_exp + 1], where=where)
        some = sb("some" + tag, [P, NT, n_exp], where=where)
        iota = sb("slots" + tag, [P, 2, P], where=where)
        sel = sb("sel" + tag, [P, NT, P], where=where)
        selg = sb("selg" + tag, [P, NT, P], where=where)
        selgT = sb("selgT" + tag, [P, NT * P], where=where)
        xg = sb("xg" + tag, [P, KD, P], where=where)
        if in_three:
            xg_split = split_buffers("xg" + tag, [P, KD, P], where)
            w_split = split_buffers("wg" + tag, [P, 4, PART], where)
            midT_split = split_buffers("midT_" + tag, [P, 12, P], where)
        sil = sb("sil" + tag, [P, 2, 512], where=where)
        mid = sb("mid" + tag, [P, 2, 512], where=where)
        midT = sb("midT" + tag, [P, F // P, P], where=where)
        ysb = sb("ysb" + tag, [P, D], where=where)
        m_i = pool(G.iota, iota[:, :, :], pattern=[[P, 2], [1, P]], base=0, channel_multiplier=0,
                   allow_small_or_imprecise_dtypes=True)
        m = dve(V.tensor_scalar, some[:, :, :], gate[:, :, 0:n_exp], 0.0, None, ALU.is_gt, after=[after])
        pe.wait(m)
        ps, free = pair()
        product(ps[:, 0:n_exp], [(upper[:, :], some[:, 0, :])])
        product(ps[:, n_exp:2 * n_exp], [(ones[:, :], some[:, 0, :]), (upper[:, :], some[:, 1, :])])
        step = product(ps[:, 512:512 + n_exp], [(ones[:, :], some[:, 0, :]), (ones[:, :], some[:, 1, :])])
        m = pe.raised(step)
        dve(V.memset, pos[:, :, n_exp:n_exp + 1], -1.0)
        dve(V.tensor_tensor, pos[:, :, 0:n_exp], ps[:, 0:2 * n_exp].rearrange("p (t n) -> p t n", t=NT),
            some[:, :, :], ALU.mult, after=[m])
        dve(V.tensor_scalar, pos[:, :, 0:n_exp], pos[:, :, 0:n_exp], -1.0, None, ALU.add)
        over = sb("over" + tag, [1, n_exp], where=where)
        rank = sb("rank" + tag, [1, n_exp], where=where)
        num = sb("num" + tag, [1, n_exp], where=where)
        tf = sb("tf" + tag, [1, 4], where=where)
        m = dve(V.tensor_scalar, over[:, :], ps[0:1, 512:512 + n_exp], float(P), None, ALU.is_gt)
        free.append(m)
        dve(V.tensor_tensor_scan, rank[:, :], ones[0:1, 0:n_exp], over[:, :], 0.0, ALU.mult, ALU.add)
        dve(V.tensor_copy, tf[:, 0:1], rank[:, n_exp - 1:n_exp])
        dve(V.tensor_tensor, over[:, :], over[:, :], iota[0:1, 0, 0:n_exp], ALU.mult, after=[m_i])
        for k in range(MOST_OVER):
            dve(V.tensor_scalar, num[:, :], rank[:, :], float(k + 1), None, ALU.is_equal)
            dve(V.tensor_tensor, num[:, :], num[:, :], over[:, :], ALU.mult)
            dve(V.tensor_reduce, tf[:, k + 1:k + 2], num[:, :], AX.X, ALU.max)
        table_ready[tag].marks.append(dve(V.tensor_copy, tables[tag][:, :], tf[:, :]))
        dve(V.memset, ysb[:, :], 0.0)
        m = dve(V.memset, selgT[:, :], 0.0)

        def column(table, t, e):
            return At(lambda i: table[:, t, bass.ds(e(i), 1)])

        def select(c, e, b):
            for t in range(NT):
                c["sel"] = dve(V.tensor_scalar, sel[:, t, :], iota[:, b, :], column(pos, t, e), None, ALU.is_equal,
                        after=[c["gathered"]], chain=False)

        def gather(c):
            pe.wait(c["sel"])
            ps, free = pair()
            for k in range(KD):
                step = product(ps[:, k * P:(k + 1) * P], [(xn[:, t, k * P:(k + 1) * P], sel[:, t, :]) for t in range(NT)])
            c["gathered"] = m = pe.raised(step)
            m = dve(V.tensor_tensor, xg[:, :, :], ps.rearrange("p (k c) -> p k c", k=KD),
                    gain8.unsqueeze(2).to_broadcast([P, KD, P]), ALU.mult, after=[m, c["up"]], chain=False)
            free.append(m)
            if shift8 is not None:
                m = dve(V.tensor_tensor, xg[:, :, :], xg[:, :, :], shift8.unsqueeze(2).to_broadcast([P, KD, P]),
                        ALU.add)
            c["xg"] = m
            if in_three:
                c["xg_split"] = split_into([t[:, :, :] for t in xg_split], xg[:, :, :], [m, c["up"]])

        def scatter(c):
            pe.wait(c["y"], c["selgT"])
            for t in range(NT):
                ps, free = pair()
                for half in range(2):
                    step = product(ps[:, half * 512:(half + 1) * 512],
                                   [(selgT[:, t * P:(t + 1) * P], ysb[:, half * 512:(half + 1) * 512])])
                c["scattered"] = m = pe.raised(step)
                free.append(dve(V.tensor_tensor, acc[:, t, :], acc[:, t, :], ps, ALU.add, after=[m]))

        def turn_mid(c, ch, nf):
            pe.wait(c["mid", ch % 2])
            ps, free = pair()
            for f in range(nf):
                step = pe.put(PE_.transpose, ps[:, f * P:(f + 1) * P], mid[:, ch % 2, f * P:(f + 1) * P], ident[:, :])
            c["turned", ch % 2] = m = pe.raised(step)
            if in_three and ch % 2:
                dst = [part[:, 2 * (ch - 1):2 * (ch - 1) + nf, :].rearrange("p f c -> p (f c)") for part in midT_split]
                c["midT_split"] = m = split_into(dst, ps[:, 0:nf * P], [m, c["down"]])
                free.append(m)
                return
            m = act(S.copy, midT[:, 4 * ch:4 * ch + nf, :].rearrange("p f c -> p (f c)"), ps[:, 0:nf * P],
                    after=[m, c["down"]], chain=False)
            free.append(m)
            c["midT"] = m

        def layers(c, e, b, after_gate, after_up, before_down=lambda: None):
            for t in range(NT):
                m_selg = dve(V.tensor_scalar, selg[:, t, :], iota[:, b, :], column(pos, t, e), column(gate, t, e),
                             ALU.is_equal, ALU.mult, after=[c["selg_read"]], chain=False)
            chunks = [min(512, F - c0) for c0 in range(0, F, 512)]
            made = [None] * 4
            for ch, n in enumerate(chunks):
                pe.wait(c["xg"])
                ps, free = pair()
                marks = []
                for g_ in range(2):
                    split = in_three and (ch, g_) != (0, 0)
                    n_next = 0
                    if in_three:
                        n_next = n if g_ == 0 else chunks[ch + 1] if ch + 1 < len(chunks) else 0
                    if split:
                        pe.wait(c["xg_split"])
                        used[0] += 1
                    else:
                        w = take()[:, 0:KD * n].rearrange("p (k n) -> p k n", k=KD)
                    if n_next:
                        w_next = take(act, count=False)[:, 0:KD * n_next].rearrange("p (k n) -> p k n", k=KD)
                    for q in range(4):
                        if split:
                            pe.wait(made[q])
                            parts = [t[:, q, 0:2 * n].rearrange("p (k n) -> p k n", k=2) for t in w_split]
                        for k in (2 * q, 2 * q + 1):
                            if split:
                                step = split_product(ps[:, g_ * 512:g_ * 512 + n], tiles(xg_split, k),
                                                     tiles(parts, k % 2), k == 0, k == KD - 1)
                            else:
                                step = pe.put(PE_.matmul, ps[:, g_ * 512:g_ * 512 + n], xg[:, k, :], w[:, k, :],
                                              start=k == 0, stop=k == KD - 1)
                        if split:
                            c["part", q] = m_q = pe.raised(step)
                        if n_next:
                            made[q] = split_into([t[:, q, 0:2 * n_next].rearrange("p (k n) -> p k n", k=2)
                                                  for t in w_split], w_next[:, 2 * q:2 * q + 2, :], [c["part", q]])
                    marks.append(m_q if split else pe.raised(step))
                    give()
                    if g_ == 0:
                        m = act(S.activation, sil[:, ch % 2, 0:n], ps[:, 0:n], ACT.Silu,
                                after=[marks[0], c["mid", ch % 2]], chain=False)
                        if ch == 0:
                            after_gate()
                        else:
                            turn_mid(c, ch - 1, chunks[ch - 1] // P)
                c["mid", ch % 2] = m = dve(V.tensor_tensor, mid[:, ch % 2, 0:n], sil[:, ch % 2, 0:n],
                                           ps[:, 512:512 + n], ALU.mult,
                                           after=[m, marks[1], c["turned", ch % 2]], chain=False)
                free.append(m)
            c["up"] = marks[1]
            after_up()
            turn_mid(c, len(chunks) - 1, chunks[-1] // P)
            before_down()
            pe.wait(m_selg)
            ps, free = pair()
            for t in range(NT):
                step = pe.put(PE_.transpose, ps[:, t * P:(t + 1) * P], selg[:, t, :], ident[:, :])
            c["selg_read"] = m = pe.raised(step)
            c["selgT"] = m = act(S.copy, selgT[:, :], ps[:, 0:NT * P], after=[m, c["scattered"]], chain=False)
            free.append(m)
            pe.wait(c["midT"])
            if in_three:
                pe.wait(c["midT_split"])
            ps, free = pair()
            n_k = F // P
            for k0 in range(0, n_k, 4):
                split = in_three and k0 % 8 == 4
                kn = min(4, n_k - k0)
                kn_next = min(4, n_k - k0 - 4) if in_three and not split else 0
                if split:
                    used[0] += 1
                else:
                    wd = take().rearrange("p (k n) -> p k n", k=4)
                if kn_next:
                    w_next = take(act, count=False).rearrange("p (k n) -> p k n", k=4)
                for k in range(kn):
                    if split:
                        pe.wait(made[k])
                    for half in range(2):
                        o, cut = ps[:, half * 512:(half + 1) * 512], slice(half * 512, (half + 1) * 512)
                        first, last = k0 + k == 0, k0 + k == n_k - 1
                        if split:
                            step = split_product(o, tiles(midT_split, (k0 - 4) // 2 + k), [t[:, k, cut] for t in w_split],
                                                 first, last)
                        else:
                            step = pe.put(PE_.matmul, o, midT[:, k0 + k, :], wd[:, k, cut], start=first, stop=last)
                    if split and not last:
                        c["part", k] = pe.raised(step)
                    if k < kn_next:
                        made[k] = split_into([t[:, k, :] for t in w_split], w_next[:, k, :], [c["part", k]])
                if k0 + 4 >= n_k:
                    c["down"] = m = pe.raised(step)
                    if split:
                        c["part", k] = m
                give()
            c["y"] = m = act(S.copy, ysb[:, :], ps, after=[m, c["scattered"]], chain=False)
            free.append(m)

        return select, gather, scatter, layers

    def run_experts(turns, per_turn, units, select, gather, scatter, layers, tag, beside=None):
        engines = [pe, act, dve]
        flat = Carry()
        flat.open = {}
        for name in ("gathered", "up"):
            flat[name] = None
        select(flat, lambda i: 0, 0)
        gather(flat)
        marks = [e.mark() for e in everyone]
        for e in everyone:
            e.wait(*marks)
        with unit_loop(turns, units, [ada_used] if beside else []):
            turn_first = turn[0] % 4
            c = Carry()
            c.open = {}
            banks = [Later(back=1) for _ in range(4)]
            for n in range(4):
                pair_free[n] = [banks[n]]
            for j in range(per_turn):
                e = lambda i, j=j: per_turn * i + j
                def after_gate(j=j):
                    select(c, lambda i: per_turn * i + j + 1, 0)
                    scatter(c)
                    if beside:
                        beside[0](c, j)

                def before_down(j=j):
                    if beside:
                        beside[1](c, j)

                layers(c, e, 0, after_gate, lambda: gather(c), before_down)
            for name, later in c.open.items():
                later.marks.append(c[name])
            for n in range(4):
                banks[n].marks += [m for m in pair_free[n] if m is not banks[n]]
        marks = [e.mark() for e in everyone]
        for e in everyone:
            e.wait(*marks)
        for n in range(4):
            pair_free[n] = []
        flat = Carry()
        flat.open = {}
        for name in ("gathered", "up", "y", "selgT", "scattered", "selg_read", ("mid", 0), ("mid", 1), ("turned", 0),
                     ("turned", 1), "down", "xg", "midT", "midT_split", "xg_split", *(("part", q) for q in range(4))):
            flat[name] = None
        scatter(flat)
        signal_now()
        for e in engines:
            e.wait(table_ready[tag])
            load_table(e, tag)
        for k in range(MOST_OVER):
            phase()
            with case(tag, k, engines) as raises:
                first = unit_used.n
                own = Carry(flat)
                own.open = {}
                select(own, lambda i: i, 1)
                gather(own)
                layers(own, lambda i: i, 1, lambda: None, lambda: None)
                scatter(own)
                signal_now()
                raises[pe].append((unit_used.sem, first, unit_used.n - first))
            for n in range(4):
                pair_free[n] = [e.mark() for e in engines]
        phase()

    cond = sb("cond", [P, 8])
    cond_ready = act(S.activation, cond[:, :], colrange("c_2", 0, 8), ACT.Silu)
    mod_all = sb("mod_all", [P, 96])
    fe = ExitStack()
    ada_place.append(sb("ada_buf", [P, 2, KD, ADA], where=fe))
    ada_sum = sb("ada_sum", [P, 2, ADA], where=fe)
    dve.put(nc.vector.sem_inc, ada_used.sem, 2)
    ada_used.n += 2

    def ada_chunk(c, j):
        b = j % 2
        buf = ada_place[0]
        dve.put(nc.vector.wait_ge, ada_loaded[b], At(lambda i: i * 32 + 16 * (j // 2 + 1)))
        dve(V.tensor_scalar, ada_sum[:, b, :], buf[:, b, 0, :], cond[:, 0:1], None, ALU.mult,
            after=[cond_ready, c["ada_read", b]])
        for k in range(1, KD):
            dve.wait(dve.mark())
            step = dve.put(V.scalar_tensor_tensor, ada_sum[:, b, :], buf[:, b, k, :], cond[:, k:k + 1],
                           ada_sum[:, b, :], ALU.mult, ALU.add)
            m = dve.raised(step, ada_used) if k == KD - 1 else dve.raised(step)
        c["ada_sum", b] = m

    def ada_columns(c, j):
        b = j % 2
        pe.wait(c["ada_sum", b])
        ps, free = pair()
        for f in range(3):
            step = product(ps[:, f:f + 1], [(ada_sum[:, b, f * P:(f + 1) * P], ones[:, 0:1])])
        c["ada_read", b] = m = pe.raised(step)
        free.append(dve(V.tensor_copy, At(lambda i: mod_all[:, bass.ds(48 * (j // 2) + 3 * (j % 2) + 6 * i, 3)]),
                        ps[:, 0:3], after=[m], chain=False))

    tmp = ExitStack()
    m, xn = norm_transposed(lambda k: col("norm_ffn", k), None, fe, "b")
    logits = sb("logits", [P, NT, 36], where=fe)
    lg8 = sb("lg8", [P, NT, 8], where=fe)
    pe.wait(m)
    ps, free = pair()
    for t in range(NT):
        step = product(ps[:, t * 512:t * 512 + 36], [(hT[:, k, t * P:(t + 1) * P], w_rout[:, k, 0:36]) for k in range(KD)])
    m = pe.raised(step)
    m = dve(V.tensor_tensor, logits[:, :, :], ps.rearrange("p (t n) -> p t n", t=NT)[:, :, 0:36],
            b_rout[:, :].unsqueeze(1).to_broadcast([P, NT, 36]), ALU.add, after=[m])
    free.append(m)
    dve(V.memset, lg8[:, :, 4:8], -BIG)
    dve(V.tensor_copy, lg8[:, :, 0:4], logits[:, :, 0:4])
    gb = sb("gbest", [P, NT, 8], where=fe)
    gi = sb("gindex", [P, NT, 8], U32, where=fe)
    gf = sb("gf", [P, NT, 1], where=fe)
    pg = sb("pg", [P, NT, 8], where=fe)
    gs = sb("gs", [P, NT], where=fe)
    for t in range(NT):
        dve(V.max, gb[:, t, :], lg8[:, t, :])
        m = dve(V.max_index, gi[:, t, :], gb[:, t, :], lg8[:, t, :])
    m = dve(V.tensor_scalar, gb[:, :, 1:2], gb[:, :, 0:1], -1.0, None, ALU.mult)
    for t in range(NT):
        m = act(S.activation, pg[:, t, :], lg8[:, t, :], ACT.Exp, bias=gb[:, t, 1:2], accum_out=gs[:, t:t + 1], after=[m])
    dve(V.reciprocal, gs[:, :], gs[:, :], after=[m])
    dve(V.tensor_copy, gf[:, :, :], gi[:, :, 0:1])
    grp_of = sb("grp_of", [P, 32], where=fe)
    m = pool(G.iota, grp_of[:, :].rearrange("p (g e) -> p g e", g=4), pattern=[[1, 4], [0, 8]], base=0,
             channel_multiplier=0, allow_small_or_imprecise_dtypes=True)
    inside = sb("inside", [P, NT, 32], where=fe)
    le = logits[:, :, 4:36]
    for t in range(NT):
        dve(V.tensor_scalar, inside[:, t, :], grp_of[:, :], gf[:, t, :], None, ALU.is_equal, after=[m])
    dve(V.tensor_tensor, le, le, inside[:, :, :], ALU.mult)
    dve(V.tensor_scalar, inside[:, :, :], inside[:, :, :], -1.0, BIG, ALU.add, ALU.mult)
    m = dve(V.tensor_tensor, le, le, inside[:, :, :], ALU.add)
    gate, m = expert_gates(le, 32, fe, "a", [m])
    for t in range(NT):
        m = dve(V.tensor_scalar, gate[:, t, :], gate[:, t, :], gs[:, t:t + 1], None, ALU.mult)
    tools = expert_tools(32, 512, gate, xn, colrange("norm_ffn", 0, 8), None, x, fe, "a", m, False)
    run_experts(8, 4, 12, *tools, "a", (ada_chunk, ada_columns))
    fe.close()

    mod = sb("mod", [P, 48])
    gate_b = sb("gate_b", [P, 2, D])
    fgain = sb("fgain", [P, 2, KD])

    def modulation(layer):
        ad = ExitStack()
        spread = sb(f"spread{layer}", [P, 2, 8, P], where=ad)
        dve(V.tensor_tensor, mod[:, :], mod_all[:, 48 * layer:48 * layer + 48], colrange("ada_b_2", 48 * layer, 48 * layer + 48),
            ALU.add)
        for s_ in range(2):
            g0 = 16 * layer + 8 * s_
            dve(V.scalar_tensor_tensor, fgain[:, s_, :], mod[:, 24 * s_ + 8:24 * s_ + 16], 1.0,
                colrange("norm_g_2", g0, g0 + 8), ALU.add, ALU.mult)
            m = dve(V.tensor_tensor, spread[:, s_, :, :], ident[:, :].unsqueeze(1).to_broadcast([P, 8, P]),
                    mod[:, 24 * s_ + 16:24 * s_ + 24].unsqueeze(2).to_broadcast([P, 8, P]), ALU.mult)
            pe.wait(m)
            ps, free = pair()
            for half in range(2):
                step = product(ps[:, half * 512:(half + 1) * 512],
                               [(ones[:, :], spread[:, s_, 4 * half:4 * half + 4, :].rearrange("p a b -> p (a b)"))])
            m = pe.raised(step)
            free.append(act(S.copy, gate_b[:, s_, :], ps, after=[m]))
        phase()
        ad.close()

    def modulated(s_, tag, h):
        tmp = ExitStack()
        m, _ = norm_transposed(lambda k: fgain[:, s_, k:k + 1], lambda k: mod[:, 24 * s_ + k:24 * s_ + k + 1], tmp, tag, h)
        phase()
        tmp.close()
        pe.wait(m)

    def gated_add(half, s_, ps, m, tmp_, free_mark):
        dst = x[:, :, 512 * half:512 * half + 512]
        gv = gate_b[:, s_, 512 * half:512 * half + 512].unsqueeze(1).to_broadcast([P, NT, 512])
        m = dve(V.tensor_tensor, tmp_[:, :, :], ps, gv, ALU.mult, after=[m])
        dve(V.tensor_tensor, dst, dst, tmp_[:, :, :], ALU.add)
        return m

    ml = ExitStack()
    lat = sb("lat", [P, NT, 672], where=ml)
    sl = ExitStack()
    split = Split("l", [row_parts(512), row_parts(160)], sl)
    h = split_buffers("h_mla", [P, KD, T], sl)
    modulation(0)
    modulated(0, "c", h)
    unit_by_token(split, h, 512, by_token_rows(lat, 0, 512))
    unit_by_token(split, h, 160, by_token_rows(lat, 512, 160))
    phase()
    sl.close()
    pos_i = sb("pos_i", [NT, P], mybir.dt.int32, where=ml)
    lsq = sb("lsq", [P, 384], where=ml)
    pos_f = lsq[0:NT, 0:P]
    load(pos_i[:, :], A["positions_2"][0].rearrange("(t p) -> t p", p=P))
    pos = sb("pos", [P, NT], where=ml)
    ang = sb("ang", [P, 2, NT, 16], where=ml)
    kq = sb("kq", [P, 2, NT, 16], where=ml)
    m = dve(V.tensor_copy, pos_f, pos_i[:, :], after=[small_loads.mark()])
    pe.wait(m)
    ps, free = pair()
    m = pe.raised(pe.put(PE_.transpose, ps[:, 0:NT], pos_f, ident[0:NT, 0:NT]))
    free.append(dve(V.tensor_copy, pos[:, :], ps[:, 0:NT], after=[m]))
    freq = sb("freq", [P, 16], where=ml)
    for n in range(16):
        f = float(np.float32(10000.0) ** np.float32(-2.0 * n / 32))
        pool(G.memset, freq[:, n:n + 1], f)
    for t in range(NT):
        dve(V.tensor_scalar, ang[:, 1, t, :], freq[:, :], pos[:, t:t + 1], None, ALU.mult, after=[pool.mark()])
    magic = 1.5 * 2.0 ** 23
    c1 = 6.28125
    c2 = float(np.float32(np.floor((2 * math.pi - c1) * 2 ** 21) / 2 ** 21))
    c3 = 2 * math.pi - c1 - c2
    dve(V.tensor_copy, ang[:, 0, :, :], ang[:, 1, :, :])
    dve(V.tensor_scalar, kq[:, 1, :, :], ang[:, 1, :, :], 1.0 / (2 * math.pi), None, ALU.mult)
    dve(V.tensor_scalar, kq[:, 0, :, :], ang[:, 0, :, :], 1.0 / (2 * math.pi), 0.25, ALU.mult, ALU.add)
    dve(V.tensor_scalar, kq[:, :, :, :], kq[:, :, :, :], magic, None, ALU.add)
    dve(V.tensor_scalar, kq[:, :, :, :], kq[:, :, :, :], -magic, None, ALU.add)
    for c in (c1, c2, c3):
        dve(V.scalar_tensor_tensor, ang[:, :, :, :].rearrange("p a t n -> p (a t n)"),
            kq[:, :, :, :].rearrange("p a t n -> p (a t n)"), -c,
            ang[:, :, :, :].rearrange("p a t n -> p (a t n)"), ALU.mult, ALU.add)
    dve(V.tensor_scalar, ang[:, 0, :, :], ang[:, 0, :, :], math.pi / 2, None, ALU.add)
    pi_in = float(np.nextafter(np.float32(math.pi), np.float32(0)))
    m = dve(V.tensor_scalar, ang[:, :, :, :], ang[:, :, :, :], pi_in, -pi_in, ALU.min, ALU.max)
    act(S.activation, ang[:, :, :, :], ang[:, :, :, :], ACT.Sin, after=[m])
    cos, sin = ang[:, 0, :, :], ang[:, 1, :, :]

    ls = sb("ls", [P, NT, 2], where=ml)
    lT = sb("lT", [P, 5, T], where=ml)
    for t in range(NT):
        act(S.activation, lsq[:, :], lat[:, t, 0:384], ACT.Square, accum_out=ls[:, t, 0:1])
        act(S.activation, lsq[:, 0:256], lat[:, t, 384:640], ACT.Square, accum_out=ls[:, t, 1:2])
    rsqrt(ls[:, :, 0:1], ls[:, :, 0:1], 1.0 / 384)
    m = rsqrt(ls[:, :, 1:2], ls[:, :, 1:2], 1.0 / 256)
    for t in range(NT):
        dve(V.tensor_scalar, lat[:, t, 0:384], lat[:, t, 0:384], ls[:, t, 0:1], None, ALU.mult, after=[m])
        m2 = dve(V.tensor_scalar, lat[:, t, 384:640], lat[:, t, 384:640], ls[:, t, 1:2], None, ALU.mult)
    pe.wait(m2)
    for f0 in (0, 4):
        fs = range(f0, min(f0 + 4, 5))
        def lat_out(n0, k, ps, m, fs=fs):
            for f in fs:
                c = col("mla_q_norm_2", f) if f < 3 else col("mla_kv_norm_2", f - 3)
                last = dve(V.tensor_scalar, lT[:, f, :], ps[:, (f - fs[0]) * T:(f - fs[0] + 1) * T], c, None, ALU.mult,
                           after=[m])
            return last
        transposed([lat[:, t, f * P:(f + 1) * P] for f in fs for t in range(NT)], lat_out)
    pe.wait(dve.mark())
    mout = sb("mout", [P, NT, D], where=ml)
    mi = ExitStack()
    mq = sb("mq", [P, NT, 1536], where=mi)
    mkv = sb("mkv", [P, NT, 2048], where=mi)
    for c in range(2):
        w = take()[:, 0:2304].rearrange("p (k n) -> p k n", k=3)
        for c0, n in ((0, 512), (512, 256)):
            ps, free = pair()
            for t in range(NT):
                step = product(ps[:, t * 512:t * 512 + n], [(lT[:, k, t * P:(t + 1) * P], w[:, k, c0:c0 + n]) for k in range(3)])
            if c0:
                give()
            m = pe.raised(step)
            free.append(act(S.copy, mq[:, :, 768 * c + c0:768 * c + c0 + n],
                            ps.rearrange("p (t n) -> p t n", t=NT)[:, :, 0:n], after=[m]))
    w = take().rearrange("p (k n) -> p k n", k=2)
    for c in range(4):
        ps, free = pair()
        for t in range(NT):
            step = product(ps[:, t * 512:(t + 1) * 512],
                           [(lT[:, 3 + k, t * P:(t + 1) * P], w[:, k, 512 * c:512 * c + 512]) for k in range(2)])
        if c == 3:
            give()
        m = pe.raised(step)
        free.append(act(S.copy, mkv[:, :, 512 * c:512 * c + 512], ps.rearrange("p (t n) -> p t n", t=NT), after=[m]))

    rt = mout[:, 0, :].rearrange("p (k h n) -> p k h n", k=4, h=16)

    def rope(v, t, n):
        c_ = cos[:, t, :].unsqueeze(1).to_broadcast([P, n, 16])
        s_ = sin[:, t, :].unsqueeze(1).to_broadcast([P, n, 16])
        a, b = v[:, :, 0:16], v[:, :, 16:32]
        r = [rt[:, k, 0:n, :] for k in range(4)]
        dve(V.tensor_tensor, r[0], a, c_, ALU.mult, after=[act.mark()])
        dve(V.tensor_tensor, r[1], b, s_, ALU.mult)
        dve(V.tensor_tensor, r[2], a, s_, ALU.mult)
        dve(V.tensor_tensor, r[3], b, c_, ALU.mult)
        dve(V.tensor_tensor, a, r[0], r[1], ALU.subtract)
        return dve(V.tensor_tensor, b, r[2], r[3], ALU.add)

    for t in range(NT):
        rope(mq[:, t, :].rearrange("p (h d) -> p h d", d=96)[:, :, 64:96], t, 16)
        rope(lat[:, t, 640:672].unsqueeze(1), t, 1)
    mqT = sb("mqT", [96, 2, 4, T], where=mi)
    mkT = sb("mkT", [96, 2, 4, T], where=mi)
    diag = sb("diag", [P, P], where=mi)
    pool(G.memset, diag[:, :], 0.0)
    m_diag = pool(G.memset, diag[0:64, 64:128], -BIG)
    wgt2 = sb("wgt2", [P, 4], where=mi)
    kcat = sb("kcat", [P, NT, 4, 96], where=mi)
    heads_ready = dve.mark()
    jobs, kcat_read = [], [None]

    def latent_job(g4, t):
        h4, buf = 4 * g4, g4 % 2

        def prepare():
            for t_ in range(NT):
                dve(V.tensor_copy, kcat[:, t_, :, 0:64],
                    mkv[:, t_, :].rearrange("p (h d) -> p h d", d=128)[:, h4:h4 + 4, 0:64], after=[act.mark(), kcat_read[0]])
                m = dve(V.tensor_copy, kcat[:, t_, :, 64:96], lat[:, t_, 640:672].unsqueeze(1).to_broadcast([P, 4, 32]))
            before = [jobs[2 * (g4 - 2) + 1]["multiplied"]] if g4 >= 2 else []
            pe.wait(m, heads_ready)
            transposed([mq[:, t_, 96 * (h4 + j):96 * (h4 + j) + 96] for j in range(4) for t_ in range(NT)],
                       lambda n0, k, ps, m: act(S.copy, mqT[:, buf, :, :].rearrange("p h t -> p (h t)"), ps[0:96, :],
                                                after=[m] + before))
            transposed([kcat[:, t_, j, :] for j in range(4) for t_ in range(NT)],
                       lambda n0, k, ps, m: act(S.copy, mkT[:, buf, :, :].rearrange("p h t -> p (h t)"), ps[0:96, :],
                                                after=[m] + before))
            kcat_read[0] = pe.mark()
            pe.wait(act.mark())

        def score(ps_, s_, marks):
            if t:
                dve(V.tensor_copy, s_[:, :, 0:P], ps_[:, :, 0:P], after=marks, chain=False)
            return dve(V.tensor_tensor, s_[:, :, t * P:(t + 1) * P], ps_[:, :, t * P:(t + 1) * P],
                       diag[:, :].unsqueeze(1).to_broadcast([P, 4, P]), ALU.add, after=marks + [m_diag], chain=False)

        def finish(ps_, den, m):
            dve(V.reciprocal, wgt2[:, :], den, after=[m])
            dst = mout[:, t, 64 * h4:64 * h4 + 256].rearrange("p (h d) -> p h d", d=64)
            return dve(V.tensor_tensor, dst, ps_, wgt2[:, :].unsqueeze(2).to_broadcast([P, 4, 64]), ALU.mult)

        return dict(n_keys=(t + 1) * P, queries=lambda j: mqT[:, buf, j, t * P:(t + 1) * P],
                    keys=lambda j: mkT[:, buf, j, :],
                    values=lambda j, c: mkv[:, c, 128 * (h4 + j) + 64:128 * (h4 + j) + 128],
                    score=score, finish=finish, prepare=prepare if t == 0 else None)

    jobs += [latent_job(g4, t) for g4 in range(4) for t in range(NT)]
    ac = ExitStack()
    attention("mla", jobs, T, 96.0 ** -0.5, ac)
    phase()
    ac.close()
    mi.close()
    oT = split_buffers("oT", [P, KD, T], ac)
    split = Split("p", [row_parts(512)] * 2, ac)
    token_tiles_transposed(mout, oT, KD, [dve.mark()])
    ga = sb("ga", [P, NT, 512], where=ac)
    for half in range(2):
        unit_by_token(split, oT, 512, lambda ps, m, half=half: gated_add(half, 0, ps, m, ga, None))
    phase()
    ac.close()
    ml.close()

    ff = ExitStack()
    mlp(2816, lambda half, ps, m, tmp_: gated_add(half, 1, ps, m, tmp_, None), ff, "f")
    phase()
    ff.close()

    modulation(1)
    sm = ExitStack()
    z = sb("z", [P, NT, 2048], where=sm)
    ys = sb("ys", [P, NT, 4], where=sm)
    si = ExitStack()
    xbc = sb("xbc", [P, 24, T], where=si)
    pad = ExitStack()
    upad = sb("upad2", [P, 2, 4, T + 3], where=pad)
    split = Split("s", [row_parts(512)] * 4 + [feature_parts()] * 6, pad)
    h = split_buffers("h_ssm", [P, KD, T], pad)
    modulated(0, "e", h)
    for c in range(4):
        unit_by_token(split, h, 512, lambda ps, m, c=c: act(S.activation, z[:, :, 512 * c:512 * c + 512], ps, ACT.Silu, after=[m]))
    m_pad = dve(V.memset, upad[:, :, :, 0:3], 0.0)
    act.wait(m_pad)
    conv_done = {}
    for u in range(6):
        buf = upad[:, u % 2, :, :]
        def evacuate(ps, m, buf=buf, u=u):
            return act(S.copy, buf[:, :, 3:T + 3], ps, after=[m, conv_done.get(u - 2)])
        unit_by_feature(split, h, evacuate)
        m_in = act.mark()
        for f in range(4):
            c = 4 * u + f
            conv_done[u] = conv_silu(buf, xbc[:, c, :], f, lambda j, c=c: col("ssm_conv_w_2", 24 * j + c), 4,
                                     after=[m_in])
    for c in range(24):
        m = act(S.activation, xbc[:, c, :], xbc[:, c, :], ACT.Silu, bias=col("ssm_conv_b_2", c),
                after=[conv_done[c // 4]])
    phase()
    pad.close()
    dt = sb("dt", [P, NT, 32], where=si)
    da = sb("da", [P, NT, 32], where=si)
    t3 = sb("t3b", [P, 3, NT, 32], where=si)
    ps, free = pair()
    for t in range(NT):
        step = product(ps[:, t * 512:t * 512 + 32], [(hT[:, k, t * P:(t + 1) * P], w_thin[:, k, 32:64]) for k in range(KD)])
    m = pe.raised(step)

    def over_tiles(v):
        return v.unsqueeze(1).to_broadcast([P, NT, 32])

    m = dve(V.tensor_tensor, dt[:, :, :], ps.rearrange("p (t n) -> p t n", t=NT)[:, :, 0:32], over_tiles(ssm_v[:, 0, :]),
            ALU.add, after=[m])
    free.append(m)
    m = softplus(dt[:, :, :], [t3[:, n, :, :] for n in range(3)], dt[:, :, :])
    act(S.activation, ssm_v[:, 1, :], ssm_v[:, 1, :], ACT.Exp)
    m = dve(V.scalar_tensor_tensor, da[:, 0, :], dt[:, 0, :], -1.0, ssm_v[:, 1, :], ALU.mult, ALU.mult, after=[act.mark()])
    m = dve(V.scalar_tensor_tensor, da[:, 1, :], dt[:, 1, :], -1.0, ssm_v[:, 1, :], ALU.mult, ALU.mult)
    pe.wait(m)
    daT = sb("daT", [32, T], where=si)
    csT = sb("csT", [32, T], where=si)
    cs = sb("cs", [P, NT, 32], where=si)
    on32 = sb("on32", [32, T], where=si)
    transposed([da[:, t, :] for t in range(NT)],
               lambda n0, k, ps, m: dve(V.tensor_copy, daT[:, :], ps[0:32, 0:T], after=[m]))
    dve(V.memset, on32[:, :], 1.0)
    m = dve(V.tensor_tensor_scan, csT[:, :], on32[:, :], daT[:, :], 0.0, ALU.mult, ALU.add)
    pe.wait(m)
    ps, free = pair()
    for t in range(NT):
        step = pe.put(PE_.transpose, ps[:, t * 32:t * 32 + 32], csT[:, t * P:(t + 1) * P], ident[0:32, 0:32])
    m = pe.raised(step)
    free.append(dve(V.tensor_copy, cs[:, :, :].rearrange("p t h -> p (t h)"), ps[:, 0:64], after=[m]))
    xs = sb("xs", [P, NT, 2048], where=si)
    pe.wait(act.mark())
    for f0 in range(0, 16, 4):
        transposed([xbc[:, f, t * P:(t + 1) * P] for t in range(NT) for f in range(f0, f0 + 4)],
                   lambda n0, k, ps, m, f0=f0: act(S.copy, xs[:, :, f0 * P:(f0 + 4) * P],
                                                   ps.rearrange("p (t n) -> p t n", t=NT), after=[m]))
    cb = sb("cb", [P, 4, 3, P], where=si)
    for g0 in range(0, 4, 2):
        ps, free = pair()
        for g_ in range(g0, g0 + 2):
            o_ = (g_ - g0) * 512
            product(ps[:, o_:o_ + T], [(xbc[:, 16 + g_, 0:P], xbc[:, 20 + g_, :])])
            step = product(ps[:, o_ + T:o_ + T + P], [(xbc[:, 16 + g_, P:T], xbc[:, 20 + g_, P:T])])
        m = pe.raised(step)
        for g_ in range(g0, g0 + 2):
            o_ = (g_ - g0) * 512
            v = ps[:, o_:o_ + 3 * P].rearrange("p (a c) -> p a c", a=3)
            dve(V.tensor_tensor, cb[:, g_, 0:3:2, :], v[:, 0:3:2, :], upper[:, :].unsqueeze(1).to_broadcast([P, 2, P]),
                ALU.mult, after=[m])
            last = dve(V.tensor_copy, cb[:, g_, 1, :], v[:, 1, :])
        free.append(last)
    tmpy = sb("tmpy", [P, NT, 512], where=si)
    NM = 4
    Mt = [sb(f"Mt{b}", [P, 3 * P], where=si) for b in range(NM)]
    Mfree = [None] * NM
    y = hT[:, 0:4, :].rearrange("p k t -> p (k t)").rearrange("p (t n) -> p t n", t=NT)
    pe.wait(dve.mark(), act.mark())
    state = {}

    def decays(h):
        b = h % NM
        ps, free = pair()
        step = product(ps[:, 0:T], [(ident[0:32, h:h + 1].to_broadcast([32, P]), csT[:, :])])
        m = pe.raised(step)
        dve(V.tensor_scalar, Mt[b][:, 0:T], ps[:, 0:T], cs[:, 0, h:h + 1], 0.0, ALU.subtract, ALU.min,
            after=[m, Mfree[b]], chain=False)
        m = dve(V.tensor_scalar, Mt[b][:, T:T + P], ps[:, P:T], cs[:, 1, h:h + 1], 0.0, ALU.subtract, ALU.min,
                chain=False)
        free.append(m)
        state[h] = act(S.activation, Mt[b][:, :], Mt[b][:, :], ACT.Exp, after=[m], chain=False)

    def weigh(h):
        b = h % NM
        cbv = cb[:, h // 8, :, :].rearrange("p a c -> p (a c)")
        dve(V.scalar_tensor_tensor, Mt[b][:, 0:T], Mt[b][:, 0:T], dt[:, 0, h:h + 1], cbv[:, 0:T], ALU.mult, ALU.mult,
            after=[state[h]])
        state[h] = dve(V.scalar_tensor_tensor, Mt[b][:, T:T + P], Mt[b][:, T:T + P], dt[:, 1, h:h + 1],
                       cbv[:, T:T + P], ALU.mult, ALU.mult, chain=False)

    for g_ in range(4):
        if g_ == 0:
            decays(0)
            decays(1)
        ysum, yfree = pair()
        held.append((turn[0] - 1) % 4)
        for hh in range(8):
            h = 8 * g_ + hh
            weigh(h)
            if h + 2 < 32:
                decays(h + 2)
            pe.wait(state[h])
            b = h % NM
            xv = [xs[:, s_, 64 * h:64 * h + 64] for s_ in range(2)]
            product(ysum[:, 64 * hh:64 * hh + 64], [(Mt[b][:, 0:P], xv[0])])
            step = product(ysum[:, 512 + 64 * hh:512 + 64 * hh + 64], [(Mt[b][:, P:T], xv[0]), (Mt[b][:, T:T + P], xv[1])])
            Mfree[b] = pe.raised(step)
        yv = ysum.rearrange("p (t n) -> p t n", t=NT)
        gx = slice(512 * g_, 512 * g_ + 512)
        m = dve(V.tensor_tensor, tmpy[:, :, :].rearrange("p t (h d) -> p t h d", d=64),
                xs[:, :, gx].rearrange("p t (h d) -> p t h d", d=64),
                ssm_v[:, 2, 8 * g_:8 * g_ + 8].unsqueeze(1).unsqueeze(3).to_broadcast([P, NT, 8, 64]), ALU.mult,
                after=Mfree)
        m = dve(V.tensor_tensor, tmpy[:, :, :], tmpy[:, :, :], yv, ALU.add)
        yfree.append(m)
        held.clear()
        m = dve(V.tensor_tensor, z[:, :, gx], z[:, :, gx], tmpy[:, :, :], ALU.mult)
        for t in range(NT):
            m = act(S.activation, y[:, t, :], z[:, t, gx], ACT.Square, accum_out=ys[:, t, g_:g_ + 1], after=[m])
    m = rsqrt(ys[:, :, :], ys[:, :, :], 1.0 / 512)
    for t in range(NT):
        zt = z[:, t, :].rearrange("p (g n) -> p g n", g=4)
        m2 = dve(V.tensor_tensor, zt, zt, ys[:, t, :].unsqueeze(2).to_broadcast([P, 4, 512]), ALU.mult, after=[m])
    pe.wait(m2)
    phase()
    si.close()
    so = ExitStack()
    zTt = split_buffers("zT", [P, 16, T], so)
    split = Split("q", [row_parts(D, 4)] * 4, so)
    zs = sb("zs", [P, 2, 4, T], where=so)
    ga = sb("gated_ssm", [P, NT, 512], where=so)
    read = {}
    for n, f0 in enumerate(range(0, 16, 4)):
        def z_out(n0, k, ps, m, f0=f0, n=n):
            for f in range(4):
                last = dve(V.tensor_scalar, zs[:, n % 2, f, :], ps[:, f * T:(f + 1) * T], col("ssm_norm_2", f0 + f), None,
                           ALU.mult, after=[m, read.get(n - 2)], chain=False)
            read[n] = split_into(tiles(zTt, slice(f0, f0 + 4)), zs[:, n % 2, :, :], [last])
            return last
        transposed([z[:, t, f * P:(f + 1) * P] for f in range(f0, f0 + 4) for t in range(NT)], z_out)
    acc = [pair(), pair()]
    outs = [[ps[:, t * 512:(t + 1) * 512] for t in range(NT)] for ps, _ in acc]
    for n in range(4):
        pe.wait(read[n])
        m = rows_by_token(split, zTt, 4, outs, first=4 * n, kt=16)
    for half in range(2):
        acc[half][1].append(gated_add(half, 0, acc[half][0].rearrange("p (t n) -> p t n", t=NT), m, ga, None))
    phase()
    so.close()
    sm.close()

    me = ExitStack()
    fg = gate_b[:, 0, :]
    load(fg, A["final_norm_2"].partition_broadcast(P))
    m, xn = norm_transposed(lambda k: fgain[:, 1, k:k + 1], lambda k: mod[:, 24 + k:24 + k + 1], me, "g")
    pe.wait(m)
    lo2 = sb("lo2", [P, NT, 8], where=me)
    ps, free = pair()
    for t in range(NT):
        step = product(ps[:, t * 512:t * 512 + 8], [(hT[:, k, t * P:(t + 1) * P], w_rout[:, k, 36:44]) for k in range(KD)])
    m = pe.raised(step)
    m = act(S.copy, lo2[:, :, :], ps.rearrange("p (t n) -> p t n", t=NT)[:, :, 0:8], after=[m])
    free.append(m)
    gate2, m = expert_gates(lo2, 8, me, "b", [m])
    total = sb("total", [P, NT, D], where=me)
    m = dve(V.memset, total[:, :, :], 0.0)
    tools = expert_tools(8, 2816, gate2, xn, fgain[:, 1, :], mod[:, 24:32], total, me, "b", m, True)
    run_experts(4, 2, 36, *tools, "b")
    dve(V.tensor_tensor, total[:, :, :], total[:, :, :], gate_b[:, 1, :].unsqueeze(1).to_broadcast([P, NT, D]), ALU.mult)
    m = dve(V.tensor_tensor, x[:, :, :], x[:, :, :], total[:, :, :], ALU.add)
    fs = sb("fs", [P, NT], where=me)
    for t in range(NT):
        act(S.activation, total[:, t, :], x[:, t, :], ACT.Square, accum_out=fs[:, t:t + 1], after=[m])
    m = rsqrt(fs[:, :], fs[:, :], 1.0 / D)
    for t in range(NT):
        m = dve(V.scalar_tensor_tensor, total[:, t, :], x[:, t, :], fs[:, t:t + 1], fg, ALU.mult, ALU.mult,
                after=[m, small_loads.mark()])
    sp.wait(m)
    sp.raised(sp.put(nc.sync.dma_start, out[0].rearrange("(t p) n -> p t n", p=P), total[:, :, :]), stored, 16)
    sp.put(nc.sync.wait_ge, stored.sem, stored.n)
    me.close()

    with ctx, nc.Block() as blk:
        blk.sync(lambda eng: sp.play(eng))
        blk.gpsimd(lambda eng: pool.play(eng))
        blk.scalar(lambda eng: act.play(eng))
        blk.vector(lambda eng: dve.play(eng))
        blk.tensor(lambda eng: pe.play(eng))



def kernel(**inputs):
    import concourse.bacc as bacc
    from concourse.bass_utils import run_bass_kernel_spmd

    nc = bacc.Bacc("TRN2", target_bir_lowering=False, num_devices=1)
    arrays, A = {}, {}
    for name, value in inputs.items():
        a = np.ascontiguousarray(value)
        arrays["in_" + name] = a
        A[name] = nc.dram_tensor("in_" + name, a.shape, mybir.dt.from_np(a.dtype), kind="ExternalInput").ap()
    out = nc.dram_tensor("out", (1, T, D), F32, kind="ExternalOutput").ap()
    block(nc, A, out)
    result = run_bass_kernel_spmd(nc, [arrays], core_ids=[0])
    return result.results[0]["out"]
```
